# Optimizing a Trainium2 kernel written in Bass

```python
import jax, jax.numpy as jnp
from jax import lax
import numpy as np

D_MODEL = 1024
BATCH = 1
SEQ = 512
DEPTH = 2

PLE_DIM = 256
MLA_HEADS = 8
MLA_NOPE = 64
MLA_ROPE = 32
MLA_V = 64
MLA_QK = MLA_NOPE + MLA_ROPE
MLA_Q_LORA = 384
MLA_KV_LORA = 128
ROPE_THETA = 10000.0
Q_BLOCK = 128
FNET_GROUPS = 4
GQA_Q_HEADS = 8
GQA_KV_HEADS = 2
GQA_GROUP = GQA_Q_HEADS // GQA_KV_HEADS
GQA_HEAD_DIM = 64
WINDOW = 128
WIN_BLOCK = 128
FFN_DIM = -(-8 * D_MODEL // (3 * 256)) * 256
RMS_EPS = 1e-6

IN_SPLITS = (MLA_Q_LORA, MLA_KV_LORA, MLA_ROPE,
             GQA_Q_HEADS * GQA_HEAD_DIM, GQA_KV_HEADS * GQA_HEAD_DIM, GQA_KV_HEADS * GQA_HEAD_DIM,
             D_MODEL, D_MODEL, D_MODEL)
IN_COLS = sum(IN_SPLITS)


def rms_norm(x, gain):
    xf = x.astype(jnp.float32)
    y = xf * lax.rsqrt(jnp.mean(xf * xf, axis=-1, keepdims=True) + RMS_EPS)
    return (y * gain.astype(jnp.float32)).astype(x.dtype)

def apply_rope(t, positions):
    half = t.shape[-1] // 2
    inv_freq = ROPE_THETA ** (-jnp.arange(half, dtype=jnp.float32) / half)
    ang = positions.astype(jnp.float32)[..., None] * inv_freq
    ang = ang.reshape(ang.shape[:2] + (1,) * (t.ndim - 3) + (half,))
    cos, sin = jnp.cos(ang), jnp.sin(ang)
    tf = t.astype(jnp.float32)
    t1, t2 = tf[..., :half], tf[..., half:]
    return jnp.concatenate([t1 * cos - t2 * sin, t1 * sin + t2 * cos], axis=-1).astype(t.dtype)

def alibi_slopes(n_heads):
    return 2.0 ** (-8.0 * (np.arange(n_heads, dtype=np.float32) + 1.0) / n_heads)

def mla_attention(c_q, c_kv, k_rope, positions, q_norm, w_uq, kv_norm, w_ukv):
    B, S, _ = c_q.shape
    q = (rms_norm(c_q, q_norm) @ w_uq).reshape(B, S, MLA_HEADS, MLA_QK)
    q_nope = q[..., :MLA_NOPE]
    q_rope = apply_rope(q[..., MLA_NOPE:], positions)
    kv = (rms_norm(c_kv, kv_norm) @ w_ukv).reshape(B, S, MLA_HEADS, MLA_NOPE + MLA_V)
    k_nope, v = kv[..., :MLA_NOPE], kv[..., MLA_NOPE:]
    k_r = apply_rope(k_rope, positions)
    scale = MLA_QK ** -0.5
    nb = S // Q_BLOCK
    qn_b = q_nope.reshape(B, nb, Q_BLOCK, MLA_HEADS, MLA_NOPE).transpose(1, 0, 2, 3, 4)
    qr_b = q_rope.reshape(B, nb, Q_BLOCK, MLA_HEADS, MLA_ROPE).transpose(1, 0, 2, 3, 4)

    def attend(blk):
        qn, qr = blk
        s = (jnp.einsum('bqhd,bkhd->bhqk', qn, k_nope)
             + jnp.einsum('bqhr,bkr->bhqk', qr, k_r)).astype(jnp.float32) * scale
        probs = jax.nn.softmax(s, axis=-1).astype(v.dtype)
        return jnp.einsum('bhqk,bkhd->bqhd', probs, v)

    o = lax.map(attend, (qn_b, qr_b))
    return o.transpose(1, 0, 2, 3, 4).reshape(B, S, MLA_HEADS * MLA_V)

def fourier_mix(h):
    B, S, D = h.shape
    hg = h.astype(jnp.float32).reshape(B, S, FNET_GROUPS, D // FNET_GROUPS)
    f = jnp.fft.fftn(hg, axes=(1, 3), norm='ortho').real
    return f.reshape(B, S, D).astype(h.dtype)

def windowed_gqa(q, k, v, positions, sink):
    B, S, _ = q.shape
    nb = S // WIN_BLOCK
    q = q.reshape(B, nb, WIN_BLOCK, GQA_KV_HEADS, GQA_GROUP, GQA_HEAD_DIM)
    k = k.reshape(B, S, GQA_KV_HEADS, GQA_HEAD_DIM)
    v = v.reshape(B, S, GQA_KV_HEADS, GQA_HEAD_DIM)

    def windows(t):
        pad = ((0, 0), (WIN_BLOCK, WIN_BLOCK)) + ((0, 0),) * (t.ndim - 2)
        tb = jnp.pad(t, pad).reshape((B, nb + 2, WIN_BLOCK) + t.shape[2:])
        return jnp.concatenate([tb[:, :-2], tb[:, 1:-1], tb[:, 2:]], axis=2)

    kw, vw, pw = windows(k), windows(v), windows(positions)
    scale = GQA_HEAD_DIM ** -0.5
    s = jnp.einsum('bnqhgd,bnkhd->bnhgqk', q, kw).astype(jnp.float32) * scale
    pq = positions.reshape(B, nb, WIN_BLOCK)
    dist = jnp.abs(pq[..., :, None] - pw[..., None, :]).astype(jnp.float32)
    slopes = jnp.asarray(alibi_slopes(GQA_Q_HEADS)).reshape(GQA_KV_HEADS, GQA_GROUP)
    s = s - slopes[None, None, :, :, None, None] * dist[:, :, None, None]
    qi = jnp.arange(WIN_BLOCK)
    kj = jnp.arange(3 * WIN_BLOCK)
    band = jnp.abs(kj[None, :] - WIN_BLOCK - qi[:, None]) <= WINDOW
    key_idx = jnp.arange(nb)[:, None] * WIN_BLOCK - WIN_BLOCK + kj[None, :]
    valid = (key_idx >= 0) & (key_idx < S)
    mask = band[None] & valid[:, None, :]
    s = jnp.where(mask[None, :, None, None], s, -jnp.inf)
    sink_l = sink.astype(jnp.float32).reshape(GQA_KV_HEADS, GQA_GROUP)[None, None, :, :, None, None]
    m = jnp.maximum(jnp.max(s, axis=-1, keepdims=True), sink_l)
    e = jnp.exp(s - m)
    probs = (e / (jnp.sum(e, axis=-1, keepdims=True) + jnp.exp(sink_l - m))).astype(v.dtype)
    o = jnp.einsum('bnhgqk,bnkhd->bnqhgd', probs, vw)
    return o.reshape(B, S, GQA_Q_HEADS * GQA_HEAD_DIM)

def first_inputs(seed: int = 0) -> dict:
    key = jax.random.key(seed)
    ks = iter(jax.random.split(key, 32))

    def w(shape, fan_in):
        return jax.random.normal(next(ks), shape, jnp.float32) * (fan_in ** -0.5)

    def gain(n):
        return 1.0 + 0.1 * jax.random.normal(next(ks), (DEPTH, n), jnp.float32)

    x = jax.random.normal(next(ks), (BATCH, SEQ, D_MODEL), jnp.float32)
    p = jax.random.normal(next(ks), (DEPTH, BATCH, SEQ, PLE_DIM), jnp.float32)
    offset = jax.random.randint(next(ks), (BATCH, 1), 0, 4096, jnp.int32)
    positions = (offset + jnp.arange(SEQ, dtype=jnp.int32)[None, :]).astype(jnp.int32)
    return {
        'x': x,
        'p': p,
        'positions': positions,
        'norm_mix_pre': gain(D_MODEL),
        'w_in': w((DEPTH, D_MODEL, IN_COLS), D_MODEL),
        'mla_q_norm': gain(MLA_Q_LORA),
        'w_uq': w((DEPTH, MLA_Q_LORA, MLA_HEADS * MLA_QK), MLA_Q_LORA),
        'mla_kv_norm': gain(MLA_KV_LORA),
        'w_ukv': w((DEPTH, MLA_KV_LORA, MLA_HEADS * (MLA_NOPE + MLA_V)), MLA_KV_LORA),
        'gqa_sink': 0.5 * jax.random.normal(next(ks), (DEPTH, GQA_Q_HEADS), jnp.float32),
        'w_branch_a': w((DEPTH, MLA_HEADS * MLA_V, D_MODEL), MLA_HEADS * MLA_V),
        'w_branch_b': w((DEPTH, D_MODEL, D_MODEL), D_MODEL),
        'w_branch_c': w((DEPTH, GQA_Q_HEADS * GQA_HEAD_DIM, D_MODEL), GQA_Q_HEADS * GQA_HEAD_DIM),
        'w_out': w((DEPTH, D_MODEL, D_MODEL), D_MODEL),
        'norm_mix_post': gain(D_MODEL),
        'norm_ffn_pre': gain(D_MODEL),
        'w_ffn_gate': w((DEPTH, D_MODEL, FFN_DIM), D_MODEL),
        'w_ffn_up': w((DEPTH, D_MODEL, FFN_DIM), D_MODEL),
        'w_ffn_down': w((DEPTH, FFN_DIM, D_MODEL), FFN_DIM),
        'norm_ffn_post': gain(D_MODEL),
        'w_ple_proj': w((DEPTH, PLE_DIM, D_MODEL), PLE_DIM),
        'w_ple_gate': w((DEPTH, D_MODEL, D_MODEL), D_MODEL),
        'norm_ple': gain(D_MODEL),
    }

def first_block(x, p, positions, norm_mix_pre, w_in, mla_q_norm, w_uq, mla_kv_norm, w_ukv,
              gqa_sink, w_branch_a, w_branch_b, w_branch_c, w_out, norm_mix_post,
              norm_ffn_pre, w_ffn_gate, w_ffn_up, w_ffn_down, norm_ffn_post,
              w_ple_proj, w_ple_gate, norm_ple):
    split_points = list(np.cumsum(IN_SPLITS)[:-1])
    for i in range(DEPTH):
        h = rms_norm(x, norm_mix_pre[i])
        z = h @ w_in[i]
        c_q, c_kv, k_rope, q_c, k_c, v_c, g_a, g_b, g_c = jnp.split(z, split_points, axis=-1)
        o_a = mla_attention(c_q, c_kv, k_rope, positions, mla_q_norm[i], w_uq[i],
                            mla_kv_norm[i], w_ukv[i])
        o_b = fourier_mix(h)
        o_c = windowed_gqa(q_c, k_c, v_c, positions, gqa_sink[i])
        merged = (jax.nn.sigmoid(g_a) * (o_a @ w_branch_a[i])
                  + jax.nn.sigmoid(g_b) * (o_b @ w_branch_b[i])
                  + jax.nn.sigmoid(g_c) * (o_c @ w_branch_c[i]))
        x = x + rms_norm(merged @ w_out[i], norm_mix_post[i])
        h = rms_norm(x, norm_ffn_pre[i])
        ff = (jax.nn.silu(h @ w_ffn_gate[i]) * (h @ w_ffn_up[i])) @ w_ffn_down[i]
        x = x + rms_norm(ff, norm_ffn_post[i])
        e = (p[i] @ w_ple_proj[i]) * jax.nn.sigmoid(x @ w_ple_gate[i])
        x = x + rms_norm(e, norm_ple[i])
    return x


DEPTH_2 = 1

CHUNK = 64
N_MEM = 256
BRANCH_WIDTH = 512
N_BRANCH = 3
LRU_WIDTH = BRANCH_WIDTH
LRU_BLOCKS = 8
LRU_BLOCK = LRU_WIDTH // LRU_BLOCKS
CONV_WIDTH = 4
LRU_C = 8.0
POOL_WIDTH = BRANCH_WIDTH
POOL_WINDOWS = (2, 4, 8, 16)
POOL_GROUPS = len(POOL_WINDOWS)
POOL_GROUP = POOL_WIDTH // POOL_GROUPS
ATT_HEADS = 8
ATT_HEAD_DIM = 64
ATT_WIDTH = ATT_HEADS * ATT_HEAD_DIM
IDX_HEADS = 8
IDX_DIM = 64
MAX_TOPK = 256
MEM_HEADS = 4
MEM_HEAD_DIM = 128
MEM_WIDTH = MEM_HEADS * MEM_HEAD_DIM
D_FF = ((8 * D_MODEL // 3 + 255) // 256) * 256

IN_SIZES = (LRU_WIDTH,
            LRU_WIDTH,
            POOL_WIDTH,
            ATT_WIDTH,
            ATT_HEAD_DIM,
            ATT_HEAD_DIM,
            IDX_HEADS * IDX_DIM,
            IDX_DIM,
            IDX_HEADS,
            N_BRANCH * D_MODEL)
D_IN = sum(IN_SIZES)


def rms_norm_2(x, g):
    xf = x.astype(jnp.float32)
    y = xf * lax.rsqrt(jnp.mean(xf * xf, axis=-1, keepdims=True) + RMS_EPS)
    return (y * g.astype(jnp.float32)).astype(x.dtype)

def split_columns(h, sizes):
    parts, start = [], 0
    for n in sizes:
        parts.append(h[..., start:start + n])
        start += n
    return parts

def causal_depthwise_conv(x, w, b):
    c = x.shape[-1]
    y = lax.conv_general_dilated(x, w[:, None, :].astype(x.dtype), window_strides=(1,),
                                 padding=[(w.shape[0] - 1, 0)],
                                 dimension_numbers=('NWC', 'WIO', 'NWC'),
                                 feature_group_count=c)
    return y + b

def rg_lru(x, w_a, b_a, w_x, b_x, a_param):
    bsz, s, _ = x.shape
    xb = x.reshape(bsz, s, LRU_BLOCKS, LRU_BLOCK)
    r = jax.nn.sigmoid((jnp.einsum('bshi,hij->bshj', xb, w_a).reshape(bsz, s, LRU_WIDTH) + b_a).astype(jnp.float32))
    i = jax.nn.sigmoid((jnp.einsum('bshi,hij->bshj', xb, w_x).reshape(bsz, s, LRU_WIDTH) + b_x).astype(jnp.float32))
    log_a = -LRU_C * r * jax.nn.softplus(-a_param.astype(jnp.float32))
    a = jnp.exp(log_a)
    mult = jnp.sqrt(jnp.maximum(1.0 - jnp.exp(2.0 * log_a), 0.0))
    u = x.astype(jnp.float32) * i * mult

    def combine(left, right):
        return left[0] * right[0], right[0] * left[1] + right[1]

    _, h = lax.associative_scan(combine, (a, u), axis=1)
    return h.astype(x.dtype)

def multiscale_pool(p, w_pool, pool_scale):
    bsz, s, _ = p.shape
    pf = p.astype(jnp.float32).reshape(bsz, s, POOL_GROUPS, POOL_GROUP)
    cs = jnp.pad(jnp.cumsum(pf, axis=1), ((0, 0), (1, 0), (0, 0), (0, 0)))
    t = jnp.arange(s)
    means = []
    for g, w in enumerate(POOL_WINDOWS):
        start = jnp.maximum(t + 1 - w, 0)
        win_sum = cs[:, 1:, g] - cs[:, start, g]
        count = (t + 1 - start).astype(jnp.float32)[None, :, None]
        means.append(win_sum / count)
    pooled = jnp.stack(means, axis=2) - pf
    mixed = jnp.einsum('bsgc,gcd->bsgd', pooled, w_pool.astype(jnp.float32)).reshape(bsz, s, POOL_WIDTH)
    return (mixed * pool_scale.astype(jnp.float32)).astype(p.dtype)

def dsa_attention(q, k, v, q_idx, k_idx, w_idx):
    bsz, s = q.shape[:2]
    top_k = min(MAX_TOPK, s // 4)
    nb = s // Q_BLOCK
    key_chunk = jnp.arange(s) // CHUNK
    k_idx_f = k_idx.astype(jnp.float32)

    def to_blocks(a):
        return jnp.moveaxis(a.reshape(bsz, nb, Q_BLOCK, *a.shape[2:]), 1, 0)

    def one_block(args):
        qb, qib, wb, pos = args
        q_chunk = pos // CHUNK
        admissible = key_chunk[None, :] <= q_chunk[:, None]
        logits = jnp.einsum('bqhd,bsd->bqhs', qib.astype(jnp.float32), k_idx_f) * (IDX_DIM ** -0.5)
        score = jnp.einsum('bqh,bqhs->bqs', wb.astype(jnp.float32) * (IDX_HEADS ** -0.5), jax.nn.relu(logits))
        score = jnp.where(admissible[None], score, -jnp.inf)
        _, sel = lax.top_k(score, top_k)
        kg = jax.vmap(lambda kk, ii: kk[ii])(k, sel)
        vg = jax.vmap(lambda vv, ii: vv[ii])(v, sel)
        valid = key_chunk[sel] <= q_chunk[None, :, None]
        att = jnp.einsum('bqhd,bqkd->bqhk', qb, kg).astype(jnp.float32) * (ATT_HEAD_DIM ** -0.5)
        att = jnp.where(valid[:, :, None, :], att, -jnp.inf)
        prob = jax.nn.softmax(att, axis=-1).astype(vg.dtype)
        return jnp.einsum('bqhk,bqkd->bqhd', prob, vg)

    q_pos = jnp.arange(s).reshape(nb, Q_BLOCK)
    out = lax.map(one_block, (to_blocks(q), to_blocks(q_idx), to_blocks(w_idx), q_pos))
    return jnp.moveaxis(out, 0, 1).reshape(bsz, s, ATT_WIDTH)

def memory_cross_attention(h, m, w_q, w_kv, w_o):
    bsz, s, _ = h.shape
    q = (h @ w_q).reshape(bsz, s, MEM_HEADS, MEM_HEAD_DIM)
    k, v = jnp.split(m @ w_kv, 2, axis=-1)
    k = k.reshape(bsz, -1, MEM_HEADS, MEM_HEAD_DIM)
    v = v.reshape(bsz, -1, MEM_HEADS, MEM_HEAD_DIM)
    att = jnp.einsum('bshd,bmhd->bhsm', q, k).astype(jnp.float32) * (MEM_HEAD_DIM ** -0.5)
    prob = jax.nn.softmax(att, axis=-1).astype(v.dtype)
    o = jnp.einsum('bhsm,bmhd->bshd', prob, v).reshape(bsz, s, MEM_WIDTH)
    return o @ w_o

def second_inputs(seed: int = 0) -> dict:
    key = jax.random.key(seed)
    ks = iter(jax.random.split(key, 40))

    def nrm(shape, scale):
        return jax.random.normal(next(ks), shape, jnp.float32) * scale

    def gain(shape):
        return 1.0 + nrm(shape, 0.02)

    L = DEPTH_2
    u = jax.random.uniform(next(ks), (L, LRU_WIDTH), jnp.float32, 0.9, 0.999)
    a0 = u ** (1.0 / LRU_C)
    lru_a_param = jnp.log(a0) - jnp.log1p(-a0)
    return {
        'x': nrm((BATCH, SEQ, D_MODEL), 1.0),
        'mem': nrm((BATCH, N_MEM, D_MODEL), 1.0),
        'g_mix_pre': gain((L, D_MODEL)),
        'w_in': nrm((L, D_MODEL, D_IN), D_MODEL ** -0.5),
        'conv_w': nrm((L, CONV_WIDTH, LRU_WIDTH), CONV_WIDTH ** -0.5),
        'conv_b': nrm((L, LRU_WIDTH), 0.02),
        'lru_w_a': nrm((L, LRU_BLOCKS, LRU_BLOCK, LRU_BLOCK), LRU_BLOCK ** -0.5),
        'lru_b_a': nrm((L, LRU_WIDTH), 0.02),
        'lru_w_x': nrm((L, LRU_BLOCKS, LRU_BLOCK, LRU_BLOCK), LRU_BLOCK ** -0.5),
        'lru_b_x': nrm((L, LRU_WIDTH), 0.02),
        'lru_a_param': lru_a_param,
        'w_pool': nrm((L, POOL_GROUPS, POOL_GROUP, POOL_GROUP), POOL_GROUP ** -0.5),
        'pool_scale': gain((L, POOL_WIDTH)),
        'w_branch': nrm((L, N_BRANCH, BRANCH_WIDTH, D_MODEL), BRANCH_WIDTH ** -0.5),
        'b_gate': nrm((L, N_BRANCH, D_MODEL), 0.02),
        'w_out': nrm((L, D_MODEL, D_MODEL), D_MODEL ** -0.5),
        'g_mix_post': gain((L, D_MODEL)),
        'g_mem_pre': gain((L, D_MODEL)),
        'g_mem_kv': gain((L, D_MODEL)),
        'w_mem_q': nrm((L, D_MODEL, MEM_WIDTH), D_MODEL ** -0.5),
        'w_mem_kv': nrm((L, D_MODEL, 2 * MEM_WIDTH), D_MODEL ** -0.5),
        'w_mem_o': nrm((L, MEM_WIDTH, D_MODEL), MEM_WIDTH ** -0.5),
        'g_mem_post': gain((L, D_MODEL)),
        'g_ffn_pre': gain((L, D_MODEL)),
        'w_ffn_in': nrm((L, D_MODEL, 2 * D_FF), D_MODEL ** -0.5),
        'w_ffn_out': nrm((L, D_FF, D_MODEL), D_FF ** -0.5),
        'g_ffn_post': gain((L, D_MODEL)),
    }

def second_block(x, mem, g_mix_pre, w_in, conv_w, conv_b, lru_w_a, lru_b_a, lru_w_x, lru_b_x,
              lru_a_param, w_pool, pool_scale, w_branch, b_gate, w_out, g_mix_post,
              g_mem_pre, g_mem_kv, w_mem_q, w_mem_kv, w_mem_o, g_mem_post,
              g_ffn_pre, w_ffn_in, w_ffn_out, g_ffn_post):
    bsz, s, _ = x.shape
    for l in range(DEPTH_2):
        h = rms_norm_2(x, g_mix_pre[l])
        (lru_x, lru_gate, pool_in, q, k, v, q_idx, k_idx, w_idx,
         gate_logits) = split_columns(h @ w_in[l], IN_SIZES)
        ua = causal_depthwise_conv(lru_x, conv_w[l], conv_b[l])
        ya = rg_lru(ua, lru_w_a[l], lru_b_a[l], lru_w_x[l], lru_b_x[l], lru_a_param[l]) * jax.nn.gelu(lru_gate)
        yb = multiscale_pool(pool_in, w_pool[l], pool_scale[l])
        yc = dsa_attention(q.reshape(bsz, s, ATT_HEADS, ATT_HEAD_DIM), k, v,
                           q_idx.reshape(bsz, s, IDX_HEADS, IDX_DIM), k_idx, w_idx)
        up = jnp.einsum('bsnc,ncd->bsnd', jnp.stack([ya, yb, yc], axis=2), w_branch[l])
        gates = jax.nn.sigmoid(gate_logits.reshape(bsz, s, N_BRANCH, D_MODEL) + b_gate[l])
        merged = jnp.sum(gates * up, axis=2)
        x = x + rms_norm_2(merged @ w_out[l], g_mix_post[l])
        h = rms_norm_2(x, g_mem_pre[l])
        m = rms_norm_2(mem, g_mem_kv[l])
        x = x + rms_norm_2(memory_cross_attention(h, m, w_mem_q[l], w_mem_kv[l], w_mem_o[l]), g_mem_post[l])
        h = rms_norm_2(x, g_ffn_pre[l])
        f_gate, f_up = jnp.split(h @ w_ffn_in[l], 2, axis=-1)
        x = x + rms_norm_2((jax.nn.silu(f_gate) * f_up) @ w_ffn_out[l], g_ffn_post[l])
    return x


def setup_inputs(seed=0):
    out = dict(first_inputs(seed))
    for name, value in second_inputs(seed + 1).items():
        if name != "x":
            out[name + "_2"] = value
    return out


def reference(
    x, p, positions, norm_mix_pre, w_in, mla_q_norm, w_uq, mla_kv_norm, w_ukv, gqa_sink,
    w_branch_a, w_branch_b, w_branch_c, w_out, norm_mix_post, norm_ffn_pre, w_ffn_gate,
    w_ffn_up, w_ffn_down, norm_ffn_post, w_ple_proj, w_ple_gate, norm_ple, mem_2, g_mix_pre_2,
    w_in_2, conv_w_2, conv_b_2, lru_w_a_2, lru_b_a_2, lru_w_x_2, lru_b_x_2, lru_a_param_2,
    w_pool_2, pool_scale_2, w_branch_2, b_gate_2, w_out_2, g_mix_post_2, g_mem_pre_2,
    g_mem_kv_2, w_mem_q_2, w_mem_kv_2, w_mem_o_2, g_mem_post_2, g_ffn_pre_2, w_ffn_in_2,
    w_ffn_out_2, g_ffn_post_2,
):
    x = first_block(
        x, p, positions, norm_mix_pre, w_in, mla_q_norm, w_uq, mla_kv_norm, w_ukv, gqa_sink,
        w_branch_a, w_branch_b, w_branch_c, w_out, norm_mix_post, norm_ffn_pre, w_ffn_gate,
        w_ffn_up, w_ffn_down, norm_ffn_post, w_ple_proj, w_ple_gate, norm_ple,
    )
    return second_block(
        x, mem_2, g_mix_pre_2, w_in_2, conv_w_2, conv_b_2, lru_w_a_2, lru_b_a_2, lru_w_x_2,
        lru_b_x_2, lru_a_param_2, w_pool_2, pool_scale_2, w_branch_2, b_gate_2, w_out_2,
        g_mix_post_2, g_mem_pre_2, g_mem_kv_2, w_mem_q_2, w_mem_kv_2, w_mem_o_2, g_mem_post_2,
        g_ffn_pre_2, w_ffn_in_2, w_ffn_out_2, g_ffn_post_2,
    )


_drawn_inputs = setup_inputs


def setup_inputs(seed=0):
    import zlib

    import numpy as np

    out = dict(_drawn_inputs(seed))
    spreads = {}
    factors = {'mla_q_norm': 3.863,
     'gqa_sink': 5.128,
     'g_mix_pre_2': 5.053,
     'lru_b_a_2': 8.0,
     'lru_b_x_2': 8.0,
     'pool_scale_2': 8.0,
     'b_gate_2': 8.0,
     'g_mix_post_2': 7.368,
     'g_mem_pre_2': 8.0,
     'g_mem_kv_2': 5.414,
     'g_mem_post_2': 28.584,
     'g_ffn_pre_2': 21.753,
     'g_ffn_post_2': 37.976}
    for name, (base, spread) in spreads.items():
        noise = np.random.default_rng([zlib.crc32(name.encode()), seed]).standard_normal(out[name].shape)
        drawn = base * np.exp(spread * noise) if base else spread * noise
        out[name] = __import__('jax').numpy.asarray(drawn.astype(out[name].dtype))
    for name, factor in factors.items():
        out[name] = (out[name] * factor).astype(out[name].dtype)
    return out
```

```python
from contextlib import ExitStack

import numpy as np

import concourse.bass as bass
from concourse import mybir

F32 = mybir.dt.float32
F32R = mybir.dt.float32r
I32 = mybir.dt.int32
ALU = mybir.AluOpType
ACT = mybir.ActivationFunctionType
AX_X = mybir.AxisListType.X

P = 128
S = 512
D = 1024
DEPTH = 2
KD = D // P
ST = S // P
EPS = 1e-6
PLE_DIM = 256
MLA_HEADS, NOPE, ROPE, MLA_V = 8, 64, 32, 64
MLA_QK = NOPE + ROPE
Q_LORA, KV_LORA = 384, 128
GROUPS = 4
GW = D // GROUPS
HEADS, KV_HEADS, HD = 8, 2, 64
FFN = 2816
KF = FFN // P
N_MEM, MEM_HEADS = 256, 4
POOL_W = (2, 4, 8, 16)
PADW = 16
TOPK = 128
BLK = 16
UC = BLK * P
NEG = -1.0e38
TAKEN = -3.0e38
MASKED = -1.0e30
FAR = 1.0e30
TWO_PI_A = 6.28125
TWO_PI_B = 4059.0 / 2 ** 21
TWO_PI_C = 2 * np.pi - TWO_PI_A - TWO_PI_B
ROUND = 1.5 * 2 ** 23



def pair_tiles(first, second, n):
    out = []
    for m in range(n):
        at = m * (first + second)
        out += [list(range(at, at + first)), list(range(at + first, at + first + second))]
    return out


def plain_tiles(k, n):
    return [list(range(m * k, m * k + k)) for m in range(n)]


def down_tiles():
    out = []
    for m in range(KD):
        out.append([(m // 2) * 48 + (k // 8) * 16 + (m % 2) * 8 + k % 8 for k in range(KF)])
    return out


TILES = {
    "z1": plain_tiles(8, 11) + [list(range(80, 88))],
    "uq": plain_tiles(3, 8) + [[24 + j] for j in range(4)] + [[28, 29, 30, 31]] * 4,
    "bm": pair_tiles(8, 8, KD),
    "am": pair_tiles(8, 4, KD),
    "cm": pair_tiles(8, 4, KD),
    "bm2": pair_tiles(8, 4, KD),
    "wout": plain_tiles(8, KD),
    "gu": pair_tiles(8, 8, KF),
    "dn": down_tiles(),
    "pp": plain_tiles(2, KD),
    "ple": plain_tiles(8, KD),
    "z2": plain_tiles(8, 22) + [list(range(176, 184))] * 2,
    "lru": plain_tiles(1, 12),
    "mq": plain_tiles(8, 4),
    "mk": plain_tiles(8, 4),
    "mv": [list(range(32))] * 2,
    "mo": plain_tiles(4, KD),
}


def end_units(tiles):
    return [max(t) // BLK for t in tiles]


def releases(name):
    if name == "four1":
        return [("T", 16)]
    if name == "four2":
        return [("PU", 1), ("T", 4), ("PU", 2), ("T", 8)]
    tiles = TILES[name]
    units = max(max(t) for t in tiles) // BLK + 1
    out, parts = [], 0
    for u in range(units):
        if name == "dn":
            n, done = 2 * (u // 3) + 1, u % 3 == 2
        else:
            n = max(i for i, t in enumerate(tiles) if any(b // BLK == u for b in t))
            done = max(tiles[n]) // BLK == u
        parts += not done
        out.append(("T", n + 1) if done else ("PU", parts))
    return out


def stage(name, A=0, **more):
    c = dict(more)
    if name in TILES or name in ("four1", "four2"):
        rel = releases(name)
        c["U"] = len(rel)
        c["PU"] = sum(kind == "PU" for kind, _ in rel)
        c["T"] = {"four1": 16, "four2": 8}.get(name) or len(TILES[name])
    c["A"] = A
    return name, c


STAGES1 = [
    stage("norm1", R=8, SQ=8, SS=8, N=1),
    stage("four1", A=16), stage("four2", A=8), stage("bm", A=8),
    stage("z1", A=7, SS=4), stage("qn", N=2, R=4), stage("uq", A=16),
    stage("mla", I=32, H=8, O=4), stage("gqa", I=32, H=8, O=4),
    stage("am", A=8), stage("cm", A=8, R=8),
    stage("wout", A=8, SS=2, AD=6), stage("post1", N=1, X=8),
    stage("norm2", R=8, SQ=8, SS=8, N=1), stage("gu", A=KF, R=KF),
    stage("dn", A=8, SS=2, AD=6), stage("post2", N=1, X=8),
    stage("pp", A=8), stage("xple", R=8), stage("ple", A=8, SQ=8, SS=2, AD=6), stage("post3", N=1, X=8),
]
STAGES2 = [
    stage("norm1", R=8, SQ=8, SS=8, N=1),
    stage("z2", A=14, R=8), stage("lru", A=12, R=4), stage("idx"),
    stage("bm2", A=8), stage("am", A=8), stage("dsa", I=32, H=8, O=4), stage("cm", A=8, R=8),
    stage("wout", A=8, SS=2, AD=6), stage("post1", N=1, X=8),
    stage("normh", R=8, SQ=8, SS=8, N=1), stage("normm", R=8, SQ=8, SS=8, N=1),
    stage("mq", A=4), stage("mk", A=4), stage("mv", A=2), stage("mem", I=16, H=4, O=4),
    stage("mo", A=8, SS=2, AD=6), stage("postm", N=1, X=8),
    stage("norm2", R=8, SQ=8, SS=8, N=1), stage("gu", A=KF, R=KF),
    stage("dn", A=8, SS=2, AD=6), stage("post2", N=1, X=8),
]
KINDS = ("U", "T", "PU", "A", "R", "SQ", "AD", "SS", "N", "X", "I", "H", "O")


def bases(stages):
    at, out = dict.fromkeys(KINDS, 0), {}
    for name, c in stages:
        out[name] = dict(at)
        for k in KINDS:
            at[k] += c.get(k, 0)
    return out, at


BASE1, TOTAL1 = bases(STAGES1)
BASE2, TOTAL2 = bases(STAGES2)
UNITS = DEPTH * TOTAL1["U"] + TOTAL2["U"]
UNITS_PADDED = UNITS + UNITS % 2
assert TOTAL1["U"] % 2 == 0 and TOTAL1["T"] % 4 == 0
CHAIN_PER_LAYER = 1024

VEC1, _n = {}, 0
for _name, _w in (("mix_pre", 8), ("q_norm", 3), ("kv_norm", 1), ("mix_post", 8), ("ffn_pre", 8), ("ffn_post", 8),
                  ("ple", 8), ("sink", 8)):
    VEC1[_name] = _n
    _n += _w
NV1 = _n
CST, _n = {}, 0
for _name, _w in (("ident", P), ("ones", P), ("window", 3 * P), ("freq", 1), ("phase", 1), ("sign", 1), ("head", 64),
                  ("mix_pre", 8), ("mix_post", 8), ("mem_pre", 8), ("mem_kv", 8), ("mem_post", 8), ("ffn_pre", 8),
                  ("ffn_post", 8), ("conv_w", 16), ("conv_b", 4), ("b_a", 4), ("b_x", 4), ("a_param", 4),
                  ("pool", 4), ("b_gate", 24)):
    CST[_name] = _n
    _n += _w
NCST = _n
KB = 1024
MAP_AT = 2304


class Counts:

    def __init__(self, base, layer):
        self.base, self.layer = base, layer

    def at(self, kind, stage_name, n):
        return self.layer * TOTAL1[kind] + (self.base[stage_name][kind] + n)

    def raw(self, u):
        return (self.layer * (TOTAL1["U"] // 2) + (u // 2 + 1)) * 16


def block_kernel(nc, stream, xT, pT, memT, vec1, cst, pos, out):
    with ExitStack() as ctx:
        def sem(name):
            return ctx.enter_context(nc.semaphore(name))

        def sb(name, kb, shape, dt=F32):
            return nc.alloc_sbuf_tensor_at(name, [P] + shape, dt, offset=MAP_AT + int(kb * KB))

        raw = [sb(f"raw{i}", 8 * i, [UC]) for i in range(2)]
        w_hi = [sb(f"w_hi{i}", 16 + 8 * i, [UC], F32R) for i in range(2)]
        w_lo = [sb(f"w_lo{i}", 32 + 8 * i, [UC], F32R) for i in range(2)]
        x = sb("x", 48, [KD, S])
        h_hi = sb("h_hi", 64, [KD, S], F32R)
        h_lo = sb("h_lo", 80, [KD, S], F32R)
        y = sb("y", 64, [KD, S])
        res = sb("res", 96, [4, S])
        sg = sb("sg", 104, [2, S])
        sq = sb("sq", 108, [2, S])
        rstd = sb("rstd", 112, [2, S])
        sq_acc = rstd[:, 1, :]
        st_max = sb("st_max", 116, [32])
        st_neg = sb("st_neg", 116.25, [32])
        st_sum = sb("st_sum", 116.5, [32])
        st_rec = sb("st_rec", 116.75, [32])
        st_snk = sb("st_snk", 117, [32])
        top8 = sb("top8", 117.25, [8])
        wsc = sb("wsc", 117.5, [ST, 8])
        lruc = sb("lruc", 117.75, [4, 8])
        cs = sb("cs", 118, [S])
        cst_sb = sb("cst_sb", 120, [NCST])
        vec = sb("vec", 124, [NV1])
        posf = sb("posf", 124.5, [S + ST])
        AR = 128

        def ar(name, kb, shape, dt=F32):
            return sb(name, AR + kb, shape, dt)

        U_hi = ar("U_hi", 0, [GROUPS, ST, S], F32R)
        U_lo = ar("U_lo", 32, [GROUPS, ST, S], F32R)
        ob_hi = ar("ob_hi", 64, [KD, S], F32R)
        ob_lo0 = ar("ob_lo0", 80, [4, S], F32R)
        ob_lo1 = ar("ob_lo1", 0, [4, S], F32R)
        merged1 = ar("merged1", 8, [KD, S])
        cq = ar("cq", 24, [4, S])
        cqn_hi = ar("cqn_hi", 32, [4, S], F32R)
        cqn_lo = ar("cqn_lo", 40, [4, S], F32R)
        qc = ar("qc", 48, [4, S])
        kdup = ar("kdup", 56, [KV_HEADS, S])
        vc = ar("vc", 60, [ST, P])
        kr = ar("kr", 62, [S])
        q_a = ar("q_a", 64, [MLA_HEADS, S])
        k_a = [ar("k_a0", 80, [4, S]), ar("k_a1", 0, [4, S])]
        v_a = ar("v_a", 24, [ST, S])
        dist = ar("dist", 32, [ST, 3 * P])
        pT0_1 = ar("pT0_1", 38, [ST, S])
        oa_hi = [ar(f"oa_hi{i}", 64 + 4 * i, [S], F32R) for i in range(4)]
        oa_lo = [ar(f"oa_lo{i}", 66 + 4 * i, [S], F32R) for i in range(4)]
        oc_hi = ar("oc_hi", 80, [4, S], F32R)
        oc_lo = ar("oc_lo", 0, [4, S], F32R)
        m_hi1 = ar("m_hi1", 24, [KD, S], F32R)
        m_lo1 = ar("m_lo1", 40, [KD, S], F32R)
        a_hi = ar("a_hi", 0, [KF, S], F32R)
        a_lo = ar("a_lo", 44, [KF, S], F32R)
        e = ar("e", 0, [KD, S])
        p_f = ar("p_f", 88, [2, S])
        p_hi = sb("p_hi", 88, [2, S], F32R)
        p_lo = sb("p_lo", 92, [2, S], F32R)
        pT1 = sb("pT1", 96, [ST, S])
        prob1 = [sb("prob1_0", 104, [S]), sb("prob1_1", 106, [S]), ar("prob1_2", 46, [S])]
        rope_t = [sb("rope_t0", 104, [S]), sb("rope_t1", 106, [S])]
        pos_i = ar("pos_i", 0, [S + ST], I32)
        ang = [ar(f"ang{i}", 4 + 2 * i, [S]) for i in range(4)]
        lx = ar("lx", 0, [4, S])
        lg = ar("lg", 8, [4, S])
        qd = ar("qd", 16, [4, S])
        qi = ar("qi", 24, [4, S])
        kk = ar("kk", 32, [S])
        ki = ar("ki", 34, [S])
        vw = ar("vw", 36, [ST, P])
        pz = ar("pz", 38, [4, PADW + S])
        win = [ar("win0", 46.5, [PADW + S]), ar("win1", 48.75, [PADW + S])]
        pool_hi = ar("pool_hi", 51, [4, S], F32R)
        pool_lo = ar("pool_lo", 59, [4, S], F32R)
        ua = ar("ua", 67, [4, S])
        ua_hi = ar("ua_hi", 75, [4, S], F32R)
        ua_lo = ar("ua_lo", 83, [4, S], F32R)
        lr = ar("lr", 38, [4, S])
        li = ar("li", 75, [4, S])
        lm = ar("lm", 83, [4, S])
        yb_hi = ar("yb_hi", 51, [4, S], F32R)
        yb_lo = ar("yb_lo", 59, [4, S], F32R)
        ya_hi = ar("ya_hi", 0, [4, S], F32R)
        ya_lo = ar("ya_lo", 8, [4, S], F32R)
        score = ar("score", 38, [ST, S])
        merged2 = ar("merged2", 75, [KD, S])
        pT0_2 = ar("pT0_2", 67, [ST, S])
        prob2 = [sb("prob2_0", 104, [S]), sb("prob2_1", 106, [S]), ar("prob2_2", 46.5, [S])]
        od_hi = ar("od_hi", 16, [4, S], F32R)
        od_lo = ar("od_lo", 24, [4, S], F32R)
        m_hi2 = ar("m_hi2", 0, [KD, S], F32R)
        m_lo2 = ar("m_lo2", 51, [KD, S], F32R)
        mq = ar("mq", 0, [4, S])
        memf = ar("memf", 8, [KD, N_MEM])
        mem_hi = ar("mem_hi", 16, [KD, N_MEM], F32R)
        mem_lo = ar("mem_lo", 24, [KD, N_MEM], F32R)
        mk = ar("mk", 32, [4, N_MEM])
        mv = ar("mv", 36, [2, S])
        pT0_m = ar("pT0_m", 40, [ST, S])
        prob_m = [sb("prob_m0", 104, [S]), sb("prob_m1", 106, [S]), ar("prob_m2", 48, [S])]
        om_hi = ar("om_hi", 50, [4, S], F32R)
        om_lo = ar("om_lo", 58, [4, S], F32R)

        bank = [ctx.enter_context(nc.psum_tensor(f"bank{i}", [P, S], F32)) for i in range(8)]
        SS_BANK, SS_BANK2 = bank[7], bank[6]

        ident = cst_sb[:, CST["ident"]:CST["ident"] + P]
        ones = cst_sb[:, CST["ones"]:CST["ones"] + P]

        def cc(name, j=0, lo=0, hi=P):
            return cst_sb[lo:hi, CST[name] + j:CST[name] + j + 1]

        def vv(name, j=0):
            return vec[:, VEC1[name] + j:VEC1[name] + j + 1]

        raw_ready = [sem("raw_ready0"), sem("raw_ready1")]
        hi_ready = sem("hi_ready")
        lo_ready = sem("lo_ready")
        tile_done = sem("tile_done")
        part_done = sem("part_done")
        act_took = sem("act_took")
        tile_free = sem("tile_free")
        x_loaded = sem("x_loaded")
        x_ready = sem("x_ready")
        res_ready = sem("res_ready")
        res_hi = sem("res_hi")
        res_split = sem("res_split")
        sq_ready = sem("sq_ready")
        sq_added = sem("sq_added")
        ss_done = sem("ss_done")
        rms_ready = sem("rms_ready")
        vec_loaded = sem("vec_loaded")
        p_loaded = sem("p_loaded")
        p_hi_ready = sem("p_hi_ready")
        p_split = sem("p_split")
        cst_loaded = sem("cst_loaded")
        pos_loaded = sem("pos_loaded")
        mem_loaded = sem("mem_loaded")
        pos_ready = sem("pos_ready")
        angle_ready = sem("angle_ready")
        sin_ready = sem("sin_ready")
        kr_copied = sem("kr_copied")
        dist_ready = sem("dist_ready")
        logits_done = sem("logits_done")
        shift_ready = sem("shift_ready")
        exp_done = sem("exp_done")
        prob_ready = sem("prob_ready")
        turned = sem("turned")
        turn_taken = sem("turn_taken")
        head_done = sem("head_done")
        o_hi_ready = sem("o_hi_ready")
        o_split = sem("o_split")
        vchain = sem("vchain")
        achain = sem("achain")
        pad_ready = sem("pad_ready")
        lru_gates = sem("lru_gates")
        softplus_ready = sem("softplus_ready")
        idx_done = sem("idx_done")
        idx_relu = sem("idx_relu")
        idx_added = sem("idx_added")
        out_done = sem("out_done")

        block = ctx.enter_context(nc.Block())

        def windowed(b):
            return range(max(b - 1, 0), min(b + 2, ST))

        ATT = {
            "mla": dict(heads=8, keys=lambda b: range(ST), scale=MLA_QK ** -0.5, pT=[pT0_1, pT1], prob=prob1, biased=False,
                        q=lambda h, b: q_a[0:MLA_QK, h, b * P:(b + 1) * P],
                        k=lambda h, ks: k_a[h // 4][0:MLA_QK, h % 4, ks.start * P:ks.stop * P],
                        v=lambda h, t: v_a[:, t, h * MLA_V:(h + 1) * MLA_V],
                        o=lambda i: (oa_hi[i][:, :], oa_lo[i][:, :]), per_tile=2),
            "gqa": dict(heads=8, keys=windowed, scale=HD ** -0.5, pT=[pT0_1, pT1], prob=prob1, biased=True,
                        q=lambda h, b: qc[64 * (h % 2):64 * (h % 2) + 64, h // 2, b * P:(b + 1) * P],
                        k=lambda h, ks: kdup[64 * (h % 2):64 * (h % 2) + 64, h // 4, ks.start * P:ks.stop * P],
                        v=lambda h, t: vc[:, t, (h // 4) * HD:(h // 4 + 1) * HD],
                        o=lambda i: (oc_hi[:, i, :], oc_lo[:, i, :]), per_tile=2),
            "dsa": dict(heads=8, keys=lambda b: range(b + 1), scale=HD ** -0.5, pT=[pT0_2, pT1], prob=prob2, biased=True,
                        q=lambda h, b: qd[64 * (h % 2):64 * (h % 2) + 64, h // 2, b * P:(b + 1) * P],
                        k=lambda h, ks: kk[64 * (h % 2):64 * (h % 2) + 64, ks.start * P:ks.stop * P],
                        v=lambda h, t: vw[:, t, 0:HD],
                        o=lambda i: (od_hi[:, i, :], od_lo[:, i, :]), per_tile=2),
            "mem": dict(heads=MEM_HEADS, keys=lambda b: range(N_MEM // P), scale=P ** -0.5, pT=[pT0_m, pT1], prob=prob_m,
                        biased=False,
                        q=lambda h, b: mq[:, h, b * P:(b + 1) * P],
                        k=lambda h, ks: mk[:, h, ks.start * P:ks.stop * P],
                        v=lambda h, t: mv[:, t, h * P:(h + 1) * P],
                        o=lambda i: (om_hi[:, i, :], om_lo[:, i, :]), per_tile=1),
        }

        NORMS = {
            1: {"norm1": ("mix_pre", x, h_hi, h_lo, S), "norm2": ("ffn_pre", x, h_hi, h_lo, S)},
            2: {"norm1": ("mix_pre", x, h_hi, h_lo, S), "norm2": ("ffn_pre", x, h_hi, h_lo, S),
                "normh": ("mem_pre", x, h_hi, h_lo, S), "normm": ("mem_kv", memf, mem_hi, mem_lo, N_MEM)},
        }
        MERGES = {
            (1, "bm"): lambda k: (ob_hi[:, k, :], (ob_lo0 if k < 4 else ob_lo1)[:, k % 4, :]),
            (1, "am"): lambda k: (oa_hi[k][:, :], oa_lo[k][:, :]),
            (1, "cm"): lambda k: (oc_hi[:, k, :], oc_lo[:, k, :]),
            (2, "bm2"): lambda k: (yb_hi[:, k, :], yb_lo[:, k, :]),
            (2, "am"): lambda k: (ya_hi[:, k, :], ya_lo[:, k, :]),
            (2, "cm"): lambda k: (od_hi[:, k, :], od_lo[:, k, :]),
        }
        MERGED = {1: (merged1, m_hi1, m_lo1), 2: (merged2, m_hi2, m_lo2)}

        @block.sync
        def _(sp):
            for p in range(2):
                sp.dma_start(raw[p][:, :], stream[p]).then_inc(raw_ready[p], 16)
                if p == 0:
                    sp.dma_start(x[:, :, :], xT.rearrange("(k p) s -> p k s", p=P)).then_inc(x_loaded, 16)
            with sp.Fori(1, UNITS_PADDED // 2) as i:
                for p in range(2):
                    sp.wait_ge(lo_ready, i * 2 + (p - 1))
                    sp.dma_start(raw[p][:, :], stream[bass.ds(i * 2 + p, 1)].rearrange("a p n -> (a p) n")).then_inc(raw_ready[p], 16)
            for p in range(2):
                sp.wait_ge(raw_ready[p], 16 * (UNITS_PADDED // 2))

        @block.tensor
        def _(pe):
            def mac(ps, w, bb, ncol, xh, xl, start, stop, swap=False):
                wh = w_hi[w][:, bb * P:bb * P + ncol]
                wl = w_lo[w][:, bb * P:bb * P + ncol]
                if swap:
                    nc.tensor.matmul(ps, xh, wh, start=start, stop=False)
                    nc.tensor.matmul(ps, xh, wl, start=False, stop=False)
                    return nc.tensor.matmul(ps, xl, wh, start=False, stop=stop)
                nc.tensor.matmul(ps, wh, xh, start=start, stop=False)
                nc.tensor.matmul(ps, wh, xl, start=False, stop=False)
                return nc.tensor.matmul(ps, wl, xh, start=False, stop=stop)

            def free_bank(c, st, n):
                t = c.base[st]["T"] + n
                if t >= 4 or c.base is BASE2:
                    pe.wait_ge(tile_free, c.at("T", st, n - 3))
                return bank[t % 4]

            def run(c, st, operand, first=0, last=None, width=S, after=None, together=False):
                tiles = TILES[st]
                u0 = c.base[st]["U"]
                ends = {}
                for n, t in enumerate(tiles):
                    for j, b in enumerate(t):
                        ends[b // BLK] = (n, j)
                seen = -1 if first == 0 else tiles[first - 1][-1] // BLK
                if together:
                    pe.wait_ge(lo_ready, c.at("U", st, 1))
                    seen, first = 0, 2
                    two = [free_bank(c, st, n)[:, 0:width] for n in range(2)]
                    for j in range(KD):
                        for n in range(2):
                            xh, xl, need = operand(n, j)
                            if need is not None:
                                pe.wait_ge(need[0], need[1])
                            mm = mac(two[n], u0 % 2, tiles[n][j], P, xh, xl, j == 0, j == KD - 1)
                            if j == KD - 1:
                                mm.then_inc(tile_done, 1)
                for n in range(first, len(tiles) if last is None else last):
                    t = tiles[n]
                    ps = free_bank(c, st, n)[:, 0:width]
                    for j, b in enumerate(t):
                        u = b // BLK
                        if u > seen:
                            pe.wait_ge(lo_ready, c.at("U", st, u + 1))
                            seen = u
                        xh, xl, need = operand(n, j)
                        if need is not None:
                            pe.wait_ge(need[0], need[1])
                        mm = mac(ps, (u0 + u) % 2, b % BLK, P, xh, xl, j == 0, j == len(t) - 1)
                        if j == len(t) - 1:
                            mm.then_inc(tile_done, 1)
                        elif ends[u] == (n, j):
                            mm.then_inc(part_done, 1)
                    if after is not None:
                        after(n)

            def down(c, a_need):
                st = "dn"
                u0 = c.base[st]["U"]
                for u in range(12):
                    pair, part = u // 3, u % 3
                    pe.wait_ge(lo_ready, c.at("U", st, u + 1))
                    ks = range(8 * part, min(8 * part + 8, KF))
                    for q in range(2):
                        n = 2 * pair + q
                        ps = free_bank(c, st, n) if part == 0 else bank[(c.base[st]["T"] + n) % 4]
                        for k in ks:
                            if u == 0 and q == 0 or k >= 16 and u == 2 and q == 0 or k >= 8 and u == 1 and q == 0:
                                pe.wait_ge(res_split, a_need(k))
                            mm = mac(ps[:, :], (u0 + u) % 2, 8 * q + k % 8, P, a_hi[:, k, :], a_lo[:, k, :],
                                     k == 0, k == KF - 1)
                        if part == 2:
                            mm.then_inc(tile_done, 1)
                        elif q == 1:
                            mm.then_inc(part_done, 1)
                project_sum(c, "dn", act_took, "A")

            def square_sum(ready, value, src, start, stop, ps=None):
                pe.wait_ge(ready, value)
                ps = SS_BANK if ps is None else ps
                nc.tensor.matmul(ps[:, 0:src.shape[-1]], ones, src, start=start, stop=stop).then_inc(ss_done, 1)

            def project_sum(c, st, ready, kind):
                square_sum(sq_added, c.at("AD", st, 6), sq_acc, True, False)
                square_sum(ready, c.at(kind, st, KD), sq[:, 1, :], False, True)

            def norm(c, st, which):
                width = NORMS[which][st][4]
                for m in range(KD):
                    square_sum(sq_ready, c.at("SQ", st, m + 1), sq[:, m % 2, 0:width], m == 0, m == KD - 1)

            def attention(c, st, ready):
                a = ATT[st]
                items = [(h, b) for h in range(a["heads"]) for b in range(ST)]
                for sem_, value in ready:
                    pe.wait_ge(sem_, value)
                for t in range(len(items) + 2):
                    if t < len(items):
                        h, b = items[t]
                        if t >= 3:
                            pe.wait_ge(exp_done, c.at("I", st, t - 2))
                        ks = a["keys"](b)
                        nc.tensor.matmul(bank[t % 3][:, 0:len(ks) * P], a["q"](h, b), a["k"](h, ks),
                                         start=True, stop=True).then_inc(logits_done, 1)
                    if t >= 2:
                        i = t - 2
                        h, b = items[i]
                        pe.wait_ge(prob_ready, c.at("I", st, i + 1))
                        if i >= 2:
                            pe.wait_ge(turn_taken, c.at("I", st, i - 1))
                        n = len(a["keys"](b))
                        for j in range(n):
                            mm = nc.tensor.transpose(bank[3 + i % 2][:, j * P:(j + 1) * P],
                                                     a["prob"][i % 3][:, j * P:(j + 1) * P], ident)
                        mm.then_inc(turned, 1)
                        if b == ST - 1 and h >= 1:
                            values(c, st, h - 1)
                values(c, st, a["heads"] - 1)

            def values(c, st, h):
                a = ATT[st]
                per = a["per_tile"]
                pe.wait_ge(turn_taken, c.at("I", st, ST * h + ST))
                tile = h // per
                if h % per == 0 and tile >= 2:
                    pe.wait_ge(o_split, c.at("O", st, tile - 1))
                rows = P // per
                ps = bank[5 + tile % 2]
                lo = rows * (h % per)
                if len(set(tuple(a["keys"](b)) for b in range(ST))) == 1:
                    n = len(a["keys"](0))
                    for t in range(n):
                        mm = nc.tensor.matmul(ps[lo:lo + rows, :], a["v"](h, t), a["pT"][h % 2][:, t, :],
                                              start=t == 0, stop=t == n - 1)
                else:
                    for b in range(ST):
                        ks = a["keys"](b)
                        for j, t in enumerate(ks):
                            mm = nc.tensor.matmul(ps[lo:lo + rows, b * P:(b + 1) * P], a["v"](h, t),
                                                  a["pT"][h % 2][:, j, b * P:(b + 1) * P],
                                                  start=j == 0, stop=j == len(ks) - 1)
                mm.then_inc(head_done, 1)

            def merge(c, which, st, need=None):
                def operand(n, j):
                    if n % 2 == 0:
                        return h_hi[:, j, :], h_lo[:, j, :], None
                    xh, xl = MERGES[which, st](j)
                    return xh, xl, need(j) if need is not None and n == 1 else None
                run(c, st, operand)

            def project(c, st, hi, lo, need):
                run(c, st, lambda n, j: (hi(j), lo(j), need(j) if n == 0 else None))
                project_sum(c, st, act_took, "A")

            def gate_up(c):
                st = "gu"
                u0, t0 = c.base[st]["U"], c.base[st]["T"]

                def pair(i, waits):
                    for p in range(2):
                        pe.wait_ge(lo_ready, c.at("U", st, p + 1) + i * 2)
                        if waits and p == 0:
                            pe.wait_ge(tile_free, c.at("T", st, -2))
                            for k in range(KD):
                                pe.wait_ge(res_split, c.at("R", "norm2", k + 1))
                                for g in range(2):
                                    mm = mac(bank[(t0 + g) % 4][:, :], u0 % 2, 8 * g + k, P, h_hi[:, k, :], h_lo[:, k, :],
                                             k == 0, k == KD - 1)
                                    if k == KD - 1:
                                        mm.then_inc(tile_done, 1)
                            continue
                        for g in range(2):
                            pe.wait_ge(tile_free, c.at("T", st, 2 * p + g - 3) + i * 4)
                            for k in range(KD):
                                mm = mac(bank[(t0 + 2 * p + g) % 4][:, :], (u0 + p) % 2, 8 * g + k, P,
                                         h_hi[:, k, :], h_lo[:, k, :], k == 0, k == KD - 1)
                            mm.then_inc(tile_done, 1)
                pair(0, True)
                with pe.Fori(1, KF // 2) as i:
                    pair(i, False)

            def first_block(L):
                c = Counts(BASE1, L)
                norm(c, "norm1", 1)
                pe.wait_ge(lo_ready, c.at("U", "four1", 1))
                u = c.base["four1"]["U"] % 2
                for n in range(16):
                    g, t = n // ST, n % ST
                    ps = free_bank(c, "four1", n)
                    for j in range(2):
                        k = 2 * g + j
                        if t == 0:
                            pe.wait_ge(res_split, c.at("R", "norm1", k + 1))
                        mm = mac(ps[:, :], u, 4 * j, S, h_hi[:, k, t * P:(t + 1) * P], h_lo[:, k, t * P:(t + 1) * P],
                                 j == 0, j == 1, swap=True)
                    mm.then_inc(tile_done, 1)
                for half in range(2):
                    for part in range(2):
                        n_u = 2 * half + part
                        pe.wait_ge(lo_ready, c.at("U", "four2", n_u + 1))
                        u = (c.base["four2"]["U"] + n_u) % 2
                        for j in range(4):
                            m = 4 * half + j
                            g, col = m // 2, part * GW + (m % 2) * P
                            ps = free_bank(c, "four2", m) if part == 0 else bank[(c.base["four2"]["T"] + m) % 4]
                            if part == 0 and j % 2 == 0:
                                pe.wait_ge(tile_free, c.at("T", "four1", 4 * g + 4))
                            for t in range(ST):
                                mm = mac(ps[:, :], u, 4 * t, S, U_hi[:, g, t, col:col + P], U_lo[:, g, t, col:col + P],
                                         part == 0 and t == 0, part == 1 and t == ST - 1, swap=True)
                            if part == 1:
                                mm.then_inc(tile_done, 1)
                        if part == 0:
                            mm.then_inc(part_done, 1)
                merge(c, 1, "bm", lambda k: (tile_free, c.at("T", "four2", k + 1)))
                def after_z1(n):
                    if 1 <= n <= 3:
                        square_sum(act_took, c.at("A", "z1", n), sq[:, (n - 1) % 2, :], n == 1, n == 3)
                    if n == 4:
                        square_sum(act_took, c.at("A", "z1", 4), sq[:, 1, :], True, True, ps=SS_BANK2)
                run(c, "z1", lambda n, j: (h_hi[:, j, :], h_lo[:, j, :], None), last=10, after=after_z1)
                values_by_token(c, "z1", 10, lambda t, k: (h_hi[:, k, t * P:(t + 1) * P], h_lo[:, k, t * P:(t + 1) * P]))
                run(c, "uq", lambda n, j: (cqn_hi[:, j if n < 8 else 3, :], cqn_lo[:, j if n < 8 else 3, :],
                                           (res_split, c.at("R", "qn", (j if n < 8 else 3) + 1)) if n in (0, 8) else None), last=12)
                for t in range(ST):
                    ps = free_bank(c, "uq", 12 + t)
                    mac(ps[:, :], (c.base["uq"]["U"] + 1) % 2, 12, S, cqn_hi[:, 3, t * P:(t + 1) * P],
                        cqn_lo[:, 3, t * P:(t + 1) * P], True, True, swap=True).then_inc(tile_done, 1)
                attention(c, "mla", [(tile_free, c.at("T", "uq", 16)), (kr_copied, c.layer + 1)])
                attention(c, "gqa", [])
                merge(c, 1, "am", lambda k: (o_split, c.at("O", "mla", k + 1)))
                merge(c, 1, "cm", lambda k: (o_split, c.at("O", "gqa", k + 1)))
                project(c, "wout", lambda k: m_hi1[:, k, :], lambda k: m_lo1[:, k, :],
                        lambda k: (res_split, c.at("R", "cm", k + 1)))
                norm(c, "norm2", 1)
                gate_up(c)
                down(c, lambda k: c.at("R", "gu", k + 1))

                run(c, "pp", lambda n, j: (p_hi[:, j, :], p_lo[:, j, :], (p_split, c.layer + 1) if n == 0 and j == 0 else None))
                run(c, "ple", lambda n, j: (h_hi[:, j, :], h_lo[:, j, :], (res_split, c.at("R", "xple", j + 1)) if n == 0 else None),
                    together=True)
                project_sum(c, "ple", sq_ready, "SQ")

            def values_by_token(c, st, n0, x_of):
                t0 = TILES[st][n0]
                u = t0[0] // BLK
                pe.wait_ge(lo_ready, c.at("U", st, u + 1))
                for q in range(2):
                    ps = free_bank(c, st, n0 + q)
                    for half in range(2):
                        for k, b in enumerate(t0):
                            xh, xl = x_of(2 * q + half, k)
                            mm = mac(ps[:, half * P:(half + 1) * P], (c.base[st]["U"] + u) % 2, b % BLK, P, xh, xl,
                                     k == 0, k == KD - 1, swap=True)
                    mm.then_inc(tile_done, 1)

            pe.wait_ge(cst_loaded, 16)
            with pe.Fori(0, DEPTH) as L:
                first_block(L)

            c = Counts(BASE2, DEPTH)
            norm(c, "norm1", 2)
            run(c, "z2", lambda n, j: (h_hi[:, j, :], h_lo[:, j, :], (res_split, c.at("R", "norm1", j + 1)) if n == 0 else None),
                last=22, together=True)
            values_by_token(c, "z2", 22, lambda t, k: (h_hi[:, k, t * P:(t + 1) * P], h_lo[:, k, t * P:(t + 1) * P]))

            def lru_operand(n, j):
                if n < 4:
                    return pool_hi[:, n, :], pool_lo[:, n, :], (res_split, c.at("R", "z2", 4 + n + 1))
                return ua_hi[:, n % 4, :], ua_lo[:, n % 4, :], (res_split, c.at("R", "z2", n % 4 + 1)) if n < 8 else None
            run(c, "lru", lru_operand)
            pe.wait_ge(tile_free, c.at("T", "lru", 12))
            for t in range(32):
                b, hh = t // 8, t % 8
                if t >= 3:
                    pe.wait_ge(idx_relu, t - 2)
                r = slice(64 * (hh % 2), 64 * (hh % 2) + 64)
                nc.tensor.matmul(bank[t % 3][:, 0:(b + 1) * P], qi[r, hh // 2, b * P:(b + 1) * P], ki[r, 0:(b + 1) * P],
                                 start=True, stop=True).then_inc(idx_done, 1)
            pe.wait_ge(idx_relu, 32)
            merge(c, 2, "bm2", lambda k: (tile_free, c.at("T", "lru", k + 1)))
            merge(c, 2, "am", lambda k: (res_split, c.at("R", "lru", k + 1)))
            attention(c, "dsa", [(tile_free, c.at("T", "am", 16))])
            merge(c, 2, "cm", lambda k: (o_split, c.at("O", "dsa", k + 1)))
            project(c, "wout", lambda k: m_hi2[:, k, :], lambda k: m_lo2[:, k, :], lambda k: (res_split, c.at("R", "cm", k + 1)))
            norm(c, "normh", 2)
            norm(c, "normm", 2)
            run(c, "mq", lambda n, j: (h_hi[:, j, :], h_lo[:, j, :], (res_split, c.at("R", "normh", j + 1)) if n == 0 else None),
                together=True)
            run(c, "mk", lambda n, j: (mem_hi[:, j, :], mem_lo[:, j, :], (res_split, c.at("R", "normm", j + 1)) if n == 0 else None),
                width=N_MEM, together=True)
            for half in range(2):
                pe.wait_ge(lo_ready, c.at("U", "mv", half + 1))
                for t in range(2):
                    ps = free_bank(c, "mv", t) if half == 0 else bank[(c.base["mv"]["T"] + t) % 4]
                    for j in range(4):
                        k = 4 * half + j
                        mm = mac(ps[:, :], (c.base["mv"]["U"] + half) % 2, 4 * j, S, mem_hi[:, k, t * P:(t + 1) * P],
                                 mem_lo[:, k, t * P:(t + 1) * P], k == 0, k == KD - 1, swap=True)
                    if half == 1:
                        mm.then_inc(tile_done, 1)
                if half == 0:
                    mm.then_inc(part_done, 1)
            attention(c, "mem", [(tile_free, c.at("T", "mv", 2))])
            project(c, "mo", lambda k: om_hi[:, k, :], lambda k: om_lo[:, k, :], lambda k: (o_split, c.at("O", "mem", k + 1)))
            norm(c, "norm2", 2)
            gate_up(c)
            down(c, lambda k: c.at("R", "gu", k + 1))

        RR1, RR2 = {}, {}
        for table, stages in ((RR1, STAGES1), (RR2, STAGES2)):
            n = 0
            for name, cnt in stages:
                table[name] = n
                n += 0 if name in ("gu", "xple") else cnt.get("R", 0)
            table["all"] = n

        def result_value(c, st, m):
            return c.layer * RR1["all"] + ((RR1 if c.base is BASE1 else RR2)[st] + m + 1)

        def unit_steps(st, evac, split, n_units=None):
            if st == "four1":
                ends = [0] * 16
            elif st == "four2":
                ends = [1] * 4 + [3] * 4
            elif st == "dn":
                ends = [3 * (m // 2) + 2 for m in range(KD)]
            else:
                ends = end_units(TILES[st])
            for u in range(max(ends) + 1):
                for n, end in enumerate(ends):
                    if end == u:
                        evac(n)
                split(u)

        @block.scalar
        def _(act):
            chain = {"n": 0, "base": 0}

            def link(ins):
                chain["n"] += 1
                ins.then_inc(achain, 1)
                act.wait_ge(achain, chain["base"] + chain["n"])

            def split_unit(c, st, u, extra=None):
                v = c.base[st]["U"] + u + 2
                if c.base is BASE2 and v >= TOTAL2["U"]:
                    return
                kind, n = releases(st)[u]
                act.wait_ge(tile_done if kind == "T" else part_done, c.at(kind, st, n))
                act.wait_ge(raw_ready[v % 2], c.raw(v))
                nc.scalar.activation(w_hi[v % 2][:, :], raw[v % 2][:, :], ACT.Copy).then_inc(hi_ready, 1)

            def stage_loop(c, st, evac):
                unit_steps(st, evac, lambda u: split_unit(c, st, u))

            def take_hi(c, st, n, a, dst, func=ACT.Copy, src=None, **kw):
                act.wait_ge(tile_done, c.at("T", st, n + 1))
                t = c.base[st]["T"] + n
                ps = bank[t % 4] if src is None else src(bank[t % 4])
                nc.scalar.activation(dst, ps[:, :] if src is None else ps, func, **kw).then_inc(act_took, 1)

            def square_slot(c, st, j):
                if j >= 2:
                    if "AD" in dict(STAGES1 + STAGES2)[st]:
                        act.wait_ge(sq_added, c.at("AD", st, max(j - 2, 1)))
                    else:
                        act.wait_ge(ss_done, c.at("SS", st, j - 1))
                return sq[:, j % 2, :]

            def squares_of_psum(c, st, n):
                take_hi(c, st, n, n, square_slot(c, st, n), ACT.Square)

            def squares(c, st, j, src, ready, width=S):
                act.wait_ge(ready[0], ready[1])
                nc.scalar.activation(square_slot(c, st, j)[:, 0:width], src, ACT.Square).then_inc(sq_ready, 1)

            def log_table():
                act.preload_act_table_set("natural_log_exp_and_others")

            def root(ss_stage, c, ss, width, features, slot=0, ps=None):
                act.wait_ge(ss_done, c.at("SS", ss_stage, ss))
                ps = SS_BANK if ps is None else ps
                r = rstd[:, slot, 0:width]
                link(nc.scalar.activation(r, ps[:, 0:width], ACT.Ln, bias=EPS, scale=1.0 / features))
                nc.scalar.activation(r, r, ACT.Exp, scale=-0.5).then_inc(rms_ready, 1)

            def split_hi(c, st, r, dst, src, ready):
                act.wait_ge(ready[0], ready[1])
                nc.scalar.activation(dst, src, ACT.Copy).then_inc(res_hi, 1)

            def norm(c, st, which, ready):
                _, src, hi, lo, width = NORMS[which][st]
                for m in range(KD):
                    squares(c, st, m, src[:, m, :], ready(m), width)
                root(st, c, KD, width, D)
                for m in range(KD):
                    r = c.base[st]["R"] + m
                    split_hi(c, st, m, hi[:, m, :], res[:, r % 4, 0:width], (res_ready, result_value(c, st, m)))

            def merge(c, which, st, b_gate=None):
                def evac(n):
                    m = n // 2
                    if n % 2 == 0:
                        act.wait_ge(tile_free, c.at("T", st, n - 2))
                        kw = {} if b_gate is None else {"bias": cc("b_gate", 8 * b_gate + m)}
                        take_hi(c, st, n, m, sg[:, m % 2, :], ACT.Sigmoid, **kw)
                    elif st == "cm":
                        r = c.base[st]["R"] + m
                        split_hi(c, st, m, MERGED[which][1][:, m, :], res[:, r % 4, :], (res_ready, result_value(c, st, m)))
                stage_loop(c, st, evac)

            def attention(c, st, sink=False):
                a = ATT[st]
                items = [(h, b) for h in range(a["heads"]) for b in range(ST)]
                for t in range(len(items) + 2):
                    if t < len(items):
                        h, b = items[t]
                        n = len(a["keys"](b)) * P
                        act.wait_ge(shift_ready, c.at("I", st, t + 1))
                        if not a["biased"] and t >= 3:
                            act.wait_ge(turned, c.at("I", st, t - 2))
                        if sink:
                            nc.scalar.activation(st_snk[:, t:t + 1], vv("sink", h), ACT.Exp, bias=st_neg[:, t:t + 1])
                        src = a["prob"][t % 3] if a["biased"] else bank[t % 3]
                        nc.scalar.activation(a["prob"][t % 3][:, 0:n], src[:, 0:n], ACT.Exp, bias=st_neg[:, t:t + 1],
                                             scale=a["scale"], accum_out=st_sum[:, t:t + 1]).then_inc(exp_done, 1)
                    if t >= 2:
                        i = t - 2
                        h, b = items[i]
                        n = len(a["keys"](b))
                        act.wait_ge(turned, c.at("I", st, i + 1))
                        if h >= 2 and b == 0:
                            act.wait_ge(head_done, c.at("H", st, h - 1))
                        nc.scalar.activation(a["pT"][h % 2][:, 0:n, b * P:(b + 1) * P],
                                             bank[3 + i % 2][:, 0:n * P].rearrange("p (t q) -> p t q", t=n),
                                             ACT.Copy).then_inc(turn_taken, 1)
                        if b == ST - 1 and h >= 1 and h % a["per_tile"] == 0:
                            output_hi(c, st, h // a["per_tile"] - 1)
                output_hi(c, st, a["heads"] // a["per_tile"] - 1)

            def output_hi(c, st, i):
                a = ATT[st]
                act.wait_ge(head_done, c.at("H", st, (i + 1) * a["per_tile"]))
                nc.scalar.activation(a["o"](i)[0], bank[5 + i % 2][:, :], ACT.Copy).then_inc(o_hi_ready, 1)

            def gate_up(c):
                st = "gu"
                t0, u0, r0 = c.base[st]["T"], c.base[st]["U"], c.base[st]["R"]
                with act.Fori(0, KF // 2) as i:
                    for p in range(2):
                        act.wait_ge(tile_free, c.at("T", st, 2 * p - 2) + i * 4)
                        act.wait_ge(tile_done, c.at("T", st, 2 * p + 1) + i * 4)
                        nc.scalar.activation(sg[:, p, :], bank[(t0 + 2 * p) % 4][:, :], ACT.Silu).then_inc(act_took, 1)
                        act.wait_ge(tile_free, c.at("T", st, 2 * p + 2) + i * 4)
                        nc.scalar.activation(a_hi[:, bass.ds(i * 2 + p, 1), :].rearrange("p a s -> p (a s)"), res[:, p, :], ACT.Copy).then_inc(res_hi, 1)
                        act.wait_ge(tile_done, c.at("T", st, 2 * p + 2) + i * 4)
                        v = (u0 + p) % 2
                        act.wait_ge(raw_ready[v], c.raw(u0 + p + 2) + i * 16)
                        nc.scalar.activation(w_hi[v][:, :], raw[v][:, :], ACT.Copy).then_inc(hi_ready, 1)

            def project(c, st):
                log_table()
                stage_loop(c, st, lambda n: squares_of_psum(c, st, n))

            act.dma_start(cst_sb[:, :], cst).then_inc(cst_loaded, 16)
            act.dma_start(pos_i[:, :], pos).then_inc(pos_loaded, 16)
            act.wait_ge(angle_ready, 1)
            nc.scalar.activation(cs[64:P, :], ang[2][64:P, :], ACT.Sin).then_inc(sin_ready, 1)
            for v in range(2):
                act.wait_ge(raw_ready[v], 16)
                nc.scalar.activation(w_hi[v][:, :], raw[v][:, :], ACT.Copy).then_inc(hi_ready, 1)

            def first_block(L):
                c = Counts(BASE1, L)
                chain["n"], chain["base"] = 0, L * CHAIN_PER_LAYER
                act.wait_ge(x_ready, L * TOTAL1["X"] + 8)
                act.dma_start(vec[:, :], vec1[bass.ds(L, 1)].rearrange("a p n -> (a p) n")).then_inc(vec_loaded, 16)
                act.dma_start(p_f[:, :, :], pT[bass.ds(L, 1)].rearrange("a (k p) s -> p (a k) s", p=P)).then_inc(p_loaded, 16)
                norm(c, "norm1", 1, lambda m: (x_ready, L * TOTAL1["X"] + (m + 1)))
                stage_loop(c, "four1", lambda n: take_hi(c, "four1", n, n, U_hi[:, n // ST, n % ST, :]))

                stage_loop(c, "four2", lambda n: take_hi(c, "four2", n, n, ob_hi[:, n, :]))
                merge(c, 1, "bm")

                def evac_z1(n):
                    if n < 4:
                        if n == 0:
                            log_table()
                        squares_of_psum(c, "z1", n)
                    elif n == 5:
                        root("z1", c, 3, S, Q_LORA)
                        root("z1", c, 4, S, KV_LORA, slot=1, ps=SS_BANK2)
                        act.wait_ge(tile_done, c.at("T", "z1", 6))
                        ps = bank[(c.base["z1"]["T"] + 5) % 4]
                        nc.scalar.activation(kdup[0:64, 0, :], ps[0:64, :], ACT.Copy)
                        nc.scalar.activation(kdup[64:P, 1, :], ps[64:P, :], ACT.Copy).then_inc(act_took, 1)
                    elif 6 <= n < 10:
                        j = n - 6
                        split_hi(c, "qn", j, cqn_hi[:, j, :], res[:, (c.base["qn"]["R"] + j) % 4, :], (res_ready, result_value(c, "qn", j)))
                    elif n >= 10:
                        t = 2 * (n - 10)
                        take_hi(c, "z1", n, n, vc[:, t, :], src=lambda ps: ps[:, 0:P])
                stage_loop(c, "z1", evac_z1)

                def evac_uq(n):
                    if n < 8:
                        take_hi(c, "uq", n, n, q_a[0:NOPE, n, :], src=lambda ps: ps[0:NOPE, :])
                    elif n < 12:
                        j = 2 * (n - 8)
                        take_hi(c, "uq", n, n, k_a[j // 4][0:NOPE, j % 4, :], src=lambda ps: ps[0:NOPE, :])
                    else:
                        take_hi(c, "uq", n, n, v_a[:, n - 12, 0:S // 2], src=lambda ps: ps[:, 0:S // 2])
                stage_loop(c, "uq", evac_uq)
                for b in range(ST):
                    ks = windowed(b)
                    if b == 0:
                        act.wait_ge(tile_done, c.at("T", "uq", 16))
                    act.activation(dist[:, b, 0:len(ks) * P], posf[:, ks.start * P:ks.stop * P], ACT.Abs, scale=-1.0,
                                   bias=posf[:, S + b:S + b + 1]).then_inc(dist_ready, 1)
                attention(c, "mla")
                attention(c, "gqa", sink=True)
                merge(c, 1, "am")
                merge(c, 1, "cm")
                project(c, "wout")
                root("wout", c, 2, S, D)
                norm(c, "norm2", 1, lambda m: (x_ready, c.at("X", "post1", m + 1) + 8))
                gate_up(c)
                act.wait_ge(p_loaded, L * 16 + 16)
                act.activation(p_hi[:, :, :], p_f[:, :, :], ACT.Copy).then_inc(p_hi_ready, 1)
                project(c, "dn")
                root("dn", c, 2, S, D)
                stage_loop(c, "pp", lambda n: take_hi(c, "pp", n, n, e[:, n, :]))
                for m in range(KD):
                    split_hi(c, "xple", m, h_hi[:, m, :], x[:, m, :], (x_ready, c.at("X", "post2", m + 1) + 8))

                def evac_ple(n):
                    act.wait_ge(tile_free, c.at("T", "ple", n - 1))
                    take_hi(c, "ple", n, n, sg[:, n % 2, :], ACT.Sigmoid)
                    squares(c, "ple", n, e[:, n, :], (tile_free, c.at("T", "ple", n + 1)))
                stage_loop(c, "ple", evac_ple)
                root("ple", c, 2, S, D)
                assert chain["n"] <= CHAIN_PER_LAYER
                act.sem_inc(achain, CHAIN_PER_LAYER - chain["n"])

            with act.Fori(0, DEPTH) as L:
                first_block(L)

            c = Counts(BASE2, DEPTH)
            chain["n"], chain["base"] = 0, DEPTH * CHAIN_PER_LAYER
            norm(c, "norm1", 2, lambda m: (x_ready, DEPTH * TOTAL1["X"] + (m + 1)))
            ap4 = cst_sb[:, CST["a_param"]:CST["a_param"] + 4]
            link(nc.scalar.activation(lruc[:, 0, 0:4], ap4, ACT.Abs))
            link(nc.scalar.activation(lruc[:, 1, 0:4], lruc[:, 0, 0:4], ACT.Exp, scale=-1.0))
            link(nc.scalar.activation(lruc[:, 2, 0:4], lruc[:, 1, 0:4], ACT.Ln, bias=1.0))
            nc.scalar.activation(lruc[:, 3, 0:4], ap4, ACT.Relu, scale=-1.0).then_inc(softplus_ready, 1)

            def evac_z2(n):
                if n < 4:
                    take_hi(c, "z2", n, n, lx[:, n, :])
                    return
                if n < 8:
                    return
                if n < 12:
                    take_hi(c, "z2", n, n, lg[:, n - 8, :], ACT.Gelu_apprx_tanh)
                elif n < 16:
                    if n == 12:
                        for j in range(4):
                            split_hi(c, "z2", j, ua_hi[:, j, :], ua[:, j, :], (res_ready, result_value(c, "z2", j)))
                        for j in range(4):
                            r = c.base["z2"]["R"] + 4 + j
                            split_hi(c, "z2", 4 + j, pool_hi[:, j, :], res[:, r % 4, :], (res_ready, result_value(c, "z2", 4 + j)))
                elif n < 20:
                    take_hi(c, "z2", n, n, qi[:, n - 16, :])
                elif n >= 22:
                    take_hi(c, "z2", n, n, vw[:, 2 * (n - 22), :], src=lambda ps: ps[:, 0:P])
            stage_loop(c, "z2", evac_z2)

            def evac_lru(n):
                if n < 4:
                    act.wait_ge(tile_done, c.at("T", "lru", 4))
                    take_hi(c, "lru", n, n, yb_hi[:, n, :], ACT.Identity, scale=cc("pool", n))
                elif n < 8:
                    take_hi(c, "lru", n, n, lr[:, n - 4, :], ACT.Sigmoid, bias=cc("b_a", n - 4))
                else:
                    act.wait_ge(tile_done, c.at("T", "lru", 12))
                    take_hi(c, "lru", n, n, li[:, n - 8, :], ACT.Sigmoid, bias=cc("b_x", n - 8))
            stage_loop(c, "lru", evac_lru)
            act.wait_ge(softplus_ready, 2)
            for j in range(4):
                nc.scalar.activation(lm[:, j, :], lr[:, j, :], ACT.Exp, scale=lruc[:, 1, 4 + j:5 + j]).then_inc(achain, 1)
            chain["n"] += 4
            act.wait_ge(achain, chain["base"] + chain["n"])
            for j in range(4):
                nc.scalar.activation(lr[:, j, :], lr[:, j, :], ACT.Exp, scale=lruc[:, 0, 4 + j:5 + j])
            for j in range(4):
                link(nc.scalar.activation(lm[:, j, :], lm[:, j, :], ACT.Relu, scale=-1.0, bias=1.0))
            for j in range(4):
                nc.scalar.activation(lm[:, j, :], lm[:, j, :], ACT.Sqrt).then_inc(lru_gates, 1)
            for j in range(4):
                split_hi(c, "lru", j, ya_hi[:, j, :], ua[:, j, :], (res_ready, result_value(c, "lru", j)))
            for t in range(32):
                b = t // 8
                act.wait_ge(idx_done, t + 1)
                if t >= 2:
                    act.wait_ge(idx_added, t - 1)
                nc.scalar.activation(sq[:, t % 2, 0:(b + 1) * P], bank[t % 3][:, 0:(b + 1) * P], ACT.Relu).then_inc(idx_relu, 1)
            merge(c, 2, "bm2", 1)
            merge(c, 2, "am", 0)
            attention(c, "dsa")
            merge(c, 2, "cm", 2)
            project(c, "wout")
            act.dma_start(memf[:, :, :], memT.rearrange("(k p) s -> p k s", p=P)).then_inc(mem_loaded, 16)
            root("wout", c, 2, S, D)
            norm(c, "normh", 2, lambda m: (x_ready, c.at("X", "post1", m + 1) + 8))
            norm(c, "normm", 2, lambda m: (mem_loaded, 16))
            stage_loop(c, "mq", lambda n: take_hi(c, "mq", n, n, mq[:, n, 0:S // 2], src=lambda ps: ps[:, 0:S // 2]))
            stage_loop(c, "mk", lambda n: take_hi(c, "mk", n, n, mk[:, n, 0:P], src=lambda ps: ps[:, 0:P]))
            stage_loop(c, "mv", lambda n: take_hi(c, "mv", n, n, mv[:, n, 0:S // 2], src=lambda ps: ps[:, 0:S // 2]))
            attention(c, "mem")
            project(c, "mo")
            root("mo", c, 2, S, D)
            norm(c, "norm2", 2, lambda m: (x_ready, c.at("X", "postm", m + 1) + 8))
            gate_up(c)
            project(c, "dn")
            root("dn", c, 2, S, D)
            for m in range(KD):
                act.wait_ge(x_ready, c.at("X", "post2", m + 1) + 8)
                act.dma_start(out[m * P:(m + 1) * P, :], x[:, m, :]).then_inc(out_done, 16)
            act.wait_ge(out_done, 16 * KD)

        @block.vector
        def _(dve):
            chain = {"n": 0, "base": 0}

            def link(ins):
                chain["n"] += 1
                ins.then_inc(vchain, 1)
                dve.wait_ge(vchain, chain["base"] + chain["n"])

            def split_unit(c, st, u):
                v = c.base[st]["U"] + u + 2
                if c.base is BASE2 and v >= TOTAL2["U"]:
                    return
                dve.wait_ge(hi_ready, c.at("U", st, u + 3))
                low_part(v % 2)

            def low_part(s):
                nc.vector.tensor_tensor(w_lo[s][:, :], raw[s][:, :], w_hi[s][:, :].bitcast(F32), ALU.subtract).then_inc(lo_ready, 1)

            def stage_loop(c, st, evac):
                unit_steps(st, evac, lambda u: split_unit(c, st, u))

            def ps_of(c, st, n):
                return bank[(c.base[st]["T"] + n) % 4]

            def take_lo(c, st, n, a, dst, hi):
                dve.wait_ge(act_took, c.at("A", st, a + 1))
                nc.vector.tensor_tensor(dst, ps_of(c, st, n)[:, :], hi.bitcast(F32), ALU.subtract).then_inc(tile_free, 1)

            def copy_out(c, st, n, a, dst, src, wait_act=True):
                if wait_act:
                    dve.wait_ge(act_took, c.at("A", st, a + 1))
                else:
                    dve.wait_ge(tile_done, c.at("T", st, n + 1))
                nc.vector.tensor_copy(dst, src(ps_of(c, st, n))).then_inc(tile_free, 1)

            def pass_on(c, st, n):
                dve.wait_ge(tile_free, c.at("T", st, n))
                dve.sem_inc(tile_free, 1)


            def result_slot(c, st, m):
                r = c.base[st]["R"] + m
                if r >= 4 or c.base is BASE2:
                    dve.wait_ge(res_split, c.at("R", st, m - 3))
                return res[:, r % 4, :]

            def norm(c, st, which):
                gain, src, _, _, width = NORMS[which][st]
                g = vv if which == 1 else cc
                dve.wait_ge(rms_ready, c.at("N", st, 1))
                for m in range(KD):
                    dst = result_slot(c, st, m)
                    nc.vector.scalar_tensor_tensor(out=dst[:, 0:width], in0=src[:, m, :], scalar=g(gain, m),
                                                   in1=rstd[:, 0, 0:width], op0=ALU.mult, op1=ALU.mult).then_inc(res_ready, 1)

            def post(c, st, which, gain, src, also=None):
                g = vv if which == 1 else cc
                dve.wait_ge(rms_ready, c.at("N", st, 1))
                first = chain["n"]
                for m in range(KD + 1):
                    if m < KD:
                        if m >= 2:
                            dve.wait_ge(x_ready, c.at("X", st, m - 1) + 8)
                        nc.vector.scalar_tensor_tensor(out=sg[:, m % 2, :], in0=src[:, m, :], scalar=g(gain, m),
                                                       in1=rstd[:, 0, :], op0=ALU.mult, op1=ALU.mult).then_inc(vchain, 1)
                        chain["n"] += 1
                    if m >= 1:
                        dve.wait_ge(vchain, chain["base"] + first + m)
                        nc.vector.tensor_tensor(x[:, m - 1, :], x[:, m - 1, :], sg[:, (m - 1) % 2, :], ALU.add).then_inc(x_ready, 1)
                    if also is not None:
                        also(m)

            def merge(c, which, st, order, extra=None):
                merged = MERGED[which][0]

                def evac(n):
                    if n % 2 == 0:
                        return
                    m = n // 2
                    dve.wait_ge(act_took, c.at("A", st, m + 1))
                    dve.wait_ge(tile_done, c.at("T", st, n + 1))
                    ps = ps_of(c, st, n)
                    if order == 0:
                        nc.vector.tensor_tensor(merged[:, m, :], ps[:, :], sg[:, m % 2, :], ALU.mult).then_inc(tile_free, 2)
                    else:
                        r = rstd[:, m % 2, :]
                        nc.vector.tensor_tensor(r, ps[:, :], sg[:, m % 2, :], ALU.mult).then_inc(tile_free, 2)
                        dve.wait_ge(tile_free, c.at("T", st, n + 1))
                        if order == 1:
                            link(nc.vector.tensor_tensor(merged[:, m, :], merged[:, m, :], r, ALU.add))
                        else:
                            dst = result_slot(c, st, m)
                            nc.vector.tensor_tensor(dst, merged[:, m, :], r, ALU.add).then_inc(res_ready, 1)
                    if extra is not None:
                        extra(m)
                stage_loop(c, st, evac)

            def attention(c, st, bias=None, sink=False):
                a = ATT[st]
                items = [(h, b) for h in range(a["heads"]) for b in range(ST)]
                taken = 0
                for t in range(len(items) + 1):
                    if t < len(items):
                        h, b = items[t]
                        n = len(a["keys"](b)) * P
                        dve.wait_ge(logits_done, c.at("I", st, t + 1))
                        src = bank[t % 3]
                        if a["biased"]:
                            if t >= 3:
                                dve.wait_ge(turned, c.at("I", st, t - 2))
                            src = a["prob"][t % 3]
                            tile, factor = bias(h, b)
                            link(nc.vector.scalar_tensor_tensor(out=src[:, 0:n], in0=tile, scalar=factor, in1=bank[t % 3][:, 0:n],
                                                                op0=ALU.mult, op1=ALU.add))
                        link(nc.vector.reduce_max(st_max[:, t:t + 1], src[:, 0:n], AX_X))
                        if sink:
                            link(nc.vector.tensor_scalar(st_neg[:, t:t + 1], st_max[:, t:t + 1], a["scale"], vv("sink", h), ALU.mult, ALU.max))
                            nc.vector.tensor_scalar(st_neg[:, t:t + 1], st_neg[:, t:t + 1], -1.0, None, ALU.mult).then_inc(shift_ready, 1)
                        else:
                            nc.vector.tensor_scalar(st_neg[:, t:t + 1], st_max[:, t:t + 1], -a["scale"], None, ALU.mult).then_inc(shift_ready, 1)
                    if t >= 1:
                        i = t - 1
                        h, b = items[i]
                        n = len(a["keys"](b)) * P
                        dve.wait_ge(exp_done, c.at("I", st, i + 1))
                        if sink:
                            link(nc.vector.tensor_tensor(st_sum[:, i:i + 1], st_sum[:, i:i + 1], st_snk[:, i:i + 1], ALU.add))
                        link(nc.vector.reciprocal(st_rec[:, i:i + 1], st_sum[:, i:i + 1]))
                        p = a["prob"][i % 3]
                        nc.vector.tensor_scalar(p[:, 0:n], p[:, 0:n], st_rec[:, i:i + 1], None, ALU.mult).then_inc(prob_ready, 1)
                        if b == 1 and h >= 2 and (h + 1) % a["per_tile"] == 0 and (h + 1) // a["per_tile"] >= 2:
                            done = (h - 1) // a["per_tile"]
                            while taken < done:
                                output_lo(c, st, taken)
                                taken += 1
                while taken < a["heads"] // a["per_tile"]:
                    output_lo(c, st, taken)
                    taken += 1

            def output_lo(c, st, i):
                hi, lo = ATT[st]["o"](i)
                dve.wait_ge(o_hi_ready, c.at("O", st, i + 1))
                nc.vector.tensor_tensor(lo, bank[5 + i % 2][:, :], hi.bitcast(F32), ALU.subtract).then_inc(o_split, 1)

            def gate_up(c):
                st = "gu"
                t0, u0 = c.base[st]["T"], c.base[st]["U"]
                with dve.Fori(0, KF // 2) as i:
                    for p in range(2):
                        dve.wait_ge(act_took, c.at("A", st, p + 1) + i * 2)
                        dve.wait_ge(tile_done, c.at("T", st, 2 * p + 2) + i * 4)
                        dve.wait_ge(res_split, c.at("R", st, p - 1) + i * 2)
                        nc.vector.tensor_tensor(res[:, p, :], bank[(t0 + 2 * p + 1) % 4][:, :], sg[:, p, :], ALU.mult).then_inc(tile_free, 2)
                        dve.wait_ge(hi_ready, c.at("U", st, p + 3) + i * 2)
                        low_part((u0 + p) % 2)

            def project(c, st):
                stage_loop(c, st, lambda n: copy_out(c, st, n, n, y[:, n, :], lambda ps: ps[:, :]))

            def rotate(ps, dst, last):
                link(nc.vector.tensor_tensor(rope_t[0][64:96, :], ps[64:96, :], cs[64:96, :], ALU.mult))
                link(nc.vector.tensor_tensor(rope_t[1][64:96, :], ps[96:P, :], cs[96:P, :], ALU.mult))
                link(nc.vector.tensor_tensor(dst, rope_t[0][64:96, :], rope_t[1][64:96, :], ALU.add))

            dve.wait_ge(cst_loaded, 16)
            dve.wait_ge(pos_loaded, 16)
            link(nc.vector.tensor_copy(posf[:, :], pos_i[:, :]))
            r = slice(64, P)
            link(nc.vector.tensor_scalar(ang[0][r, :], posf[r, 0:S], cc("freq", 0, 64), None, ALU.mult))
            link(nc.vector.tensor_scalar(ang[1][r, :], ang[0][r, :], cc("phase", 0, 64), float(1 / (2 * np.pi)), ALU.add, ALU.mult))
            link(nc.vector.tensor_scalar(ang[1][r, :], ang[1][r, :], ROUND, None, ALU.add))
            link(nc.vector.tensor_scalar(ang[1][r, :], ang[1][r, :], -ROUND, None, ALU.add))
            link(nc.vector.scalar_tensor_tensor(out=ang[0][r, :], in0=ang[1][r, :], scalar=-TWO_PI_A, in1=ang[0][r, :], op0=ALU.mult, op1=ALU.add))
            link(nc.vector.scalar_tensor_tensor(out=ang[0][r, :], in0=ang[1][r, :], scalar=-TWO_PI_B, in1=ang[0][r, :], op0=ALU.mult, op1=ALU.add))
            link(nc.vector.scalar_tensor_tensor(out=ang[0][r, :], in0=ang[1][r, :], scalar=-float(TWO_PI_C), in1=ang[0][r, :], op0=ALU.mult, op1=ALU.add))
            link(nc.vector.tensor_scalar(ang[2][r, :], ang[0][r, :], cc("phase", 0, 64), 3.1415925, ALU.add, ALU.min))
            nc.vector.tensor_scalar(ang[2][r, :], ang[2][r, :], -3.1415925, None, ALU.max).then_inc(angle_ready, 1)
            dve.wait_ge(sin_ready, 1)
            link(nc.vector.tensor_scalar(cs[r, :], cs[r, :], cc("sign", 0, 64), None, ALU.mult))
            for v in range(2):
                dve.wait_ge(hi_ready, v + 1)
                low_part(v)
            start_steps = chain["n"]
            dve.wait_ge(x_loaded, 16)
            dve.sem_inc(x_ready, 8)

            def first_block(L):
                c = Counts(BASE1, L)
                chain["n"], chain["base"] = 0, L * CHAIN_PER_LAYER + start_steps
                dve.wait_ge(vec_loaded, L * 16 + 16)
                norm(c, "norm1", 1)
                stage_loop(c, "four1", lambda n: take_lo(c, "four1", n, n, U_lo[:, n // ST, n % ST, :], U_hi[:, n // ST, n % ST, :]))
                stage_loop(c, "four2", lambda n: take_lo(c, "four2", n, n, (ob_lo0 if n < 4 else ob_lo1)[:, n % 4, :], ob_hi[:, n, :]))
                merge(c, 1, "bm", 0)

                def evac_z1(n):
                    if n < 4:
                        copy_out(c, "z1", n, n, cq[:, n, :], lambda ps: ps[:, :])
                    elif n == 4:
                        dve.wait_ge(tile_done, c.at("T", "z1", 5))
                        rotate(ps_of(c, "z1", 4), kr[64:96, :], None)
                        pass_on(c, "z1", 4)
                        for hd in range(MLA_HEADS):
                            ins = nc.vector.tensor_copy(k_a[hd // 4][64:96, hd % 4, :], kr[64:96, :])
                        ins.then_inc(kr_copied, 1)
                    elif n == 5:
                        dve.wait_ge(act_took, c.at("A", "z1", 5))
                        ps = ps_of(c, "z1", 5)
                        nc.vector.tensor_copy(kdup[64:P, 0, :], ps[0:64, :])
                        nc.vector.tensor_copy(kdup[0:64, 1, :], ps[64:P, :]).then_inc(tile_free, 1)
                    elif n < 10:
                        copy_out(c, "z1", n, n, qc[:, n - 6, :], lambda ps: ps[:, :], wait_act=False)
                        j = n - 6
                        if j in (0, 3):
                            dve.wait_ge(rms_ready, c.at("N", "qn", 1 + j // 3))
                        dst = result_slot(c, "qn", j)
                        nc.vector.scalar_tensor_tensor(out=dst, in0=cq[:, j, :], scalar=vv("q_norm", j) if j < 3 else vv("kv_norm"),
                                                       in1=rstd[:, j // 3, :], op0=ALU.mult, op1=ALU.mult).then_inc(res_ready, 1)
                    else:
                        t = 2 * (n - 10) + 1
                        copy_out(c, "z1", n, n - 5, vc[:, t, :], lambda ps: ps[:, P:2 * P])
                stage_loop(c, "z1", evac_z1)

                def evac_uq(n):
                    if n < 8:
                        dve.wait_ge(act_took, c.at("A", "uq", n + 1))
                        rotate(ps_of(c, "uq", n), q_a[64:96, n, :], None)
                        pass_on(c, "uq", n)
                    elif n < 12:
                        j = 2 * (n - 8) + 1
                        copy_out(c, "uq", n, n, k_a[j // 4][0:NOPE, j % 4, :], lambda ps: ps[64:P, :])
                    else:
                        copy_out(c, "uq", n, n, v_a[:, n - 12, S // 2:S], lambda ps: ps[:, S // 2:S])
                stage_loop(c, "uq", evac_uq)
                for b in range(ST):
                    n = len(windowed(b)) * P
                    off = P if b == 0 else 0
                    dve.wait_ge(dist_ready, L * ST + (b + 1))
                    link(nc.vector.tensor_tensor(dist[:, b, 0:n], dist[:, b, 0:n], cst_sb[:, CST["window"] + off:CST["window"] + off + n], ALU.add))
                attention(c, "mla")

                def alibi(h, b):
                    return dist[:, b, 0:len(windowed(b)) * P], -(2.0 ** (-8.0 * (h + 1) / HEADS)) * HD ** 0.5
                attention(c, "gqa", alibi, sink=True)
                merge(c, 1, "am", 1)
                merge(c, 1, "cm", 2)
                project(c, "wout")
                post(c, "post1", 1, "mix_post", y)
                norm(c, "norm2", 1)
                gate_up(c)
                project(c, "dn")
                def free_pp(m):
                    if m in (4, 8):
                        for n in range(m - 4, m):
                            dve.wait_ge(act_took, c.at("A", "pp", n + 1))
                            pass_on(c, "pp", n)
                        if m == 8:
                            split_unit(c, "pp", 0)
                post(c, "post2", 1, "ffn_post", y, free_pp)

                def evac_ple(n):
                    dve.wait_ge(act_took, c.at("A", "ple", n + 1))
                    dve.wait_ge(tile_free, c.at("T", "ple", n))
                    nc.vector.tensor_tensor(e[:, n, :], e[:, n, :], sg[:, n % 2, :], ALU.mult).then_inc(tile_free, 1)
                stage_loop(c, "ple", evac_ple)
                post(c, "post3", 1, "ple", e)
                assert chain["n"] <= CHAIN_PER_LAYER
                dve.sem_inc(vchain, CHAIN_PER_LAYER - chain["n"])

            with dve.Fori(0, DEPTH) as L:
                first_block(L)

            c = Counts(BASE2, DEPTH)
            chain["n"], chain["base"] = 0, DEPTH * CHAIN_PER_LAYER + start_steps
            norm(c, "norm1", 2)
            dve.wait_ge(softplus_ready, 1)
            link(nc.vector.tensor_tensor(lruc[:, 2, 4:8], lruc[:, 2, 0:4], lruc[:, 3, 0:4], ALU.add))
            link(nc.vector.tensor_scalar(lruc[:, 0, 4:8], lruc[:, 2, 4:8], -8.0, None, ALU.mult))
            nc.vector.tensor_scalar(lruc[:, 1, 4:8], lruc[:, 2, 4:8], -16.0, None, ALU.mult).then_inc(softplus_ready, 1)

            def conv(j):
                link(nc.vector.tensor_scalar(ua[:, j, :], lx[:, j, :], cc("conv_w", 12 + j), cc("conv_b", j), ALU.mult, ALU.add))
                for back in range(1, 4):
                    ins = nc.vector.scalar_tensor_tensor(out=ua[:, j, back:S], in0=lx[:, j, 0:S - back], scalar=cc("conv_w", 4 * (3 - back) + j),
                                                         in1=ua[:, j, back:S], op0=ALU.mult, op1=ALU.add)
                    if back < 3:
                        link(ins)
                    else:
                        ins.then_inc(res_ready, 1)

            def pool(g):
                src, lo = pz[:, g, :], 1
                for lev in range(g + 1):
                    back = 1 << lev
                    dst = win[lev % 2]
                    link(nc.vector.tensor_tensor(dst[:, lo:PADW + S], src[:, lo:PADW + S], src[:, lo - back:PADW + S - back], ALU.add))
                    src = dst[:, :]
                    lo += 2 * back
                link(nc.vector.tensor_tensor(src[:, PADW:PADW + 16], src[:, PADW:PADW + 16],
                                             cst_sb[:, CST["head"] + 16 * g:CST["head"] + 16 * g + 16], ALU.mult))
                dst = result_slot(c, "z2", 4 + g)
                nc.vector.scalar_tensor_tensor(out=dst, in0=src[:, PADW:PADW + S], scalar=1.0 / POOL_W[g], in1=pz[:, g, PADW:PADW + S],
                                               op0=ALU.mult, op1=ALU.subtract).then_inc(res_ready, 1)
                dve.wait_ge(res_ready, result_value(c, "z2", 4 + g))

            A_Z2 = {0: 0, 1: 1, 2: 2, 3: 3, 8: 4, 9: 5, 10: 6, 11: 7, 16: 8, 17: 9, 18: 10, 19: 11, 22: 12, 23: 13}

            def evac_z2(n):
                if n < 4:
                    dve.wait_ge(act_took, c.at("A", "z2", A_Z2[n] + 1))
                    pass_on(c, "z2", n)
                elif n < 8:
                    if n == 4:
                        dve.wait_ge(pad_ready, 1)
                    copy_out(c, "z2", n, 0, pz[:, n - 4, PADW:PADW + S], lambda ps: ps[:, :], wait_act=False)
                elif n < 12:
                    dve.wait_ge(act_took, c.at("A", "z2", A_Z2[n] + 1))
                    pass_on(c, "z2", n)
                    conv(n - 8)
                    if n == 11:
                        dve.wait_ge(tile_free, c.at("T", "z2", 8))
                        for g in range(4):
                            pool(g)
                elif n < 16:
                    copy_out(c, "z2", n, 0, qd[:, n - 12, :], lambda ps: ps[:, :], wait_act=False)
                elif n < 20:
                    dve.wait_ge(act_took, c.at("A", "z2", A_Z2[n] + 1))
                    pass_on(c, "z2", n)
                elif n < 22:
                    copy_out(c, "z2", n, 0, (kk, ki)[n - 20][:, :], lambda ps: ps[:, :], wait_act=False)
                else:
                    copy_out(c, "z2", n, A_Z2[n], vw[:, 2 * (n - 22) + 1, :], lambda ps: ps[:, P:2 * P])
            stage_loop(c, "z2", evac_z2)
            dve.wait_ge(tile_free, c.at("T", "z2", 24))
            dve.wait_ge(act_took, c.at("A", "z2", 14))
            link(nc.vector.tensor_scalar(wsc[:, :, :], vw[:, :, HD:HD + 8], 8 ** -0.5, None, ALU.mult))

            def evac_lru(n):
                dve.wait_ge(act_took, c.at("A", "lru", n + 1))
                if n < 4:
                    nc.vector.scalar_tensor_tensor(out=yb_lo[:, n, :], in0=ps_of(c, "lru", n)[:, :], scalar=cc("pool", n),
                                                   in1=yb_hi[:, n, :].bitcast(F32), op0=ALU.mult, op1=ALU.subtract).then_inc(tile_free, 1)
                else:
                    pass_on(c, "lru", n)
            stage_loop(c, "lru", evac_lru)
            for j in range(4):
                link(nc.vector.tensor_tensor(li[:, j, :], li[:, j, :], ua[:, j, :], ALU.mult))
            for j in range(4):
                dve.wait_ge(lru_gates, j + 1)
                link(nc.vector.tensor_tensor(li[:, j, :], li[:, j, :], lm[:, j, :], ALU.mult))
                link(nc.vector.tensor_tensor_scan(ua[:, j, :], lr[:, j, :], li[:, j, :], 0.0, ALU.mult, ALU.add))
                nc.vector.tensor_tensor(ua[:, j, :], ua[:, j, :], lg[:, j, :], ALU.mult).then_inc(res_ready, 1)
            for t in range(32):
                b, hh = t // 8, t % 8
                n = (b + 1) * P
                dve.wait_ge(idx_relu, t + 1)
                if hh == 0:
                    ins = nc.vector.tensor_scalar(score[:, b, 0:n], sq[:, t % 2, 0:n], wsc[:, b, hh:hh + 1], None, ALU.mult)
                else:
                    dve.wait_ge(idx_added, t)
                    ins = nc.vector.scalar_tensor_tensor(out=score[:, b, 0:n], in0=sq[:, t % 2, 0:n], scalar=wsc[:, b, hh:hh + 1],
                                                         in1=score[:, b, 0:n], op0=ALU.mult, op1=ALU.add)
                ins.then_inc(idx_added, 1)
            dve.wait_ge(idx_added, 32)
            for b in range(ST):
                if b == 0:
                    link(nc.vector.memset(score[:, 0, 0:P], 0.0))
                    link(nc.vector.memset(score[0:64, 0, 64:P], MASKED))
                else:
                    link(nc.vector.memset(score[0:64, b, b * P + 64:(b + 1) * P], NEG))

            def take_top8(b):
                n = (b + 1) * P
                link(nc.vector.max(top8[:, :], score[:, b, 0:n]))
                link(nc.vector.match_replace(out=score[:, b, 0:n], in_to_replace=top8[:, :], in_values=score[:, b, 0:n], imm_value=TAKEN))

            rounds = [b for b in range(1, ST) for _ in range(TOPK // 8)]

            def some_rounds(m):
                for b in rounds[3 * m:3 * m + 3]:
                    take_top8(b)
            merge(c, 2, "bm2", 0, extra=lambda m: some_rounds(m))
            merge(c, 2, "am", 1, extra=lambda m: some_rounds(KD + m))
            for b in range(1, ST):
                n = (b + 1) * P
                link(nc.vector.tensor_scalar(score[:, b, 0:n], score[:, b, 0:n], 0.5 * (NEG + TAKEN), MASKED, ALU.is_gt, ALU.mult))
            attention(c, "dsa", lambda h, b: (score[:, b, 0:(b + 1) * P], 1.0))
            merge(c, 2, "cm", 2)
            project(c, "wout")
            post(c, "post1", 2, "mix_post", y)
            norm(c, "normh", 2)
            dve.wait_ge(mem_loaded, 16)
            norm(c, "normm", 2)
            stage_loop(c, "mq", lambda n: copy_out(c, "mq", n, n, mq[:, n, S // 2:S], lambda ps: ps[:, S // 2:S]))
            stage_loop(c, "mk", lambda n: copy_out(c, "mk", n, n, mk[:, n, P:N_MEM], lambda ps: ps[:, P:N_MEM]))
            stage_loop(c, "mv", lambda n: copy_out(c, "mv", n, n, mv[:, n, S // 2:S], lambda ps: ps[:, S // 2:S]))
            attention(c, "mem")
            project(c, "mo")
            post(c, "postm", 2, "mem_post", y)
            norm(c, "norm2", 2)
            gate_up(c)
            project(c, "dn")
            post(c, "post2", 2, "ffn_post", y)

        @block.gpsimd
        def _(pool):
            def split_lo(c, st, m, dst, src, hi):
                pool.wait_ge(res_hi, c.at("R", st, m + 1))
                nc.gpsimd.tensor_tensor(dst, src, hi.bitcast(F32), ALU.subtract).then_inc(res_split, 1)

            def norm(c, st, which):
                _, _, hi, lo, width = NORMS[which][st]
                for m in range(KD):
                    r = c.base[st]["R"] + m
                    split_lo(c, st, m, lo[:, m, :], res[:, r % 4, 0:width], hi[:, m, :])

            def merged_lo(c, which):
                _, hi, lo = MERGED[which]
                for m in range(KD):
                    r = c.base["cm"]["R"] + m
                    split_lo(c, "cm", m, lo[:, m, :], res[:, r % 4, :], hi[:, m, :])

            def gate_up(c):
                with pool.Fori(0, KF // 2) as i:
                    for p in range(2):
                        pool.wait_ge(res_hi, c.at("R", "gu", p + 1) + i * 2)
                        nc.gpsimd.tensor_tensor(a_lo[:, bass.ds(i * 2 + p, 1), :].rearrange("p a s -> p (a s)"), res[:, p, :],
                                                a_hi[:, bass.ds(i * 2 + p, 1), :].rearrange("p a s -> p (a s)").bitcast(F32),
                                                ALU.subtract).then_inc(res_split, 1)

            def add_squares(c, st, ready, kind):
                for j in range(1, KD - 1):
                    pool.wait_ge(ready, c.at(kind, st, j + 1))
                    if j >= 2:
                        pool.wait_ge(sq_added, c.at("AD", st, j - 1))
                    nc.gpsimd.tensor_tensor(sq_acc, sq[:, 0, :] if j == 1 else sq_acc, sq[:, j % 2, :], ALU.add).then_inc(sq_added, 1)

            with pool.Fori(0, DEPTH) as L:
                c = Counts(BASE1, L)
                norm(c, "norm1", 1)
                for j in range(4):
                    r = c.base["qn"]["R"] + j
                    split_lo(c, "qn", j, cqn_lo[:, j, :], res[:, r % 4, :], cqn_hi[:, j, :])
                merged_lo(c, 1)
                add_squares(c, "wout", act_took, "A")
                norm(c, "norm2", 1)
                gate_up(c)
                pool.wait_ge(p_hi_ready, L + 1)
                nc.gpsimd.tensor_tensor(p_lo[:, :, :], p_f[:, :, :], p_hi[:, :, :].bitcast(F32), ALU.subtract).then_inc(p_split, 1)
                add_squares(c, "dn", act_took, "A")
                for m in range(KD):
                    if m == 4:
                        pool.wait_ge(tile_done, c.at("T", "pp", 8))
                    split_lo(c, "xple", m, h_lo[:, m, :], x[:, m, :], h_hi[:, m, :])
                add_squares(c, "ple", sq_ready, "SQ")

            c = Counts(BASE2, DEPTH)
            norm(c, "norm1", 2)
            nc.gpsimd.memset(pz[:, :, 0:PADW], 0.0).then_inc(pad_ready, 1)
            for j in range(4):
                split_lo(c, "z2", j, ua_lo[:, j, :], ua[:, j, :], ua_hi[:, j, :])
            for j in range(4):
                r = c.base["z2"]["R"] + 4 + j
                split_lo(c, "z2", 4 + j, pool_lo[:, j, :], res[:, r % 4, :], pool_hi[:, j, :])
            for j in range(4):
                split_lo(c, "lru", j, ya_lo[:, j, :], ua[:, j, :], ya_hi[:, j, :])
            merged_lo(c, 2)
            add_squares(c, "wout", act_took, "A")
            norm(c, "normh", 2)
            norm(c, "normm", 2)
            add_squares(c, "mo", act_took, "A")
            norm(c, "norm2", 2)
            gate_up(c)
            add_squares(c, "dn", act_took, "A")


def lay_out(inputs):
    f32 = np.float32
    stream = np.zeros((UNITS_PADDED, P, UC), f32)
    at = [0]

    def put(blocks):
        for i, b in enumerate(blocks):
            if b is not None:
                j = i % BLK
                stream[at[0] + i // BLK, :, j * P:(j + 1) * P] = b
        at[0] += -(-len(blocks) // BLK)

    def cut(w, k, lo, n=P):
        return w[k * P:(k + 1) * P, lo:lo + n]

    def column(w, lo, k=KD):
        return [cut(w, j, lo) for j in range(k)]

    def merge(w_in, gate, w, k):
        out = []
        for m in range(KD):
            out += column(w_in, gate + m * P) + column(w, m * P, k)
        return out

    def ffn(gate, up, down):
        out = []
        for m in range(KF):
            out += column(gate, m * P) + column(up, m * P)
        put(out)
        out = []
        for pair in range(KD // 2):
            for part in range(3):
                for q in range(2):
                    for k in range(8 * part, 8 * part + 8):
                        out.append(cut(down, k, (2 * pair + q) * P) if k < KF else None)
        put(out)

    def by_column(w):
        out = []
        for m in range(KD):
            out += column(w, m * P, w.shape[0] // P)
        return out

    ch = np.arange(GW)
    ang = 2 * np.pi * ((ch[:, None] * ch[None, :]) % GW) / GW
    chan = np.concatenate([np.cos(ang), np.sin(ang)], axis=1).astype(f32)
    tk = np.arange(S)
    ang = 2 * np.pi * ((tk[:, None] * tk[None, :]) % S) / S
    norm = 1 / np.sqrt(S * GW)
    tok_cos, tok_sin = (np.cos(ang) * norm).astype(f32), (-np.sin(ang) * norm).astype(f32)

    def wide(w, rows):
        return [cut(w, t, n * P) for t in rows for n in range(w.shape[1] // P)]

    for i in range(DEPTH):
        w_in = inputs["w_in"][i]
        put(wide(chan, range(2)))
        for half in range(2):
            put(wide(tok_cos, range(ST)))
            put(wide(tok_sin, range(ST)))
        at_gate = Q_LORA + KV_LORA + ROPE + HEADS * HD + 2 * KV_HEADS * HD
        at_rope = Q_LORA + KV_LORA
        at_qc = at_rope + ROPE
        at_kc = at_qc + HEADS * HD
        at_vc = at_kc + KV_HEADS * HD
        put(merge(w_in, at_gate + D, inputs["w_branch_b"][i], KD))
        rope = np.zeros((D, P), f32)
        rope[:, 0:64] = w_in[:, at_rope - 64:at_rope]
        rope[:, 64:96] = w_in[:, at_rope:at_rope + 32]
        rope[:, 96:112] = w_in[:, at_rope + 16:at_rope + 32]
        rope[:, 112:128] = w_in[:, at_rope:at_rope + 16]
        blocks = []
        for m in range(4):
            blocks += column(w_in, m * P)
        blocks += column(rope, 0) + column(w_in, at_kc)
        for m in range(4):
            blocks += column(w_in, at_qc + m * P)
        put(blocks + column(w_in, at_vc))
        w_uq, w_ukv = inputs["w_uq"][i], inputs["w_ukv"][i]
        heads = np.zeros((Q_LORA, MLA_HEADS * P), f32)
        for hd in range(MLA_HEADS):
            src, dst = hd * MLA_QK, hd * P
            heads[:, dst:dst + 96] = w_uq[:, src:src + 96]
            heads[:, dst + 96:dst + 112] = w_uq[:, src + 80:src + 96]
            heads[:, dst + 112:dst + 128] = w_uq[:, src + 64:src + 80]
        kv = w_ukv.reshape(KV_LORA, MLA_HEADS, NOPE + MLA_V)
        k_cols = kv[:, :, 0:NOPE].reshape(KV_LORA, -1)
        v_cols = kv[:, :, NOPE:].reshape(KV_LORA, -1)
        blocks = []
        for hd in range(MLA_HEADS):
            blocks += column(heads, hd * P, 3)
        put(blocks + wide(k_cols, range(1)) + wide(v_cols, range(1)))
        put(merge(w_in, at_gate, inputs["w_branch_a"][i], 4))
        put(merge(w_in, at_gate + 2 * D, inputs["w_branch_c"][i], 4))
        put(by_column(inputs["w_out"][i]))
        ffn(inputs["w_ffn_gate"][i], inputs["w_ffn_up"][i], inputs["w_ffn_down"][i])
        put(by_column(inputs["w_ple_proj"][i]))
        put(by_column(inputs["w_ple_gate"][i]))
        assert at[0] == (i + 1) * TOTAL1["U"]

    w_in = inputs["w_in_2"][0]
    sizes = dict(lru_x=512, lru_gate=512, pool=512, q=512, k=64, v=64, q_idx=512, k_idx=64, w_idx=8, gates=3 * D)
    off, n = {}, 0
    for name, width in sizes.items():
        off[name] = n
        n += width
    twice = np.zeros((D, 3 * P), f32)
    for j in range(2):
        twice[:, 64 * j:64 * j + 64] = w_in[:, off["k"]:off["k"] + 64]
        twice[:, P + 64 * j:P + 64 * j + 64] = w_in[:, off["k_idx"]:off["k_idx"] + 64]
    twice[:, 2 * P:2 * P + 64] = w_in[:, off["v"]:off["v"] + 64]
    twice[:, 2 * P + 64:2 * P + 72] = w_in[:, off["w_idx"]:off["w_idx"] + 8]
    blocks = []
    for name in ("lru_x", "pool", "lru_gate", "q", "q_idx"):
        for m in range(4):
            blocks += column(w_in, off[name] + m * P)
    for j in range(3):
        blocks += column(twice, j * P)
    put(blocks)
    blocks = [inputs["w_pool_2"][0, g] for g in range(4)]
    for name in ("lru_w_a_2", "lru_w_x_2"):
        for m in range(4):
            two = np.zeros((P, P), f32)
            two[0:64, 0:64] = inputs[name][0, 2 * m]
            two[64:, 64:] = inputs[name][0, 2 * m + 1]
            blocks.append(two)
    put(blocks)
    for br in (1, 0, 2):
        put(merge(w_in, off["gates"] + br * D, inputs["w_branch_2"][0, br], 4))
    put(by_column(inputs["w_out_2"][0]))
    blocks = []
    for m in range(4):
        blocks += column(inputs["w_mem_q_2"][0], m * P)
    put(blocks)
    w_kv = inputs["w_mem_kv_2"][0]
    blocks = []
    for m in range(4):
        blocks += column(w_kv, m * P)
    put(blocks)
    put(wide(w_kv[:, 512:], range(KD)))
    put(by_column(inputs["w_mem_o_2"][0]))
    w_f = inputs["w_ffn_in_2"][0]
    ffn(w_f[:, 0:FFN], w_f[:, FFN:], inputs["w_ffn_out_2"][0])
    assert at[0] == UNITS

    vec1 = np.zeros((DEPTH, P, NV1), f32)
    for i in range(DEPTH):
        for name, key in (("mix_pre", "norm_mix_pre"), ("q_norm", "mla_q_norm"), ("kv_norm", "mla_kv_norm"), ("mix_post", "norm_mix_post"),
                          ("ffn_pre", "norm_ffn_pre"), ("ffn_post", "norm_ffn_post"), ("ple", "norm_ple")):
            v = inputs[key][i].reshape(-1, P).T
            vec1[i, :, VEC1[name]:VEC1[name] + v.shape[1]] = v
        vec1[i, :, VEC1["sink"]:VEC1["sink"] + 8] = inputs["gqa_sink"][i][None, :]

    cst = np.zeros((P, NCST), f32)
    cst[:, CST["ident"]:CST["ident"] + P] = np.eye(P, dtype=f32)
    cst[:, CST["ones"]:CST["ones"] + P] = 1.0
    qi, kj = np.arange(P)[:, None], np.arange(3 * P)[None, :]
    cst[:, CST["window"]:CST["window"] + 3 * P] = np.where(np.abs(kj - P - qi) <= P, 0.0, FAR)
    half = ROPE // 2
    freq = (np.float32(10000.0) ** (-np.arange(half, dtype=f32) / f32(half))).astype(f32)
    cst[64:P, CST["freq"]] = np.tile(freq, 4)
    cst[64:96, CST["phase"]] = np.pi / 2
    cst[64:112, CST["sign"]] = 1.0
    cst[96:112, CST["sign"]] = -1.0
    cst[112:P, CST["sign"]] = 1.0
    for g, w in enumerate(POOL_W):
        cst[:, CST["head"] + 16 * g:CST["head"] + 16 * g + 16] = np.array([w / min(t + 1, w) for t in range(16)], f32)[None, :]
    for name, key in (("mix_pre", "g_mix_pre_2"), ("mix_post", "g_mix_post_2"), ("mem_pre", "g_mem_pre_2"), ("mem_kv", "g_mem_kv_2"),
                      ("mem_post", "g_mem_post_2"), ("ffn_pre", "g_ffn_pre_2"), ("ffn_post", "g_ffn_post_2"), ("conv_w", "conv_w_2"),
                      ("conv_b", "conv_b_2"), ("b_a", "lru_b_a_2"), ("b_x", "lru_b_x_2"), ("a_param", "lru_a_param_2"),
                      ("pool", "pool_scale_2"), ("b_gate", "b_gate_2")):
        v = inputs[key][0].reshape(-1, P).T
        cst[:, CST[name]:CST[name] + v.shape[1]] = v

    pos = np.zeros((P, S + ST), np.int32)
    pos[:, 0:S] = inputs["positions"][0][None, :]
    pos[:, S:] = inputs["positions"][0].reshape(ST, P).T
    return {
        "stream": stream,
        "xT": np.ascontiguousarray(inputs["x"][0].T),
        "pT": np.ascontiguousarray(inputs["p"][:, 0].transpose(0, 2, 1)),
        "memT": np.ascontiguousarray(inputs["mem_2"][0].T),
        "vec1": vec1, "cst": cst, "pos": pos,
    }


def kernel(**inputs):
    import concourse.bacc as bacc
    from concourse.bass_utils import run_bass_kernel_spmd

    nc = bacc.Bacc("TRN2", target_bir_lowering=False, num_devices=1, dynamic_dma_scratch_size=2048)
    arrays = lay_out({k: np.asarray(v) for k, v in inputs.items()})
    feed, args = {}, []
    for name, a in arrays.items():
        feed[f"in_{name}"] = a
        args.append(nc.dram_tensor(f"in_{name}", a.shape, mybir.dt.from_np(a.dtype), kind="ExternalInput").ap())
    args.append(nc.dram_tensor("out_T", (D, S), F32, kind="ExternalOutput").ap())
    block_kernel(nc, *args)
    got = run_bass_kernel_spmd(nc, [feed], core_ids=[0]).results[0]["out_T"]
    return np.ascontiguousarray(got.T).reshape(1, S, D)
```

```python
from contextlib import ExitStack

import numpy as np

import concourse.bass as bass
from concourse import mybir

F32 = mybir.dt.float32
F32R = mybir.dt.float32r
I32 = mybir.dt.int32
ALU = mybir.AluOpType
ACT = mybir.ActivationFunctionType
AX_X = mybir.AxisListType.X

P = 128
S = 512
D = 1024
DEPTH = 2
KD = D // P
ST = S // P
EPS = 1e-6
PLE_DIM = 256
MLA_HEADS, NOPE, ROPE, MLA_V = 8, 64, 32, 64
MLA_QK = NOPE + ROPE
Q_LORA, KV_LORA = 384, 128
GROUPS = 4
GW = D // GROUPS
GH = GW // 2
UW = GW + 32
HEADS, KV_HEADS, HD = 8, 2, 64
FFN = 2816
KF = FFN // P
N_MEM, MEM_HEADS = 256, 4
POOL_W = (2, 4, 8, 16)
PADW = 16
TOPK = 128
BLK = 16
UC = BLK * P
NEG = -1.0e38
TAKEN = -3.0e38
LAG = 3
MASKED = -1.0e30
FAR = 1.0e30
TWO_PI_A = 6.28125
TWO_PI_B = 4059.0 / 2 ** 21
TWO_PI_C = 2 * np.pi - TWO_PI_A - TWO_PI_B
ROUND = 1.5 * 2 ** 23



def pair_tiles(first, second, n):
    out = []
    for m in range(n):
        at = m * (first + second)
        out += [list(range(at, at + first)), list(range(at + first, at + first + second))]
    return out


def plain_tiles(k, n):
    return [list(range(m * k, m * k + k)) for m in range(n)]


def down_tiles():
    out = []
    for m in range(KD):
        out.append([(m // 2) * 48 + (k // 8) * 16 + (m % 2) * 8 + k % 8 for k in range(KF)])
    return out


TILES = {
    "z1": plain_tiles(8, 8),
    "z1b": plain_tiles(8, 3),
    "uq": plain_tiles(3, 8) + [[24 + j] for j in range(4)] + [[28, 29, 30, 31]] * 4,
    "bm": pair_tiles(8, 8, KD),
    "am": pair_tiles(8, 4, KD),
    "cm": pair_tiles(8, 4, KD),
    "bm2": pair_tiles(8, 4, KD),
    "wout": plain_tiles(8, KD),
    "gu": pair_tiles(8, 8, KF),
    "dn": down_tiles(),
    "pp": plain_tiles(2, KD),
    "ple": plain_tiles(8, KD),
    "z2": plain_tiles(8, 23),
    "lru": plain_tiles(1, 12),
    "mq": plain_tiles(8, 4),
    "mk": plain_tiles(8, 4),
    "mv": [list(range(32))] * 2,
    "mo": plain_tiles(4, KD),
}


def end_units(tiles):
    return [max(t) // BLK for t in tiles]


def beside(name, t, per):
    n = max(max(tile) for tile in TILES[name]) + 1
    return range(min(per * t, n), min(per * t + per, n))


def releases(name):
    if name == "four1":
        return [("T", 16)]
    if name == "four2":
        return [("PU", 1), ("T", 5)]
    tiles = TILES[name]
    units = max(max(t) for t in tiles) // BLK + 1
    out, parts = [], 0
    for u in range(units):
        if name == "dn":
            n, done = 2 * (u // 3) + 1, u % 3 == 2
        else:
            n = max(i for i, t in enumerate(tiles) if any(b // BLK == u for b in t))
            done = max(tiles[n]) // BLK == u
        parts += not done
        out.append(("T", n + 1) if done else ("PU", parts))
    return out


NO_TILES = 3


def stage(name, A=0, **more):
    c = dict(more)
    if name in TILES or name in ("four1", "four2"):
        rel = releases(name)
        c["U"] = len(rel)
        c["PU"] = sum(kind == "PU" for kind, _ in rel)
        c["T"] = {"four1": 16, "four2": 5, "z1b": 4, "ple": KD + NO_TILES}.get(name) or len(TILES[name])
    c["A"] = A
    return name, c


STAGES1 = [
    stage("norm1", R=8, SQ=8, SS=8, N=1),
    stage("four1", A=16), stage("four2", A=5), stage("bm", A=8),
    stage("z1", A=5, SS=4), stage("qn", N=2, R=4), stage("uq", A=16),
    stage("z1b", A=1), stage("mla", I=32, H=8, O=4), stage("gqa", I=32, H=8, O=4),
    stage("am", A=8), stage("cm", A=8, R=8),
    stage("wout", A=8, SS=2, AD=6), stage("post1", N=1, X=8),
    stage("norm2", W=8, SQ=8, Q=1, SS=2, N=1), stage("gu", A=KF, R=KF, G=KF),
    stage("dn", A=8, SS=2, AD=6), stage("post2", N=1, X=8),
    stage("pp", A=8), stage("xple", W=8), stage("ple", A=8, SQ=8, SS=2, AD=6), stage("post3", N=1, X=8),
]
STAGES2 = [
    stage("norm1", R=8, SQ=8, SS=8, N=1),
    stage("z2", A=13, R=8), stage("lru", A=12, R=4),
    stage("bm2", A=8), stage("am", A=8), stage("normm", R=8, SQ=8, SS=8, N=1),
    stage("mk", A=4), stage("mv", A=2), stage("dsa", I=32, H=8, O=4), stage("cm", A=8, R=8),
    stage("wout", A=8, SS=2, AD=6), stage("post1", N=1, X=8),
    stage("normh", W=8, SQ=8, Q=1, SS=2, N=1), stage("mq"), stage("mem", I=16, H=4, O=4),
    stage("mo", A=8, SS=2, AD=6), stage("postm", N=1, X=8),
    stage("norm2", W=8, SQ=8, Q=1, SS=2, N=1), stage("gu", A=KF, R=KF, G=KF),
    stage("dn", A=8, SS=2, AD=6), stage("post2", N=1, X=8),
]
KINDS = ("U", "T", "PU", "A", "R", "W", "G", "SQ", "Q", "AD", "SS", "N", "X", "I", "H", "O")


def bases(stages):
    at, out = dict.fromkeys(KINDS, 0), {}
    for name, c in stages:
        out[name] = dict(at)
        for k in KINDS:
            at[k] += c.get(k, 0)
    return out, at


BASE1, TOTAL1 = bases(STAGES1)
BASE2, TOTAL2 = bases(STAGES2)
UNITS = DEPTH * TOTAL1["U"] + TOTAL2["U"]
UNITS_PADDED = UNITS + UNITS % 2
assert TOTAL1["U"] % 2 == 0 and TOTAL1["T"] % 4 == 0
CHAIN_PER_LAYER = 1024

VEC1, _n = {}, 0
for _name, _w in (("mix_pre", 8), ("q_norm", 3), ("kv_norm", 1), ("mix_post", 8), ("ffn_pre", 8), ("ffn_post", 8),
                  ("ple", 8), ("sink", 8)):
    VEC1[_name] = _n
    _n += _w
NV1 = _n
CST, _n = {}, 0
for _name, _w in (("ident", P), ("ones", P), ("window", 3 * P), ("freq", 1), ("phase", 1), ("sign", 1), ("head", 64),
                  ("mix_pre", 8), ("mix_post", 8), ("mem_pre", 8), ("mem_kv", 8), ("mem_post", 8), ("ffn_pre", 8),
                  ("ffn_post", 8), ("conv_w", 16), ("conv_b", 4), ("b_a", 4), ("b_x", 4), ("a_param", 4),
                  ("pool", 4), ("b_gate", 24)):
    CST[_name] = _n
    _n += _w
NCST = _n
KB = 1024
MAP_AT = 2304


class Counts:

    def __init__(self, base, layer):
        self.base, self.layer = base, layer

    def at(self, kind, stage_name, n):
        return self.layer * TOTAL1[kind] + (self.base[stage_name][kind] + n)

    def raw(self, u):
        return (self.layer * (TOTAL1["U"] // 2) + (u // 2 + 1)) * 16


def block_kernel(nc, stream, xT, pT, memT, vec1, cst, pos, out):
    with ExitStack() as ctx:
        def sem(name):
            return ctx.enter_context(nc.semaphore(name))

        def sb(name, kb, shape, dt=F32):
            return nc.alloc_sbuf_tensor_at(name, [P] + shape, dt, offset=MAP_AT + int(kb * KB))

        raw = [sb(f"raw{i}", 8 * i, [UC]) for i in range(2)]
        w_hi = [sb(f"w_hi{i}", 16 + 8 * i, [UC], F32R) for i in range(2)]
        w_lo = [sb(f"w_lo{i}", 32 + 8 * i, [UC], F32R) for i in range(2)]
        x = sb("x", 48, [KD, S])
        h_hi = sb("h_hi", 64, [KD, S], F32R)
        h_lo = sb("h_lo", 80, [KD, S], F32R)
        y = sb("y", 64, [KD, S])
        res = sb("res", 96, [4, S])
        sg = sb("sg", 104, [2, S])
        sq = sb("sq", 108, [2, S])
        rstd = sb("rstd", 112, [2, S])
        sq_acc = rstd[:, 1, :]
        st_max = sb("st_max", 116, [32])
        st_neg = sb("st_neg", 116.25, [32])
        st_sum = sb("st_sum", 116.5, [32])
        st_rec = sb("st_rec", 116.75, [32])
        st_snk = sb("st_snk", 117, [32])
        top8 = sb("top8", 117.25, [8])
        wsc = sb("wsc", 117.5, [ST, 8])
        lruc = sb("lruc", 117.75, [4, 8])
        cs = sb("cs", 118, [S])
        cst_sb = sb("cst_sb", 120, [NCST])
        vec = sb("vec", 124, [NV1])
        posf = sb("posf", 124.5, [S + ST])
        AR = 128

        def ar(name, kb, shape, dt=F32):
            return sb(name, AR + kb, shape, dt)

        U_hi = ar("U_hi", 0, [GROUPS, ST, GW], F32R)
        U_lo = ar("U_lo", 32, [GROUPS, ST, GW], F32R)
        Um_hi = ar("Um_hi", 16, [ST, P], F32R)
        Um_lo = ar("Um_lo", 18, [ST, P], F32R)
        ob_hi = ar("ob_hi", 64, [GROUPS, S], F32R)
        rev_hi = ar("rev_hi", 72, [GROUPS, S], F32R)
        ob_lo = ar("ob_lo", 80, [GROUPS, S], F32R)
        rev_lo = ar("rev_lo", 50, [GROUPS, S], F32R)
        mid_hi = ar("mid_hi", 58, [S], F32R)
        mid_lo = ar("mid_lo", 60, [S], F32R)
        merged1 = ar("merged1", 8, [KD, S])
        cq = ar("cq", 24, [4, S])
        cqn_hi = ar("cqn_hi", 32, [4, S], F32R)
        cqn_lo = ar("cqn_lo", 40, [4, S], F32R)
        qc = ar("qc", 48, [4, S])
        kdup = ar("kdup", 56, [KV_HEADS, S])
        vc = ar("vc", 60, [ST, P])
        kr = ar("kr", 62, [S])
        vcT = ar("vcT", 62, [S])
        q_a = ar("q_a", 64, [MLA_HEADS, S])
        k_a = [ar("k_a0", 80, [4, S]), ar("k_a1", 0, [4, S])]
        v_a = ar("v_a", 24, [ST, S])
        dist = ar("dist", 32, [ST, 3 * P])
        pT0_1 = ar("pT0_1", 38, [ST, S])
        oa_hi = [ar(f"oa_hi{i}", 64 + 4 * i, [S], F32R) for i in range(4)]
        oa_lo = [ar(f"oa_lo{i}", 66 + 4 * i, [S], F32R) for i in range(4)]
        oc_hi = ar("oc_hi", 80, [4, S], F32R)
        oc_lo = ar("oc_lo", 0, [4, S], F32R)
        m_hi1 = ar("m_hi1", 24, [KD, S], F32R)
        m_lo1 = ar("m_lo1", 40, [KD, S], F32R)
        a_hi = ar("a_hi", 0, [KF, S], F32R)
        a_lo = ar("a_lo", 44, [KF, S], F32R)
        e = ar("e", 0, [KD, S])
        sq8 = ar("sq8", 16, [KD, S])
        p_f = ar("p_f", 88, [2, S])
        p_hi = sb("p_hi", 88, [2, S], F32R)
        p_lo = sb("p_lo", 92, [2, S], F32R)
        pT1 = sb("pT1", 96, [ST, S])
        prob1 = [sb("prob1_0", 108, [S]), sb("prob1_1", 110, [S]), ar("prob1_2", 46, [S])]
        prob_mla = prob1 + [sb("prob_mla3", 112, [S])]
        prob_gqa = prob1 + [ar("prob_gqa3", 24, [S])]
        rope_t = [sb("rope_t0", 104, [S]), sb("rope_t1", 106, [S])]
        pos_i = ar("pos_i", 0, [S + ST], I32)
        ang = [ar(f"ang{i}", 4 + 2 * i, [S]) for i in range(4)]
        lx = ar("lx", 0, [4, S])
        lg = ar("lg", 8, [4, S])
        qd = ar("qd", 16, [4, S])
        qi = ar("qi", 24, [4, S])
        kk = ar("kk", 32, [S])
        ki = ar("ki", 34, [S])
        vw = ar("vw", 36, [ST, P])
        vwT = ar("vwT", 46.5, [S])
        pz = ar("pz", 38, [4, PADW + S])
        win = [ar("win0", 46.5, [PADW + S]), ar("win1", 48.75, [PADW + S])]
        pool_hi = ar("pool_hi", 51, [4, S], F32R)
        pool_lo = ar("pool_lo", 59, [4, S], F32R)
        ua = ar("ua", 67, [4, S])
        ua_hi = ar("ua_hi", 75, [4, S], F32R)
        ua_lo = ar("ua_lo", 83, [4, S], F32R)
        lr = ar("lr", 38, [4, S])
        li = sb("li", 96, [4, S])
        lm = ar("lm", 83, [4, S])
        yb_hi = ar("yb_hi", 51, [4, S], F32R)
        yb_lo = ar("yb_lo", 59, [4, S], F32R)
        ya_hi = ar("ya_hi", 24, [4, S], F32R)
        ya_lo = ar("ya_lo", 8, [4, S], F32R)
        score = ar("score", 0, [ST, S])
        merged2 = ar("merged2", 75, [KD, S])
        pT0_2 = ar("pT0_2", 67, [ST, S])
        prob2 = [sb("prob2_0", 108, [S]), sb("prob2_1", 110, [S]), ar("prob2_2", 46.5, [S]), ar("prob2_3", 48.5, [S])]
        od_hi = ar("od_hi", 16, [4, S], F32R)
        od_lo = ar("od_lo", 24, [4, S], F32R)
        m_hi2 = ar("m_hi2", 32, [KD, S], F32R)
        m_lo2 = ar("m_lo2", 48, [KD, S], F32R)
        mq = ar("mq", 0, [4, S])
        memf = ar("memf", 51, [KD, N_MEM])
        mem_hi = ar("mem_hi", 38, [KD, N_MEM], F32R)
        mem_lo = ar("mem_lo", 59, [KD, N_MEM], F32R)
        mem_rstd = ar("mem_rstd", 46.5, [N_MEM])
        mk = ar("mk", 8, [4, N_MEM])
        mv = ar("mv", 12, [2, S])
        pT0_m = ar("pT0_m", 40, [ST, S])
        prob_m = [sb("prob_m0", 108, [S]), sb("prob_m1", 110, [S]), ar("prob_m2", 48, [S]), ar("prob_m3", 66, [S])]
        om_hi = ar("om_hi", 50, [4, S], F32R)
        om_lo = ar("om_lo", 58, [4, S], F32R)

        bank = [ctx.enter_context(nc.psum_tensor(f"bank{i}", [P, S], F32)) for i in range(8)]
        SS_BANK, SS_BANK2 = bank[7], bank[6]
        SCORES, TURNED, VALUES = bank[4:6], bank[6], bank[7]

        ident = cst_sb[:, CST["ident"]:CST["ident"] + P]
        ones = cst_sb[:, CST["ones"]:CST["ones"] + P]

        def cc(name, j=0, lo=0, hi=P):
            return cst_sb[lo:hi, CST[name] + j:CST[name] + j + 1]

        def vv(name, j=0):
            return vec[:, VEC1[name] + j:VEC1[name] + j + 1]

        raw_ready = [sem("raw_ready0"), sem("raw_ready1")]
        hi_ready = sem("hi_ready")
        lo_ready = sem("lo_ready")
        tile_done = sem("tile_done")
        part_done = sem("part_done")
        act_took = sem("act_took")
        tile_free = sem("tile_free")
        x_loaded = sem("x_loaded")
        post_ready = sem("post_ready")
        x_ready = sem("x_ready")
        raw_hi = sem("raw_hi")
        raw_split = sem("raw_split")
        sq_tree = sem("sq_tree")
        gated = sem("gated")
        res_ready = sem("res_ready")
        res_hi = sem("res_hi")
        res_split = sem("res_split")
        sq_ready = sem("sq_ready")
        sq_added = sem("sq_added")
        ss_done = sem("ss_done")
        rms_ready = sem("rms_ready")
        vec_loaded = sem("vec_loaded")
        p_loaded = sem("p_loaded")
        p_hi_ready = sem("p_hi_ready")
        p_split = sem("p_split")
        cst_loaded = sem("cst_loaded")
        pos_loaded = sem("pos_loaded")
        mem_loaded = sem("mem_loaded")
        pos_ready = sem("pos_ready")
        angle_ready = sem("angle_ready")
        sin_ready = sem("sin_ready")
        kr_copied = sem("kr_copied")
        dist_ready = sem("dist_ready")
        logits_done = sem("logits_done")
        shift_ready = sem("shift_ready")
        exp_done = sem("exp_done")
        prob_ready = sem("prob_ready")
        turned = sem("turned")
        turn_taken = sem("turn_taken")
        head_done = sem("head_done")
        o_hi_ready = sem("o_hi_ready")
        o_split = sem("o_split")
        vchain = sem("vchain")
        achain = sem("achain")
        pad_ready = sem("pad_ready")
        rev_hi_ready = sem("rev_hi_ready")
        rev_ready = sem("rev_ready")
        lru_gates = sem("lru_gates")
        softplus_ready = sem("softplus_ready")
        vw_turned = sem("vw_turned")
        idx_done = sem("idx_done")
        idx_relu = sem("idx_relu")
        idx_added = sem("idx_added")
        out_done = sem("out_done")

        block = ctx.enter_context(nc.Block())

        def windowed(b):
            return range(max(b - 1, 0), min(b + 2, ST))

        ATT = {
            "mla": dict(heads=8, keys=lambda b: range(ST), scale=MLA_QK ** -0.5, pT=[pT0_1, pT1], prob=prob_mla, biased=False,
                        q=lambda h, b: q_a[0:MLA_QK, h, b * P:(b + 1) * P],
                        k=lambda h, ks: k_a[h // 4][0:MLA_QK, h % 4, ks.start * P:ks.stop * P],
                        v=lambda h, t: v_a[:, t, h * MLA_V:(h + 1) * MLA_V],
                        o=lambda i: (oa_hi[i][:, :], oa_lo[i][:, :]), per_tile=2),
            "gqa": dict(heads=8, keys=windowed, scale=HD ** -0.5, pT=[pT0_1, pT1], prob=prob_gqa, biased=True,
                        q=lambda h, b: qc[64 * (h % 2):64 * (h % 2) + 64, h // 2, b * P:(b + 1) * P],
                        k=lambda h, ks: kdup[64 * (h % 2):64 * (h % 2) + 64, h // 4, ks.start * P:ks.stop * P],
                        v=lambda h, t: vc[:, t, (h // 4) * HD:(h // 4 + 1) * HD],
                        o=lambda i: (oc_hi[:, i, :], oc_lo[:, i, :]), per_tile=2),
            "dsa": dict(heads=8, keys=lambda b: range(b + 1), scale=HD ** -0.5, pT=[pT0_2, pT1], prob=prob2, biased=True,
                        q=lambda h, b: qd[64 * (h % 2):64 * (h % 2) + 64, h // 2, b * P:(b + 1) * P],
                        k=lambda h, ks: kk[64 * (h % 2):64 * (h % 2) + 64, ks.start * P:ks.stop * P],
                        v=lambda h, t: vw[:, t, 0:HD],
                        o=lambda i: (od_hi[:, i, :], od_lo[:, i, :]), per_tile=2),
            "mem": dict(heads=MEM_HEADS, keys=lambda b: range(N_MEM // P), scale=P ** -0.5, pT=[pT0_m, pT1], prob=prob_m,
                        biased=False,
                        q=lambda h, b: mq[:, h, b * P:(b + 1) * P],
                        k=lambda h, ks: mk[:, h, ks.start * P:ks.stop * P],
                        v=lambda h, t: mv[:, t, h * P:(h + 1) * P],
                        o=lambda i: (om_hi[:, i, :], om_lo[:, i, :]), per_tile=1),
        }

        IDX_FROM, IDX_ITEMS = 11, 32

        def idx_items(n):
            return range(min(3 * max(n - IDX_FROM, 0), IDX_ITEMS), min(3 * max(n - IDX_FROM + 1, 0), IDX_ITEMS))
        assert idx_items(22).stop == IDX_ITEMS

        NORMS = {
            1: {"norm1": ("mix_pre", x, h_hi, h_lo, S)},
            2: {"norm1": ("mix_pre", x, h_hi, h_lo, S), "normm": ("mem_kv", memf, mem_hi, mem_lo, N_MEM)},
        }
        RAW_NORMS = {(1, "norm2"): "ffn_pre", (2, "norm2"): "ffn_pre", (2, "normh"): "mem_pre"}
        MERGES = {
            (1, "bm"): lambda k: (ob_hi[:, k, :], ob_lo[:, k, :]) if k < GROUPS else (rev_hi[:, k - GROUPS, :], rev_lo[:, k - GROUPS, :]),
            (1, "am"): lambda k: (oa_hi[k][:, :], oa_lo[k][:, :]),
            (1, "cm"): lambda k: (oc_hi[:, k, :], oc_lo[:, k, :]),
            (2, "bm2"): lambda k: (yb_hi[:, k, :], yb_lo[:, k, :]),
            (2, "am"): lambda k: (ya_hi[:, k, :], ya_lo[:, k, :]),
            (2, "cm"): lambda k: (od_hi[:, k, :], od_lo[:, k, :]),
        }
        MERGED = {1: (merged1, m_hi1, m_lo1), 2: (merged2, m_hi2, m_lo2)}

        @block.sync
        def _(sp):
            for p in range(2):
                sp.dma_start(raw[p][:, :], stream[p]).then_inc(raw_ready[p], 16)
                if p == 0:
                    sp.dma_start(x[:, :, :], xT.rearrange("(k p) s -> p k s", p=P)).then_inc(x_loaded, 16)
            with sp.Fori(1, UNITS_PADDED // 2) as i:
                for p in range(2):
                    sp.wait_ge(lo_ready, i * 2 + (p - 1))
                    sp.dma_start(raw[p][:, :], stream[bass.ds(i * 2 + p, 1)].rearrange("a p n -> (a p) n")).then_inc(raw_ready[p], 16)
            for p in range(2):
                sp.wait_ge(raw_ready[p], 16 * (UNITS_PADDED // 2))

        @block.tensor
        def _(pe):
            def mac(ps, w, bb, ncol, xh, xl, start, stop, swap=False):
                wh = w_hi[w][:, bb * P:bb * P + ncol]
                wl = w_lo[w][:, bb * P:bb * P + ncol]
                if swap:
                    nc.tensor.matmul(ps, xh, wh, start=start, stop=False)
                    nc.tensor.matmul(ps, xh, wl, start=False, stop=False)
                    return nc.tensor.matmul(ps, xl, wh, start=False, stop=stop)
                nc.tensor.matmul(ps, wh, xh, start=start, stop=False)
                nc.tensor.matmul(ps, wh, xl, start=False, stop=False)
                return nc.tensor.matmul(ps, wl, xh, start=False, stop=stop)

            def free_bank(c, st, n):
                t = c.base[st]["T"] + n
                if t >= 4 or c.base is BASE2:
                    pe.wait_ge(tile_free, c.at("T", st, n - 3))
                return bank[t % 4]

            def run(c, st, operand, first=0, last=None, width=S, after=None, together=False):
                tiles = TILES[st]
                u0 = c.base[st]["U"]
                ends = {}
                for n, t in enumerate(tiles):
                    for j, b in enumerate(t):
                        ends[b // BLK] = (n, j)
                seen = -1 if first == 0 else tiles[first - 1][-1] // BLK
                if together:
                    pe.wait_ge(lo_ready, c.at("U", st, 1))
                    seen, first = 0, 2
                    two = [free_bank(c, st, n)[:, 0:width] for n in range(2)]
                    for j in range(KD):
                        for n in range(2):
                            xh, xl, need = operand(n, j)
                            if need is not None:
                                pe.wait_ge(need[0], need[1])
                            mm = mac(two[n], u0 % 2, tiles[n][j], P, xh, xl, j == 0, j == KD - 1)
                            if j == KD - 1:
                                mm.then_inc(tile_done, 1)
                    if after is not None:
                        after(1)
                for n in range(first, len(tiles) if last is None else last):
                    t = tiles[n]
                    ps = free_bank(c, st, n)[:, 0:width]
                    for j, b in enumerate(t):
                        u = b // BLK
                        if u > seen:
                            pe.wait_ge(lo_ready, c.at("U", st, u + 1))
                            seen = u
                        xh, xl, need = operand(n, j)
                        if need is not None:
                            pe.wait_ge(need[0], need[1])
                        mm = mac(ps, (u0 + u) % 2, b % BLK, P, xh, xl, j == 0, j == len(t) - 1)
                        if j == len(t) - 1:
                            mm.then_inc(tile_done, 1)
                        elif ends[u] == (n, j):
                            mm.then_inc(part_done, 1)
                    if after is not None:
                        after(n)

            def run_blocks(c, st, operand, blocks, width=S):
                for b in blocks:
                    u = b // BLK
                    n = [i for i, t in enumerate(TILES[st]) if b in t][0]
                    t = TILES[st][n]
                    j = t.index(b)
                    if j == 0:
                        free_bank(c, st, n)
                    if b % BLK == 0:
                        pe.wait_ge(lo_ready, c.at("U", st, u + 1))
                    xh, xl, need = operand(n, j)
                    if need is not None:
                        pe.wait_ge(need[0], need[1])
                    mm = mac(bank[(c.base[st]["T"] + n) % 4][:, 0:width], (c.base[st]["U"] + u) % 2, b % BLK, P, xh, xl,
                             j == 0, j == len(t) - 1)
                    if j == len(t) - 1:
                        mm.then_inc(tile_done, 1)
                    elif b % BLK == BLK - 1:
                        mm.then_inc(part_done, 1)

            def down(c, a_need):
                st = "dn"
                u0 = c.base[st]["U"]
                for u in range(12):
                    pair, part = u // 3, u % 3
                    pe.wait_ge(lo_ready, c.at("U", st, u + 1))
                    ks = range(8 * part, min(8 * part + 8, KF))
                    for q in range(2):
                        n = 2 * pair + q
                        ps = free_bank(c, st, n) if part == 0 else bank[(c.base[st]["T"] + n) % 4]
                        for k in ks:
                            if u == 0 and q == 0 or k >= 16 and u == 2 and q == 0 or k >= 8 and u == 1 and q == 0:
                                pe.wait_ge(res_split, a_need(k))
                            mm = mac(ps[:, :], (u0 + u) % 2, 8 * q + k % 8, P, a_hi[:, k, :], a_lo[:, k, :],
                                     k == 0, k == KF - 1)
                        if part == 2:
                            mm.then_inc(tile_done, 1)
                        elif q == 1:
                            mm.then_inc(part_done, 1)
                project_sum(c, "dn", act_took, "A")

            def square_sum(ready, value, src, start, stop, ps=None):
                pe.wait_ge(ready, value)
                ps = SS_BANK if ps is None else ps
                nc.tensor.matmul(ps[:, 0:src.shape[-1]], ones, src, start=start, stop=stop).then_inc(ss_done, 1)

            def tree_sum(c, st):
                for j in range(2):
                    square_sum(sq_tree, c.at("Q", st, 1), sq8[:, j, :], j == 0, j == 1)

            def project_sum(c, st, ready, kind):
                square_sum(sq_added, c.at("AD", st, 6), sq_acc, True, False)
                square_sum(ready, c.at(kind, st, KD), sq[:, 1, :], False, True)

            def norm(c, st, which):
                width = NORMS[which][st][4]
                for m in range(KD):
                    square_sum(sq_ready, c.at("SQ", st, m + 1), sq[:, m % 2, 0:width], m == 0, m == KD - 1)

            def attention(c, st, ready, also=None):
                a = ATT[st]
                items = [(h, b) for h in range(a["heads"]) for b in range(ST)]
                for sem_, value in ready:
                    pe.wait_ge(sem_, value)
                for t in range(len(items) + LAG):
                    if t < len(items):
                        h, b = items[t]
                        if t >= 2:
                            pe.wait_ge(exp_done, c.at("I", st, t - 1))
                        ks = a["keys"](b)
                        nc.tensor.matmul(SCORES[t % 2][:, 0:len(ks) * P], a["q"](h, b), a["k"](h, ks),
                                         start=True, stop=True).then_inc(logits_done, 1)
                    if t >= LAG:
                        i = t - LAG
                        h, b = items[i]
                        pe.wait_ge(prob_ready, c.at("I", st, i + 1))
                        if i >= 1:
                            pe.wait_ge(turn_taken, c.at("I", st, i))
                        n = len(a["keys"](b))
                        for j in range(n):
                            mm = nc.tensor.transpose(TURNED[:, j * P:(j + 1) * P],
                                                     a["prob"][i % 4][:, j * P:(j + 1) * P], ident)
                        mm.then_inc(turned, 1)
                        if b == ST - 1 and h >= 1:
                            values(c, st, h - 1)
                    if also is not None:
                        also(t)
                values(c, st, a["heads"] - 1)

            def values(c, st, h):
                a = ATT[st]
                per = a["per_tile"]
                pe.wait_ge(turn_taken, c.at("I", st, ST * h + ST))
                tile = h // per
                if h % per == 0 and (tile >= 1 or st != "mla"):
                    pe.wait_ge(o_split, c.at("O", st, tile))
                rows = P // per
                ps = VALUES
                lo = rows * (h % per)
                if len(set(tuple(a["keys"](b)) for b in range(ST))) == 1:
                    n = len(a["keys"](0))
                    for t in range(n):
                        mm = nc.tensor.matmul(ps[lo:lo + rows, :], a["v"](h, t), a["pT"][h % 2][:, t, :],
                                              start=t == 0, stop=t == n - 1)
                else:
                    for b in range(ST):
                        ks = a["keys"](b)
                        for j, t in enumerate(ks):
                            mm = nc.tensor.matmul(ps[lo:lo + rows, b * P:(b + 1) * P], a["v"](h, t),
                                                  a["pT"][h % 2][:, j, b * P:(b + 1) * P],
                                                  start=j == 0, stop=j == len(ks) - 1)
                mm.then_inc(head_done, 1)

            def merge_operand(which, st, need=None):
                def operand(n, j):
                    if n % 2 == 0:
                        return h_hi[:, j, :], h_lo[:, j, :], None
                    xh, xl = MERGES[which, st](j)
                    return xh, xl, need(j) if need is not None and n == 1 else None
                return operand

            def merge(c, which, st, need=None, after=None):
                run(c, st, merge_operand(which, st, need), after=after)

            def project(c, st, hi, lo, need):
                run(c, st, lambda n, j: (hi(j), lo(j), need(j) if n == 0 else None))
                project_sum(c, st, act_took, "A")

            def gate_up(c):
                st = "gu"
                u0, t0 = c.base[st]["U"], c.base[st]["T"]

                def pair(i, waits):
                    for p in range(2):
                        pe.wait_ge(lo_ready, c.at("U", st, p + 1) + i * 2)
                        if waits and p == 0:
                            pe.wait_ge(tile_free, c.at("T", st, -2))
                            for k in range(KD):
                                pe.wait_ge(raw_split, c.at("W", "norm2", k + 1))
                                for g in range(2):
                                    mm = mac(bank[(t0 + g) % 4][:, :], u0 % 2, 8 * g + k, P, h_hi[:, k, :], h_lo[:, k, :],
                                             k == 0, k == KD - 1)
                                    if k == KD - 1:
                                        mm.then_inc(tile_done, 1)
                            tree_sum(c, "norm2")
                            continue
                        for g in range(2):
                            pe.wait_ge(tile_free, c.at("T", st, 2 * p + g - 3) + i * 4)
                            for k in range(KD):
                                mm = mac(bank[(t0 + 2 * p + g) % 4][:, :], (u0 + p) % 2, 8 * g + k, P,
                                         h_hi[:, k, :], h_lo[:, k, :], k == 0, k == KD - 1)
                            mm.then_inc(tile_done, 1)
                pair(0, True)
                with pe.Fori(1, KF // 2) as i:
                    pair(i, False)

            def first_block(L):
                c = Counts(BASE1, L)
                norm(c, "norm1", 1)
                pe.wait_ge(lo_ready, c.at("U", "four1", 1))
                u = c.base["four1"]["U"] % 2
                for n in range(16):
                    g, t = n // ST, n % ST
                    ps = free_bank(c, "four1", n)
                    for j in range(2):
                        k = 2 * g + j
                        if t == 0:
                            pe.wait_ge(res_split, c.at("R", "norm1", k + 1))
                        mm = mac(ps[:, 0:UW], u, 4 * j, UW, h_hi[:, k, t * P:(t + 1) * P], h_lo[:, k, t * P:(t + 1) * P],
                                 j == 0, j == 1, swap=True)
                    mm.then_inc(tile_done, 1)
                u2 = c.base["four2"]["U"]

                def cosines(g):
                    pe.wait_ge(tile_free, c.at("T", "four1", 4 * g + 4))
                    ps = free_bank(c, "four2", 1 + g)
                    for t in range(ST):
                        mm = mac(ps[:, :], u2 % 2, 4 * t, S, U_hi[:, g, t, 0:GH], U_lo[:, g, t, 0:GH], t == 0, False, swap=True)
                    return mm
                pe.wait_ge(lo_ready, c.at("U", "four2", 1))
                cosines(0)
                cosines(1)
                pe.wait_ge(tile_free, c.at("T", "four1", 16))
                ps = free_bank(c, "four2", 0)
                for t in range(ST):
                    mm = mac(ps[:, :], u2 % 2, 4 * t, S, Um_hi[:, t, :], Um_lo[:, t, :], t == 0, t == ST - 1, swap=True)
                mm.then_inc(tile_done, 1)
                cosines(2)
                cosines(3).then_inc(part_done, 1)
                pe.wait_ge(lo_ready, c.at("U", "four2", 2))
                for g in range(GROUPS):
                    for t in range(ST):
                        mm = mac(bank[(c.base["four2"]["T"] + 1 + g) % 4][:, :], (u2 + 1) % 2, 4 * t, S, U_hi[:, g, t, GH:GW],
                                 U_lo[:, g, t, GH:GW], False, t == ST - 1, swap=True)
                    mm.then_inc(tile_done, 1)
                merge(c, 1, "bm", lambda k: (tile_free, c.at("T", "four2", k + 2)) if k < GROUPS else
                      (rev_ready, c.layer * GROUPS + (k - GROUPS + 1)))
                def after_z1(n):
                    if 1 <= n <= 3:
                        square_sum(act_took, c.at("A", "z1", n), sq[:, (n - 1) % 2, :], n == 1, n == 3)
                    if n == 4:
                        square_sum(act_took, c.at("A", "z1", 4), sq[:, 1, :], True, True, ps=SS_BANK2)
                def normed(n, j):
                    return h_hi[:, j, :], h_lo[:, j, :], None
                run(c, "z1", normed, after=after_z1)
                run(c, "uq", lambda n, j: (cqn_hi[:, j if n < 8 else 3, :], cqn_lo[:, j if n < 8 else 3, :],
                                           (res_split, c.at("R", "qn", (j if n < 8 else 3) + 1)) if n in (0, 8) else None), last=12)
                for t in range(ST):
                    ps = free_bank(c, "uq", 12 + t)
                    mac(ps[:, :], (c.base["uq"]["U"] + 1) % 2, 12, S, cqn_hi[:, 3, t * P:(t + 1) * P],
                        cqn_lo[:, 3, t * P:(t + 1) * P], True, True, swap=True).then_inc(tile_done, 1)
                attention(c, "mla", [(tile_free, c.at("T", "uq", 16)), (kr_copied, c.layer + 1)],
                          lambda t: run_blocks(c, "z1b", normed, beside("z1b", t, 1)))
                pe.wait_ge(act_took, c.at("A", "z1b", 1))
                ps = free_bank(c, "z1b", 3)
                for t in range(ST):
                    mm = nc.tensor.transpose(ps[:, t * P:(t + 1) * P], vcT[:, t * P:(t + 1) * P], ident)
                mm.then_inc(tile_done, 1)
                am = merge_operand(1, "am", lambda k: (o_split, c.at("O", "mla", k + 1)))
                attention(c, "gqa", [(tile_free, c.at("T", "z1b", 4))], lambda t: run_blocks(c, "am", am, beside("am", t, 3)))
                merge(c, 1, "cm", lambda k: (o_split, c.at("O", "gqa", k + 1)))
                project(c, "wout", lambda k: m_hi1[:, k, :], lambda k: m_lo1[:, k, :],
                        lambda k: (res_split, c.at("R", "cm", k + 1)))
                gate_up(c)
                down(c, lambda k: c.at("R", "gu", k + 1))

                run(c, "pp", lambda n, j: (p_hi[:, j, :], p_lo[:, j, :], (p_split, c.layer + 1) if n == 0 and j == 0 else None))
                run(c, "ple", lambda n, j: (h_hi[:, j, :], h_lo[:, j, :], (raw_split, c.at("W", "xple", j + 1)) if n == 0 else None),
                    together=True)
                project_sum(c, "ple", sq_ready, "SQ")
                pe.sem_inc(tile_done, NO_TILES)

            pe.wait_ge(cst_loaded, 16)
            with pe.Fori(0, DEPTH) as L:
                first_block(L)

            c = Counts(BASE2, DEPTH)
            norm(c, "norm1", 2)
            def after_z2(n):
                if n == 10:
                    pe.wait_ge(act_took, c.at("A", "z2", 9))
                    for t in range(ST):
                        mm = nc.tensor.transpose(TURNED[:, t * P:(t + 1) * P], vwT[:, t * P:(t + 1) * P], ident)
                    mm.then_inc(vw_turned, 1)
                for t in idx_items(n):
                    if t == 0:
                        pe.wait_ge(tile_free, c.at("T", "z2", 9))
                    if t >= 2:
                        pe.wait_ge(idx_relu, t - 1)
                    b, hh = t // 8, t % 8
                    r = slice(64 * (hh % 2), 64 * (hh % 2) + 64)
                    nc.tensor.matmul(SCORES[t % 2][:, 0:(b + 1) * P], qi[r, hh // 2, b * P:(b + 1) * P], ki[r, 0:(b + 1) * P],
                                     start=True, stop=True).then_inc(idx_done, 1)
            run(c, "z2", lambda n, j: (h_hi[:, j, :], h_lo[:, j, :], (res_split, c.at("R", "norm1", j + 1)) if n == 0 else None),
                together=True, after=after_z2)

            def lru_operand(n, j):
                if n < 4:
                    return pool_hi[:, n, :], pool_lo[:, n, :], (res_split, c.at("R", "z2", 4 + n + 1))
                return ua_hi[:, n % 4, :], ua_lo[:, n % 4, :], (res_split, c.at("R", "z2", n % 4 + 1)) if n < 8 else None
            run(c, "lru", lru_operand)
            merge(c, 2, "bm2", lambda k: (tile_free, c.at("T", "lru", k + 1)))

            def sum_mem(n):
                for j in range(n - 5, n - 3) if n in (5, 7, 9, 11) else ():
                    square_sum(sq_ready, c.at("SQ", "normm", j + 1), sq[:, j % 2, 0:N_MEM], j == 0, j == KD - 1)
            merge(c, 2, "am", lambda k: (res_split, c.at("R", "lru", k + 1)), after=sum_mem)

            def mem_operand(n, j):
                return mem_hi[:, j, :], mem_lo[:, j, :], (res_split, c.at("R", "normm", j + 1)) if n == 0 else None

            def mem_kv(t):
                run_blocks(c, "mk", mem_operand, beside("mk", t, 2), N_MEM)
                if 16 <= t < 32:
                    half, rows, j = (t - 16) // 8, (t - 16) % 8 // 4, t % 4
                    u = c.base["mv"]["U"] + half
                    if t % 8 == 0:
                        pe.wait_ge(lo_ready, c.at("U", "mv", half + 1))
                    if t < 24 and j == 0:
                        free_bank(c, "mv", rows)
                    k = 4 * half + j
                    mm = mac(bank[(c.base["mv"]["T"] + rows) % 4][:, :], u % 2, 4 * j, S, mem_hi[:, k, rows * P:(rows + 1) * P],
                             mem_lo[:, k, rows * P:(rows + 1) * P], k == 0, k == KD - 1, swap=True)
                    if k == KD - 1:
                        mm.then_inc(tile_done, 1)
                    elif t == 23:
                        mm.then_inc(part_done, 1)
            attention(c, "dsa", [(tile_free, c.at("T", "am", 16))], mem_kv)
            merge(c, 2, "cm", lambda k: (o_split, c.at("O", "dsa", k + 1)))
            project(c, "wout", lambda k: m_hi2[:, k, :], lambda k: m_lo2[:, k, :], lambda k: (res_split, c.at("R", "cm", k + 1)))
            run(c, "mq", lambda n, j: (h_hi[:, j, :], h_lo[:, j, :], (raw_split, c.at("W", "normh", j + 1)) if n == 0 else None),
                together=True, after=lambda n: tree_sum(c, "normh") if n == 1 else None)
            attention(c, "mem", [(tile_free, c.at("T", "mq", 4))])
            project(c, "mo", lambda k: om_hi[:, k, :], lambda k: om_lo[:, k, :], lambda k: (o_split, c.at("O", "mem", k + 1)))
            gate_up(c)
            down(c, lambda k: c.at("R", "gu", k + 1))

        RR1, RR2 = {}, {}
        for table, stages in ((RR1, STAGES1), (RR2, STAGES2)):
            n = 0
            for name, cnt in stages:
                table[name] = n
                n += 0 if name == "gu" else cnt.get("R", 0)
            table["all"] = n

        def result_value(c, st, m):
            return c.layer * RR1["all"] + ((RR1 if c.base is BASE1 else RR2)[st] + m + 1)

        def unit_steps(st, evac, split, n_units=None):
            if st == "four1":
                ends = [0] * 16
            elif st == "four2":
                ends = [0] + [1] * GROUPS
            elif st == "dn":
                ends = [3 * (m // 2) + 2 for m in range(KD)]
            else:
                ends = end_units(TILES[st])
            for u in range(max(ends) + 1):
                for n, end in enumerate(ends):
                    if end == u:
                        evac(n)
                split(u)

        @block.scalar
        def _(act):
            chain = {"n": 0, "base": 0}

            def link(ins):
                chain["n"] += 1
                ins.then_inc(achain, 1)
                act.wait_ge(achain, chain["base"] + chain["n"])

            def split_unit(c, st, u, extra=None):
                v = c.base[st]["U"] + u + 2
                if c.base is BASE2 and v >= TOTAL2["U"]:
                    return
                kind, n = releases(st)[u]
                act.wait_ge(tile_done if kind == "T" else part_done, c.at(kind, st, n))
                act.wait_ge(raw_ready[v % 2], c.raw(v))
                nc.scalar.activation(w_hi[v % 2][:, :], raw[v % 2][:, :], ACT.Copy).then_inc(hi_ready, 1)

            def stage_loop(c, st, evac):
                unit_steps(st, evac, lambda u: split_unit(c, st, u))

            def take_hi(c, st, n, a, dst, func=ACT.Copy, src=None, **kw):
                act.wait_ge(tile_done, c.at("T", st, n + 1))
                t = c.base[st]["T"] + n
                ps = bank[t % 4] if src is None else src(bank[t % 4])
                nc.scalar.activation(dst, ps[:, :] if src is None else ps, func, **kw).then_inc(act_took, 1)

            def square_slot(c, st, j):
                if j >= 2:
                    if "AD" in dict(STAGES1 + STAGES2)[st]:
                        act.wait_ge(sq_added, c.at("AD", st, max(j - 2, 1)))
                    else:
                        act.wait_ge(ss_done, c.at("SS", st, j - 1))
                return sq[:, j % 2, :]

            def squares_of_psum(c, st, n):
                take_hi(c, st, n, n, square_slot(c, st, n), ACT.Square)

            def squares(c, st, j, src, ready, width=S):
                act.wait_ge(ready[0], ready[1])
                nc.scalar.activation(square_slot(c, st, j)[:, 0:width], src, ACT.Square).then_inc(sq_ready, 1)

            def log_table():
                act.preload_act_table_set("natural_log_exp_and_others")

            def root(ss_stage, c, ss, width, features, slot=0, ps=None, dst=None):
                act.wait_ge(ss_done, c.at("SS", ss_stage, ss))
                ps = SS_BANK if ps is None else ps
                r = rstd[:, slot, 0:width] if dst is None else dst
                link(nc.scalar.activation(r, ps[:, 0:width], ACT.Ln, bias=EPS, scale=1.0 / features))
                nc.scalar.activation(r, r, ACT.Exp, scale=-0.5).then_inc(rms_ready, 1)

            def split_hi(c, st, r, dst, src, ready):
                act.wait_ge(ready[0], ready[1])
                nc.scalar.activation(dst, src, ACT.Copy).then_inc(res_hi, 1)

            def norm(c, st, which, ready, then=None):
                _, src, hi, lo, width = NORMS[which][st]
                for m in range(KD):
                    squares(c, st, m, src[:, m, :], ready(m), width)
                if then is not None:
                    then()
                root(st, c, KD, width, D)
                for m in range(KD):
                    r = c.base[st]["R"] + m
                    split_hi(c, st, m, hi[:, m, :], res[:, r % 4, 0:width], (res_ready, result_value(c, st, m)))

            def raw_norm(c, st, which, after):
                for m in range(KD):
                    act.wait_ge(x_ready, c.at("X", after, m + 1) + 8)
                    g = (vv if which == 1 else cc)(RAW_NORMS[which, st], m)
                    nc.scalar.activation(h_hi[:, m, :], x[:, m, :], ACT.Identity, scale=g).then_inc(raw_hi, 1)
                    nc.scalar.activation(sq8[:, m, :], x[:, m, :], ACT.Square).then_inc(sq_ready, 1)
                root(st, c, 2, S, D)

            def merge(c, which, st, b_gate=None, extra=None):
                def evac(n):
                    m = n // 2
                    if n % 2 == 0:
                        act.wait_ge(tile_free, c.at("T", st, n - 2))
                        kw = {} if b_gate is None else {"bias": cc("b_gate", 8 * b_gate + m)}
                        take_hi(c, st, n, m, sg[:, m % 2, :], ACT.Sigmoid, **kw)
                    elif st == "cm":
                        r = c.base[st]["R"] + m
                        split_hi(c, st, m, MERGED[which][1][:, m, :], res[:, r % 4, :], (res_ready, result_value(c, st, m)))
                    if n % 2 == 1 and extra is not None:
                        extra(m)
                stage_loop(c, st, evac)

            def attention(c, st, sink=False, also=None):
                a = ATT[st]
                items = [(h, b) for h in range(a["heads"]) for b in range(ST)]
                for t in range(len(items) + LAG):
                    if t < len(items):
                        h, b = items[t]
                        n = len(a["keys"](b)) * P
                        act.wait_ge(shift_ready, c.at("I", st, t + 1))
                        if not a["biased"] and t >= 4:
                            act.wait_ge(turned, c.at("I", st, t - 3))
                        if sink:
                            nc.scalar.activation(st_snk[:, t:t + 1], vv("sink", h), ACT.Exp, bias=st_neg[:, t:t + 1])
                        src = a["prob"][t % 4] if a["biased"] else SCORES[t % 2]
                        nc.scalar.activation(a["prob"][t % 4][:, 0:n], src[:, 0:n], ACT.Exp, bias=st_neg[:, t:t + 1],
                                             scale=a["scale"], accum_out=st_sum[:, t:t + 1]).then_inc(exp_done, 1)
                    if t >= LAG:
                        i = t - LAG
                        h, b = items[i]
                        n = len(a["keys"](b))
                        act.wait_ge(turned, c.at("I", st, i + 1))
                        if h >= 2 and b == 0:
                            act.wait_ge(head_done, c.at("H", st, h - 1))
                        nc.scalar.activation(a["pT"][h % 2][:, 0:n, b * P:(b + 1) * P],
                                             TURNED[:, 0:n * P].rearrange("p (t q) -> p t q", t=n),
                                             ACT.Copy).then_inc(turn_taken, 1)
                        if b == ST - 1 and h >= 1 and h % a["per_tile"] == 0:
                            output_hi(c, st, h // a["per_tile"] - 1)
                    if also is not None and t >= 1:
                        also(t - 1)
                output_hi(c, st, a["heads"] // a["per_tile"] - 1)

            def after_blocks(c, st, blocks, evac):
                for b in blocks:
                    for n, t in enumerate(TILES[st]):
                        if t[-1] == b:
                            evac(n)
                    if b % BLK == BLK - 1 or b == TILES[st][-1][-1]:
                        split_unit(c, st, b // BLK)

            def output_hi(c, st, i):
                a = ATT[st]
                act.wait_ge(head_done, c.at("H", st, (i + 1) * a["per_tile"]))
                nc.scalar.activation(a["o"](i)[0], VALUES[:, :], ACT.Copy).then_inc(o_hi_ready, 1)

            def gate_up(c):
                st = "gu"
                u0 = c.base[st]["U"]
                act.preload_act_table(ACT.Silu)
                with act.Fori(0, KF // 2) as i:
                    for p in range(2):
                        act.wait_ge(tile_free, c.at("T", st, 2 * p + 1) + i * 4)
                        nc.scalar.activation(sg[:, p, :], sg[:, p, :], ACT.Silu).then_inc(act_took, 1)
                        act.wait_ge(gated, c.at("G", st, p + 1) + i * 2)
                        nc.scalar.activation(a_hi[:, bass.ds(i * 2 + p, 1), :].rearrange("p a s -> p (a s)"), res[:, p, :], ACT.Copy).then_inc(res_hi, 1)
                        act.wait_ge(tile_done, c.at("T", st, 2 * p + 2) + i * 4)
                        v = (u0 + p) % 2
                        act.wait_ge(raw_ready[v], c.raw(u0 + p + 2) + i * 16)
                        nc.scalar.activation(w_hi[v][:, :], raw[v][:, :], ACT.Copy).then_inc(hi_ready, 1)

            def project(c, st):
                log_table()
                stage_loop(c, st, lambda n: squares_of_psum(c, st, n))

            act.dma_start(cst_sb[:, :], cst).then_inc(cst_loaded, 16)
            act.dma_start(pos_i[:, :], pos).then_inc(pos_loaded, 16)
            act.wait_ge(angle_ready, 1)
            nc.scalar.activation(cs[64:P, :], ang[2][64:P, :], ACT.Sin).then_inc(sin_ready, 1)
            for v in range(2):
                act.wait_ge(raw_ready[v], 16)
                nc.scalar.activation(w_hi[v][:, :], raw[v][:, :], ACT.Copy).then_inc(hi_ready, 1)

            def first_block(L):
                c = Counts(BASE1, L)
                chain["n"], chain["base"] = 0, L * CHAIN_PER_LAYER
                def load_gains():
                    act.dma_start(vec[:, :], vec1[bass.ds(L, 1)].rearrange("a p n -> (a p) n")).then_inc(vec_loaded, 16)
                    act.dma_start(p_f[:, :, :], pT[bass.ds(L, 1)].rearrange("a (k p) s -> p (a k) s", p=P)).then_inc(p_loaded, 16)
                log_table()
                norm(c, "norm1", 1, lambda m: (x_ready, L * TOTAL1["X"] + (m + 1)), load_gains)

                def evac_four1(n):
                    g, t = n // ST, n % ST
                    act.wait_ge(tile_done, c.at("T", "four1", n + 1))
                    ps = bank[(c.base["four1"]["T"] + n) % 4]
                    nc.scalar.activation(Um_hi[:, t, 32 * g:32 * g + 32], ps[:, GW:UW], ACT.Copy)
                    take_hi(c, "four1", n, n, U_hi[:, g, t, :], src=lambda ps: ps[:, 0:GW])
                stage_loop(c, "four1", evac_four1)

                def evac_four2(n):
                    if n == 0:
                        take_hi(c, "four2", 0, 0, mid_hi[:, :])
                        return
                    g = n - 1
                    act.wait_ge(tile_done, c.at("T", "four2", n + 1))
                    ps = bank[(c.base["four2"]["T"] + n) % 4]
                    nc.scalar.activation(rev_hi[:, g, 0:1], ps[:, 0:1], ACT.Copy)
                    link(nc.scalar.activation(rev_hi[:, g, S - 1:0:-1], ps[:, 1:S], ACT.Copy))
                    take_hi(c, "four2", n, n, ob_hi[:, g, :])
                    if g == 0:
                        act.wait_ge(act_took, c.at("A", "four2", 1))
                    nc.scalar.activation(rev_hi[0:1, g, :], mid_hi[32 * g:32 * g + 1, :], ACT.Copy).then_inc(rev_hi_ready, 1)
                stage_loop(c, "four2", evac_four2)
                merge(c, 1, "bm")

                def evac_z1(n):
                    if n < 4:
                        if n == 0:
                            log_table()
                        squares_of_psum(c, "z1", n)
                    elif n == 5:
                        root("z1", c, 3, S, Q_LORA)
                        root("z1", c, 4, S, KV_LORA, slot=1, ps=SS_BANK2)
                        act.wait_ge(tile_done, c.at("T", "z1", 6))
                        ps = bank[(c.base["z1"]["T"] + 5) % 4]
                        nc.scalar.activation(kdup[0:64, 0, :], ps[0:64, :], ACT.Copy)
                        nc.scalar.activation(kdup[64:P, 1, :], ps[64:P, :], ACT.Copy).then_inc(act_took, 1)
                    elif n >= 6:
                        for j in range(2 * (n - 6), 2 * (n - 6) + 2):
                            split_hi(c, "qn", j, cqn_hi[:, j, :], res[:, (c.base["qn"]["R"] + j) % 4, :], (res_ready, result_value(c, "qn", j)))
                stage_loop(c, "z1", evac_z1)

                def evac_uq(n):
                    if n < 8:
                        take_hi(c, "uq", n, n, q_a[0:NOPE, n, :], src=lambda ps: ps[0:NOPE, :])
                    elif n < 12:
                        j = 2 * (n - 8)
                        take_hi(c, "uq", n, n, k_a[j // 4][0:NOPE, j % 4, :], src=lambda ps: ps[0:NOPE, :])
                    else:
                        take_hi(c, "uq", n, n, v_a[:, n - 12, 0:S // 2], src=lambda ps: ps[:, 0:S // 2])
                stage_loop(c, "uq", evac_uq)
                for b in range(ST):
                    ks = windowed(b)
                    if b == 0:
                        act.wait_ge(tile_done, c.at("T", "uq", 16))
                    act.activation(dist[:, b, 0:len(ks) * P], posf[:, ks.start * P:ks.stop * P], ACT.Abs, scale=-1.0,
                                   bias=posf[:, S + b:S + b + 1]).then_inc(dist_ready, 1)
                def evac_z1b(n):
                    if n == 2:
                        take_hi(c, "z1b", 2, 0, vcT[:, :])
                attention(c, "mla", also=lambda t: after_blocks(c, "z1b", beside("z1b", t, 1), evac_z1b))

                def gate_am(n):
                    if n % 2 == 0:
                        act.wait_ge(tile_free, c.at("T", "am", n - 2))
                        take_hi(c, "am", n, n // 2, sg[:, n // 2 % 2, :], ACT.Tanh, scale=0.5)
                attention(c, "gqa", sink=True, also=lambda t: after_blocks(c, "am", beside("am", t, 3), gate_am))
                merge(c, 1, "cm")
                project(c, "wout")
                root("wout", c, 2, S, D)
                raw_norm(c, "norm2", 1, "post1")
                gate_up(c)
                act.wait_ge(p_loaded, L * 16 + 16)
                act.activation(p_hi[:, :, :], p_f[:, :, :], ACT.Copy).then_inc(p_hi_ready, 1)
                project(c, "dn")
                root("dn", c, 2, S, D)
                for m in range(KD):
                    take_hi(c, "pp", m, m, e[:, m, :])
                    act.wait_ge(x_ready, c.at("X", "post2", m + 1) + 8)
                    nc.scalar.activation(h_hi[:, m, :], x[:, m, :], ACT.Copy).then_inc(raw_hi, 1)
                split_unit(c, "pp", 0)

                def evac_ple(n):
                    act.wait_ge(tile_free, c.at("T", "ple", n - 1))
                    take_hi(c, "ple", n, n, sg[:, n % 2, :], ACT.Sigmoid)
                    squares(c, "ple", n, e[:, n, :], (tile_free, c.at("T", "ple", n + 1)))
                stage_loop(c, "ple", evac_ple)
                root("ple", c, 2, S, D)
                assert chain["n"] <= CHAIN_PER_LAYER
                act.sem_inc(achain, CHAIN_PER_LAYER - chain["n"])

            with act.Fori(0, DEPTH) as L:
                first_block(L)

            c = Counts(BASE2, DEPTH)
            chain["n"], chain["base"] = 0, DEPTH * CHAIN_PER_LAYER
            log_table()
            norm(c, "norm1", 2, lambda m: (x_ready, DEPTH * TOTAL1["X"] + (m + 1)))
            ap4 = cst_sb[:, CST["a_param"]:CST["a_param"] + 4]
            link(nc.scalar.activation(lruc[:, 0, 0:4], ap4, ACT.Abs))
            link(nc.scalar.activation(lruc[:, 1, 0:4], lruc[:, 0, 0:4], ACT.Exp, scale=-1.0))
            link(nc.scalar.activation(lruc[:, 2, 0:4], lruc[:, 1, 0:4], ACT.Ln, bias=1.0))
            nc.scalar.activation(lruc[:, 3, 0:4], ap4, ACT.Relu, scale=-1.0).then_inc(softplus_ready, 1)

            def evac_z2(n):
                if n < 4:
                    take_hi(c, "z2", n, n, lx[:, n, :])
                elif n < 8:
                    take_hi(c, "z2", n, n, qi[:, n - 4, :])
                elif n == 9:
                    take_hi(c, "z2", n, 8, vwT[:, :])
                elif 14 <= n < 18:
                    if n == 14:
                        for j in range(4):
                            split_hi(c, "z2", j, ua_hi[:, j, :], ua[:, j, :], (res_ready, result_value(c, "z2", j)))
                    take_hi(c, "z2", n, n - 5, lg[:, n - 14, :], ACT.Gelu_apprx_tanh)
                elif n == 19:
                    for j in range(4):
                        r = c.base["z2"]["R"] + 4 + j
                        split_hi(c, "z2", 4 + j, pool_hi[:, j, :], res[:, r % 4, :], (res_ready, result_value(c, "z2", 4 + j)))
                for t in idx_items(n):
                    act.wait_ge(idx_done, t + 1)
                    if t >= 2:
                        act.wait_ge(idx_added, t - 1)
                    w = (t // 8 + 1) * P
                    nc.scalar.activation(sq[:, t % 2, 0:w], SCORES[t % 2][:, 0:w], ACT.Relu).then_inc(idx_relu, 1)
            stage_loop(c, "z2", evac_z2)

            def evac_lru(n):
                if n < 4:
                    act.wait_ge(tile_done, c.at("T", "lru", 4))
                    take_hi(c, "lru", n, n, yb_hi[:, n, :], ACT.Identity, scale=cc("pool", n))
                elif n < 8:
                    take_hi(c, "lru", n, n, lr[:, n - 4, :], ACT.Sigmoid, bias=cc("b_a", n - 4))
                else:
                    act.wait_ge(tile_done, c.at("T", "lru", 12))
                    take_hi(c, "lru", n, n, li[:, n - 8, :], ACT.Sigmoid, bias=cc("b_x", n - 8))
            stage_loop(c, "lru", evac_lru)
            act.wait_ge(softplus_ready, 2)
            for j in range(4):
                nc.scalar.activation(lm[:, j, :], lr[:, j, :], ACT.Exp, scale=lruc[:, 1, 4 + j:5 + j]).then_inc(achain, 1)
            chain["n"] += 4
            act.wait_ge(achain, chain["base"] + chain["n"])
            for j in range(4):
                nc.scalar.activation(lr[:, j, :], lr[:, j, :], ACT.Exp, scale=lruc[:, 0, 4 + j:5 + j])
            for j in range(4):
                link(nc.scalar.activation(lm[:, j, :], lm[:, j, :], ACT.Relu, scale=-1.0, bias=1.0))
            for j in range(4):
                nc.scalar.activation(lm[:, j, :], lm[:, j, :], ACT.Sqrt).then_inc(lru_gates, 1)

            def split_ya(m):
                if 1 <= m <= 4:
                    split_hi(c, "lru", m - 1, ya_hi[:, m - 1, :], ua[:, m - 1, :], (res_ready, result_value(c, "lru", m - 1)))
                if m == KD - 1:
                    act.wait_ge(tile_done, c.at("T", "bm2", 16))
                    act.dma_start(memf[:, :, :], memT.rearrange("(k p) s -> p k s", p=P)).then_inc(mem_loaded, 16)
            merge(c, 2, "bm2", 1, split_ya)

            def mem_split(j):
                split_hi(c, "normm", j, mem_hi[:, j, :], res[:, (c.base["normm"]["R"] + j) % 4, 0:N_MEM], (res_ready, result_value(c, "normm", j)))

            def norm_mem(m):
                if 1 <= m <= 4:
                    for j in range(2 * m - 2, 2 * m):
                        squares(c, "normm", j, memf[:, j, :], (mem_loaded, 16), N_MEM)
                elif m == 5:
                    root("normm", c, KD, N_MEM, D, dst=mem_rstd[:, :])
                elif m == 6:
                    for j in range(4):
                        mem_split(j)
            merge(c, 2, "am", 0, norm_mem)
            for j in range(4, KD):
                mem_split(j)

            def evac_mem(t):
                after_blocks(c, "mk", beside("mk", t, 2), lambda n: take_hi(c, "mk", n, n, mk[:, n, :], src=lambda ps: ps[:, 0:N_MEM]))
                if t in (27, 31):
                    rows = (t - 27) // 4
                    take_hi(c, "mv", rows, rows, mv[:, rows, :])
                if t in (23, 31):
                    split_unit(c, "mv", (t - 23) // 8)
            attention(c, "dsa", also=evac_mem)
            merge(c, 2, "cm", 2)
            project(c, "wout")
            root("wout", c, 2, S, D)
            raw_norm(c, "normh", 2, "post1")
            stage_loop(c, "mq", lambda n: None)
            attention(c, "mem")
            project(c, "mo")
            root("mo", c, 2, S, D)
            raw_norm(c, "norm2", 2, "postm")
            gate_up(c)
            project(c, "dn")
            root("dn", c, 2, S, D)
            for m in range(KD):
                act.wait_ge(x_ready, c.at("X", "post2", m + 1) + 8)
                act.dma_start(out[m * P:(m + 1) * P, :], x[:, m, :]).then_inc(out_done, 16)
            act.wait_ge(out_done, 16 * KD)

        @block.vector
        def _(dve):
            chain = {"n": 0, "base": 0}

            def link(ins):
                chain["n"] += 1
                ins.then_inc(vchain, 1)
                dve.wait_ge(vchain, chain["base"] + chain["n"])

            def split_unit(c, st, u):
                v = c.base[st]["U"] + u + 2
                if c.base is BASE2 and v >= TOTAL2["U"]:
                    return
                dve.wait_ge(hi_ready, c.at("U", st, u + 3))
                low_part(v % 2)

            def low_part(s):
                nc.vector.tensor_tensor(w_lo[s][:, :], raw[s][:, :], w_hi[s][:, :].bitcast(F32), ALU.subtract).then_inc(lo_ready, 1)

            def stage_loop(c, st, evac):
                unit_steps(st, evac, lambda u: split_unit(c, st, u))

            def ps_of(c, st, n):
                return bank[(c.base[st]["T"] + n) % 4]

            def take_lo(c, st, n, a, dst, hi, width=S):
                dve.wait_ge(act_took, c.at("A", st, a + 1))
                nc.vector.tensor_tensor(dst, ps_of(c, st, n)[:, 0:width], hi.bitcast(F32), ALU.subtract).then_inc(tile_free, 1)

            def copy_out(c, st, n, a, dst, src, wait_act=True):
                if wait_act:
                    dve.wait_ge(act_took, c.at("A", st, a + 1))
                else:
                    dve.wait_ge(tile_done, c.at("T", st, n + 1))
                nc.vector.tensor_copy(dst, src(ps_of(c, st, n))).then_inc(tile_free, 1)

            def pass_on(c, st, n):
                dve.wait_ge(tile_free, c.at("T", st, n))
                dve.sem_inc(tile_free, 1)


            def result_slot(c, st, m):
                r = c.base[st]["R"] + m
                if r >= 4 or c.base is BASE2:
                    dve.wait_ge(res_split, c.at("R", st, m - 3))
                return res[:, r % 4, :]

            def norm(c, st, which):
                gain, src, _, _, width = NORMS[which][st]
                g = vv if which == 1 else cc
                dve.wait_ge(rms_ready, c.at("N", st, 1))
                for m in range(KD):
                    dst = result_slot(c, st, m)
                    nc.vector.scalar_tensor_tensor(out=dst[:, 0:width], in0=src[:, m, :], scalar=g(gain, m),
                                                   in1=rstd[:, 0, 0:width], op0=ALU.mult, op1=ALU.mult).then_inc(res_ready, 1)

            def post(c, st, which, gain, src, also=None, lo=None, lo_now=KD):
                g = vv if which == 1 else cc
                dve.wait_ge(rms_ready, c.at("N", st, 1))
                for m in range(KD + 2):
                    if m < KD:
                        if m >= 2:
                            dve.wait_ge(x_ready, c.at("X", st, m - 1) + 8)
                        nc.vector.scalar_tensor_tensor(out=sg[:, m % 2, :], in0=src[:, m, :], scalar=g(gain, m),
                                                       in1=rstd[:, 0, :], op0=ALU.mult, op1=ALU.mult).then_inc(post_ready, 1)
                    if also is not None:
                        also(m)
                    if lo is not None and 0 <= m - 2 < lo_now:
                        lo(m - 2)
                if lo is not None:
                    for m in range(lo_now, KD):
                        lo(m)

            def raw_lo(c, st, which, m):
                g = (vv if which == 1 else cc)(RAW_NORMS[which, st], m)
                dve.wait_ge(raw_hi, c.at("W", st, m + 1))
                nc.vector.scalar_tensor_tensor(out=h_lo[:, m, :], in0=x[:, m, :], scalar=g, in1=h_hi[:, m, :].bitcast(F32),
                                               op0=ALU.mult, op1=ALU.subtract).then_inc(raw_split, 1)

            def add_squares(c, st):
                dve.wait_ge(sq_ready, c.at("SQ", st, KD))
                link(nc.vector.tensor_tensor(sq8[:, 0:4, :], sq8[:, 0:4, :], sq8[:, 4:8, :], ALU.add))
                nc.vector.tensor_tensor(sq8[:, 0:2, :], sq8[:, 0:2, :], sq8[:, 2:4, :], ALU.add).then_inc(sq_tree, 1)

            def merge(c, which, st, order, extra=None):
                merged = MERGED[which][0]

                def evac(n):
                    if n % 2 == 0:
                        return
                    m = n // 2
                    dve.wait_ge(act_took, c.at("A", st, m + 1))
                    dve.wait_ge(tile_done, c.at("T", st, n + 1))
                    ps = ps_of(c, st, n)
                    if order == 0:
                        nc.vector.tensor_tensor(merged[:, m, :], ps[:, :], sg[:, m % 2, :], ALU.mult).then_inc(tile_free, 2)
                    else:
                        r = rstd[:, m % 2, :]
                        nc.vector.tensor_tensor(r, ps[:, :], sg[:, m % 2, :], ALU.mult).then_inc(tile_free, 2)
                        dve.wait_ge(tile_free, c.at("T", st, n + 1))
                        if order == 1:
                            link(nc.vector.tensor_tensor(merged[:, m, :], merged[:, m, :], r, ALU.add))
                        else:
                            dst = result_slot(c, st, m)
                            nc.vector.tensor_tensor(dst, merged[:, m, :], r, ALU.add).then_inc(res_ready, 1)
                    if extra is not None:
                        extra(m)
                stage_loop(c, st, evac)

            def after_blocks(c, st, t, per, evac):
                for b in beside(st, t - 1, per) if t >= 1 else ():
                    for n, tile in enumerate(TILES[st]):
                        if tile[-1] == b:
                            evac(n)
                for b in beside(st, t - 2, per) if t >= 2 else ():
                    if b % BLK == BLK - 1 or b == TILES[st][-1][-1]:
                        split_unit(c, st, b // BLK)

            def attention(c, st, bias=None, sink=False, also=None):
                a = ATT[st]
                items = [(h, b) for h in range(a["heads"]) for b in range(ST)]
                taken = 0
                for t in range(len(items) + 2):
                    if t < len(items):
                        h, b = items[t]
                        n = len(a["keys"](b)) * P
                        dve.wait_ge(logits_done, c.at("I", st, t + 1))
                        src = SCORES[t % 2]
                        if a["biased"]:
                            if t >= 4:
                                dve.wait_ge(turned, c.at("I", st, t - 3))
                            src = a["prob"][t % 4]
                            tile, factor = bias(h, b)
                            link(nc.vector.scalar_tensor_tensor(out=src[:, 0:n], in0=tile, scalar=factor, in1=SCORES[t % 2][:, 0:n],
                                                                op0=ALU.mult, op1=ALU.add))
                        link(nc.vector.reduce_max(st_max[:, t:t + 1], src[:, 0:n], AX_X))
                        if sink:
                            link(nc.vector.tensor_scalar(st_neg[:, t:t + 1], st_max[:, t:t + 1], a["scale"], vv("sink", h), ALU.mult, ALU.max))
                            nc.vector.tensor_scalar(st_neg[:, t:t + 1], st_neg[:, t:t + 1], -1.0, None, ALU.mult).then_inc(shift_ready, 1)
                        else:
                            nc.vector.tensor_scalar(st_neg[:, t:t + 1], st_max[:, t:t + 1], -a["scale"], None, ALU.mult).then_inc(shift_ready, 1)
                    if 1 <= t <= len(items):
                        i = t - 1
                        h, b = items[i]
                        n = len(a["keys"](b)) * P
                        dve.wait_ge(exp_done, c.at("I", st, i + 1))
                        if sink:
                            link(nc.vector.tensor_tensor(st_sum[:, i:i + 1], st_sum[:, i:i + 1], st_snk[:, i:i + 1], ALU.add))
                        link(nc.vector.reciprocal(st_rec[:, i:i + 1], st_sum[:, i:i + 1]))
                        p = a["prob"][i % 4]
                        nc.vector.tensor_scalar(p[:, 0:n], p[:, 0:n], st_rec[:, i:i + 1], None, ALU.mult).then_inc(prob_ready, 1)
                        if b == 2 and h >= 2 and (h + 1) % a["per_tile"] == 0 and (h + 1) // a["per_tile"] >= 2:
                            done = (h - 1) // a["per_tile"]
                            while taken < done:
                                output_lo(c, st, taken)
                                taken += 1
                    if also is not None:
                        also(t)
                while taken < a["heads"] // a["per_tile"]:
                    output_lo(c, st, taken)
                    taken += 1

            def output_lo(c, st, i):
                hi, lo = ATT[st]["o"](i)
                dve.wait_ge(o_hi_ready, c.at("O", st, i + 1))
                nc.vector.tensor_tensor(lo, VALUES[:, :], hi.bitcast(F32), ALU.subtract).then_inc(o_split, 1)

            def gate_up(c):
                st = "gu"
                t0, u0 = c.base[st]["T"], c.base[st]["U"]
                with dve.Fori(0, KF // 2) as i:
                    for p in range(2):
                        if p == 0:
                            dve.wait_ge(rms_ready, c.at("N", "norm2", 1))
                        dve.wait_ge(tile_done, c.at("T", st, 2 * p + 1) + i * 4)
                        dve.wait_ge(lo_ready, c.at("U", st, p + 1) + i * 2)
                        nc.vector.tensor_tensor(sg[:, p, :], bank[(t0 + 2 * p) % 4][:, :], rstd[:, 0, :], ALU.mult).then_inc(tile_free, 1)
                        dve.wait_ge(tile_done, c.at("T", st, 2 * p + 2) + i * 4)
                        dve.wait_ge(res_split, c.at("R", st, p - 1) + i * 2)
                        nc.vector.tensor_tensor(res[:, p, :], bank[(t0 + 2 * p + 1) % 4][:, :], rstd[:, 0, :], ALU.mult).then_inc(tile_free, 1)
                        dve.wait_ge(tile_free, c.at("T", st, 2 * p + 2) + i * 4)
                        dve.wait_ge(act_took, c.at("A", st, p + 1) + i * 2)
                        nc.vector.tensor_tensor(res[:, p, :], res[:, p, :], sg[:, p, :], ALU.mult).then_inc(gated, 1)
                        dve.wait_ge(hi_ready, c.at("U", st, p + 3) + i * 2)
                        low_part((u0 + p) % 2)

            def project(c, st):
                stage_loop(c, st, lambda n: copy_out(c, st, n, n, y[:, n, :], lambda ps: ps[:, :]))

            def rotate(ps, dst, last):
                link(nc.vector.tensor_tensor(rope_t[0][64:96, :], ps[64:96, :], cs[64:96, :], ALU.mult))
                link(nc.vector.tensor_tensor(rope_t[1][64:96, :], ps[96:P, :], cs[96:P, :], ALU.mult))
                link(nc.vector.tensor_tensor(dst, rope_t[0][64:96, :], rope_t[1][64:96, :], ALU.add))

            dve.wait_ge(cst_loaded, 16)
            dve.wait_ge(pos_loaded, 16)
            link(nc.vector.tensor_copy(posf[:, :], pos_i[:, :]))
            r = slice(64, P)
            link(nc.vector.tensor_scalar(ang[0][r, :], posf[r, 0:S], cc("freq", 0, 64), None, ALU.mult))
            link(nc.vector.tensor_scalar(ang[1][r, :], ang[0][r, :], cc("phase", 0, 64), float(1 / (2 * np.pi)), ALU.add, ALU.mult))
            link(nc.vector.tensor_scalar(ang[1][r, :], ang[1][r, :], ROUND, None, ALU.add))
            link(nc.vector.tensor_scalar(ang[1][r, :], ang[1][r, :], -ROUND, None, ALU.add))
            link(nc.vector.scalar_tensor_tensor(out=ang[0][r, :], in0=ang[1][r, :], scalar=-TWO_PI_A, in1=ang[0][r, :], op0=ALU.mult, op1=ALU.add))
            link(nc.vector.scalar_tensor_tensor(out=ang[0][r, :], in0=ang[1][r, :], scalar=-TWO_PI_B, in1=ang[0][r, :], op0=ALU.mult, op1=ALU.add))
            link(nc.vector.scalar_tensor_tensor(out=ang[0][r, :], in0=ang[1][r, :], scalar=-float(TWO_PI_C), in1=ang[0][r, :], op0=ALU.mult, op1=ALU.add))
            link(nc.vector.tensor_scalar(ang[2][r, :], ang[0][r, :], cc("phase", 0, 64), 3.1415925, ALU.add, ALU.min))
            nc.vector.tensor_scalar(ang[2][r, :], ang[2][r, :], -3.1415925, None, ALU.max).then_inc(angle_ready, 1)
            dve.wait_ge(sin_ready, 1)
            link(nc.vector.tensor_scalar(cs[r, :], cs[r, :], cc("sign", 0, 64), None, ALU.mult))
            for v in range(2):
                dve.wait_ge(hi_ready, v + 1)
                low_part(v)
            start_steps = chain["n"]

            def first_block(L):
                c = Counts(BASE1, L)
                chain["n"], chain["base"] = 0, L * CHAIN_PER_LAYER + start_steps
                dve.wait_ge(vec_loaded, L * 16 + 16)
                norm(c, "norm1", 1)

                def evac_four1(n):
                    g, t = n // ST, n % ST
                    m = slice(32 * g, 32 * g + 32)
                    dve.wait_ge(act_took, c.at("A", "four1", n + 1))
                    nc.vector.tensor_tensor(Um_lo[:, t, m], ps_of(c, "four1", n)[:, GW:UW], Um_hi[:, t, m].bitcast(F32), ALU.subtract)
                    take_lo(c, "four1", n, n, U_lo[:, g, t, :], U_hi[:, g, t, :], GW)
                stage_loop(c, "four1", evac_four1)

                def evac_four2(n):
                    if n == 0:
                        take_lo(c, "four2", 0, 0, mid_lo[:, :], mid_hi[:, :])
                        return
                    g = n - 1
                    take_lo(c, "four2", n, n, ob_lo[:, g, :], ob_hi[:, g, :])
                    dve.wait_ge(tile_free, c.at("T", "four2", n + 1))
                    nc.vector.tensor_copy(rev_lo[:, g, 0:1], ob_lo[:, g, 0:1])
                    link(nc.vector.tensor_copy(rev_lo[:, g, S - 1:0:-1], ob_lo[:, g, 1:S]))
                    dve.wait_ge(rev_hi_ready, c.layer * GROUPS + (g + 1))
                    nc.vector.tensor_copy(rev_lo[0:1, g, :], mid_lo[32 * g:32 * g + 1, :]).then_inc(rev_ready, 1)
                stage_loop(c, "four2", evac_four2)
                merge(c, 1, "bm", 0)

                def evac_z1(n):
                    if n < 4:
                        copy_out(c, "z1", n, n, cq[:, n, :], lambda ps: ps[:, :])
                    elif n == 4:
                        dve.wait_ge(tile_done, c.at("T", "z1", 5))
                        rotate(ps_of(c, "z1", 4), kr[64:96, :], None)
                        pass_on(c, "z1", 4)
                        for hd in range(MLA_HEADS):
                            ins = nc.vector.tensor_copy(k_a[hd // 4][64:96, hd % 4, :], kr[64:96, :])
                        ins.then_inc(kr_copied, 1)
                    elif n == 5:
                        dve.wait_ge(act_took, c.at("A", "z1", 5))
                        ps = ps_of(c, "z1", 5)
                        nc.vector.tensor_copy(kdup[64:P, 0, :], ps[0:64, :])
                        nc.vector.tensor_copy(kdup[0:64, 1, :], ps[64:P, :]).then_inc(tile_free, 1)
                    else:
                        copy_out(c, "z1", n, n, qc[:, n - 6, :], lambda ps: ps[:, :], wait_act=False)
                        for j in range(2 * (n - 6), 2 * (n - 6) + 2):
                            if j in (0, 3):
                                dve.wait_ge(rms_ready, c.at("N", "qn", 1 + j // 3))
                            dst = result_slot(c, "qn", j)
                            nc.vector.scalar_tensor_tensor(out=dst, in0=cq[:, j, :], scalar=vv("q_norm", j) if j < 3 else vv("kv_norm"),
                                                           in1=rstd[:, j // 3, :], op0=ALU.mult, op1=ALU.mult).then_inc(res_ready, 1)
                stage_loop(c, "z1", evac_z1)

                def evac_uq(n):
                    if n < 8:
                        dve.wait_ge(act_took, c.at("A", "uq", n + 1))
                        rotate(ps_of(c, "uq", n), q_a[64:96, n, :], None)
                        pass_on(c, "uq", n)
                    elif n < 12:
                        j = 2 * (n - 8) + 1
                        copy_out(c, "uq", n, n, k_a[j // 4][0:NOPE, j % 4, :], lambda ps: ps[64:P, :])
                    else:
                        copy_out(c, "uq", n, n, v_a[:, n - 12, S // 2:S], lambda ps: ps[:, S // 2:S])
                stage_loop(c, "uq", evac_uq)
                for b in range(ST):
                    n = len(windowed(b)) * P
                    off = P if b == 0 else 0
                    dve.wait_ge(dist_ready, L * ST + (b + 1))
                    link(nc.vector.tensor_tensor(dist[:, b, 0:n], dist[:, b, 0:n], cst_sb[:, CST["window"] + off:CST["window"] + off + n], ALU.add))
                def evac_z1b(n):
                    if n < 2:
                        copy_out(c, "z1b", n, 0, qc[:, 2 + n, :], lambda ps: ps[:, :], wait_act=False)
                    else:
                        dve.wait_ge(act_took, c.at("A", "z1b", 1))
                        pass_on(c, "z1b", 2)
                attention(c, "mla", also=lambda t: after_blocks(c, "z1b", t, 1, evac_z1b))
                copy_out(c, "z1b", 3, 0, vc[:, :, :], lambda ps: ps[:, :].rearrange("p (t d) -> p t d", t=ST), wait_act=False)

                def alibi(h, b):
                    return dist[:, b, 0:len(windowed(b)) * P], -(2.0 ** (-8.0 * (h + 1) / HEADS)) * HD ** 0.5
                def add_am(n):
                    if n % 2 == 1:
                        m = n // 2
                        r = rstd[:, m % 2, :]
                        dve.wait_ge(act_took, c.at("A", "am", m + 1))
                        dve.wait_ge(tile_done, c.at("T", "am", n + 1))
                        nc.vector.scalar_tensor_tensor(out=r, in0=sg[:, m % 2, :], scalar=1.0, in1=ps_of(c, "am", n)[:, :],
                                                       op0=ALU.add, op1=ALU.mult).then_inc(tile_free, 2)
                        dve.wait_ge(tile_free, c.at("T", "am", n + 1))
                        link(nc.vector.scalar_tensor_tensor(out=merged1[:, m, :], in0=r, scalar=0.5, in1=merged1[:, m, :],
                                                            op0=ALU.mult, op1=ALU.add))
                attention(c, "gqa", alibi, sink=True, also=lambda t: after_blocks(c, "am", t, 3, add_am))
                merge(c, 1, "cm", 2)
                project(c, "wout")
                post(c, "post1", 1, "mix_post", y, lo=lambda m: raw_lo(c, "norm2", 1, m))
                add_squares(c, "norm2")
                gate_up(c)
                project(c, "dn")
                def free_pp(m):
                    for n in range(m - 2, m) if m in (2, 4, 6, 8) else ():
                        dve.wait_ge(act_took, c.at("A", "pp", n + 1))
                        pass_on(c, "pp", n)

                def x_lo(m):
                    dve.wait_ge(raw_hi, c.at("W", "xple", m + 1))
                    if m == 4:
                        dve.wait_ge(tile_done, c.at("T", "pp", 8))
                    nc.vector.tensor_tensor(h_lo[:, m, :], x[:, m, :], h_hi[:, m, :].bitcast(F32), ALU.subtract).then_inc(raw_split, 1)
                post(c, "post2", 1, "ffn_post", y, free_pp, x_lo, 4)
                split_unit(c, "pp", 0)

                def evac_ple(n):
                    dve.wait_ge(act_took, c.at("A", "ple", n + 1))
                    dve.wait_ge(tile_free, c.at("T", "ple", n))
                    nc.vector.tensor_tensor(e[:, n, :], e[:, n, :], sg[:, n % 2, :], ALU.mult).then_inc(tile_free, 1)
                stage_loop(c, "ple", evac_ple)
                dve.wait_ge(tile_free, c.at("T", "ple", KD))
                dve.sem_inc(tile_free, NO_TILES)
                post(c, "post3", 1, "ple", e)
                assert chain["n"] <= CHAIN_PER_LAYER
                dve.sem_inc(vchain, CHAIN_PER_LAYER - chain["n"])

            with dve.Fori(0, DEPTH) as L:
                first_block(L)

            c = Counts(BASE2, DEPTH)
            chain["n"], chain["base"] = 0, DEPTH * CHAIN_PER_LAYER + start_steps
            norm(c, "norm1", 2)
            dve.wait_ge(softplus_ready, 1)
            link(nc.vector.tensor_tensor(lruc[:, 2, 4:8], lruc[:, 2, 0:4], lruc[:, 3, 0:4], ALU.add))
            link(nc.vector.tensor_scalar(lruc[:, 0, 4:8], lruc[:, 2, 4:8], -8.0, None, ALU.mult))
            nc.vector.tensor_scalar(lruc[:, 1, 4:8], lruc[:, 2, 4:8], -16.0, None, ALU.mult).then_inc(softplus_ready, 1)

            def conv(j):
                link(nc.vector.tensor_scalar(ua[:, j, :], lx[:, j, :], cc("conv_w", 12 + j), cc("conv_b", j), ALU.mult, ALU.add))
                for back in range(1, 4):
                    ins = nc.vector.scalar_tensor_tensor(out=ua[:, j, back:S], in0=lx[:, j, 0:S - back], scalar=cc("conv_w", 4 * (3 - back) + j),
                                                         in1=ua[:, j, back:S], op0=ALU.mult, op1=ALU.add)
                    if back < 3:
                        link(ins)
                    else:
                        ins.then_inc(res_ready, 1)

            def pool(g):
                src, lo = pz[:, g, :], 1
                for lev in range(g + 1):
                    back = 1 << lev
                    dst = win[lev % 2]
                    link(nc.vector.tensor_tensor(dst[:, lo:PADW + S], src[:, lo:PADW + S], src[:, lo - back:PADW + S - back], ALU.add))
                    src = dst[:, :]
                    lo += 2 * back
                link(nc.vector.tensor_tensor(src[:, PADW:PADW + 16], src[:, PADW:PADW + 16],
                                             cst_sb[:, CST["head"] + 16 * g:CST["head"] + 16 * g + 16], ALU.mult))
                dst = result_slot(c, "z2", 4 + g)
                nc.vector.scalar_tensor_tensor(out=dst, in0=src[:, PADW:PADW + S], scalar=1.0 / POOL_W[g], in1=pz[:, g, PADW:PADW + S],
                                               op0=ALU.mult, op1=ALU.subtract).then_inc(res_ready, 1)
                dve.wait_ge(res_ready, result_value(c, "z2", 4 + g))

            def add_idx(t):
                b, hh = t // 8, t % 8
                w = (b + 1) * P
                dve.wait_ge(idx_relu, t + 1)
                if t == 0:
                    dve.wait_ge(res_ready, result_value(c, "z2", 3))
                if hh == 0:
                    ins = nc.vector.tensor_scalar(score[:, b, 0:w], sq[:, t % 2, 0:w], wsc[:, b, hh:hh + 1], None, ALU.mult)
                else:
                    dve.wait_ge(idx_added, t)
                    ins = nc.vector.scalar_tensor_tensor(out=score[:, b, 0:w], in0=sq[:, t % 2, 0:w], scalar=wsc[:, b, hh:hh + 1],
                                                         in1=score[:, b, 0:w], op0=ALU.mult, op1=ALU.add)
                ins.then_inc(idx_added, 1)

            def hide(b):
                if b == 0:
                    link(nc.vector.memset(score[:, 0, 0:P], 0.0))
                    link(nc.vector.memset(score[0:64, 0, 64:P], MASKED))
                else:
                    link(nc.vector.memset(score[0:64, b, b * P + 64:(b + 1) * P], NEG))

            def take_top8(b):
                w = (b + 1) * P
                link(nc.vector.max(top8[:, :], score[:, b, 0:w]))
                link(nc.vector.match_replace(out=score[:, b, 0:w], in_to_replace=top8[:, :], in_values=score[:, b, 0:w], imm_value=TAKEN))

            rounds = [b for b in range(1, ST) for _ in range(TOPK // 8)]

            A_Z2 = {n: n for n in range(8)} | {9: 8} | {n: n - 5 for n in range(14, 18)}

            def evac_z2(n):
                if n in A_Z2:
                    dve.wait_ge(act_took, c.at("A", "z2", A_Z2[n] + 1))
                    pass_on(c, "z2", n)
                    if 4 <= n < 8:
                        conv(n - 4)
                    elif n >= 14:
                        if n == 14:
                            dve.wait_ge(tile_free, c.at("T", "z2", 14))
                        pool(n - 14)
                elif 10 <= n < 14:
                    if n == 10:
                        dve.wait_ge(pad_ready, 1)
                    copy_out(c, "z2", n, 0, pz[:, n - 10, PADW:PADW + S], lambda ps: ps[:, :], wait_act=False)
                    if n == 10:
                        dve.wait_ge(vw_turned, 1)
                        link(nc.vector.tensor_copy(vw[:, :, :], TURNED[:, :].rearrange("p (t d) -> p t d", t=ST)))
                        link(nc.vector.tensor_scalar(wsc[:, :, :], vw[:, :, HD:HD + 8], 8 ** -0.5, None, ALU.mult))
                else:
                    dst = {8: ki, 22: kk}.get(n)
                    copy_out(c, "z2", n, 0, qd[:, n - 18, :] if dst is None else dst[:, :], lambda ps: ps[:, :], wait_act=False)
                for t in idx_items(n):
                    add_idx(t)
                if n >= 18:
                    if n == 18:
                        dve.wait_ge(idx_added, 16)
                        hide(1)
                    take_top8(rounds[n - 18])
            stage_loop(c, "z2", evac_z2)
            def evac_lru(n):
                dve.wait_ge(act_took, c.at("A", "lru", n + 1))
                if n < 4:
                    nc.vector.scalar_tensor_tensor(out=yb_lo[:, n, :], in0=ps_of(c, "lru", n)[:, :], scalar=cc("pool", n),
                                                   in1=yb_hi[:, n, :].bitcast(F32), op0=ALU.mult, op1=ALU.subtract).then_inc(tile_free, 1)
                else:
                    pass_on(c, "lru", n)
            stage_loop(c, "lru", evac_lru)

            def recur(j):
                link(nc.vector.tensor_tensor(li[:, j, :], li[:, j, :], ua[:, j, :], ALU.mult))
                dve.wait_ge(lru_gates, j + 1)
                link(nc.vector.tensor_tensor(li[:, j, :], li[:, j, :], lm[:, j, :], ALU.mult))
                link(nc.vector.tensor_tensor_scan(ua[:, j, :], lr[:, j, :], li[:, j, :], 0.0, ALU.mult, ALU.add))
                nc.vector.tensor_tensor(ua[:, j, :], ua[:, j, :], lg[:, j, :], ALU.mult).then_inc(res_ready, 1)
            dve.wait_ge(idx_added, IDX_ITEMS)
            for b in (0, 2, 3):
                hide(b)

            def leave_out(b):
                w = (b + 1) * P
                link(nc.vector.tensor_scalar(score[:, b, 0:w], score[:, b, 0:w], 0.5 * (NEG + TAKEN), MASKED, ALU.is_gt, ALU.mult))

            def some_rounds(at):
                for i in range(at + 5, min(at + 9, len(rounds))):
                    take_top8(rounds[i])
                    if i == len(rounds) - 1 or rounds[i + 1] != rounds[i]:
                        leave_out(rounds[i])
            merge(c, 2, "bm2", 0, extra=lambda m: recur(m) if m < 4 else some_rounds(4 * m - 16))

            def am_extra(m):
                some_rounds(4 * m + 16)
                if m >= 6:
                    if m == 6:
                        dve.wait_ge(rms_ready, c.at("N", "normm", 1))
                    for j in range(4 * m - 24, 4 * m - 20):
                        dst = result_slot(c, "normm", j)
                        nc.vector.scalar_tensor_tensor(out=dst[:, 0:N_MEM], in0=memf[:, j, :], scalar=cc("mem_kv", j), in1=mem_rstd[:, :],
                                                       op0=ALU.mult, op1=ALU.mult).then_inc(res_ready, 1)
            merge(c, 2, "am", 1, extra=am_extra)
            dve.wait_ge(res_ready, result_value(c, "normm", KD - 1))

            def evac_mem(t):
                def left(st, n, a):
                    dve.wait_ge(act_took, c.at("A", st, a + 1))
                    pass_on(c, st, n)
                after_blocks(c, "mk", t, 2, lambda n: left("mk", n, n))
                if t in (28, 32):
                    left("mv", (t - 28) // 4, (t - 28) // 4)
                if t in (25, 33):
                    split_unit(c, "mv", (t - 25) // 8)
            attention(c, "dsa", lambda h, b: (score[:, b, 0:(b + 1) * P], 1.0), also=evac_mem)
            merge(c, 2, "cm", 2)
            project(c, "wout")
            post(c, "post1", 2, "mix_post", y, lo=lambda m: raw_lo(c, "normh", 2, m))
            add_squares(c, "normh")

            def norm_mq(n):
                if n == 0:
                    dve.wait_ge(rms_ready, c.at("N", "normh", 1))
                dve.wait_ge(tile_done, c.at("T", "mq", n + 1))
                nc.vector.tensor_tensor(mq[:, n, :], ps_of(c, "mq", n)[:, :], rstd[:, 0, :], ALU.mult).then_inc(tile_free, 1)
            stage_loop(c, "mq", norm_mq)
            attention(c, "mem")
            project(c, "mo")
            post(c, "postm", 2, "mem_post", y, lo=lambda m: raw_lo(c, "norm2", 2, m))
            add_squares(c, "norm2")
            gate_up(c)
            project(c, "dn")
            post(c, "post2", 2, "ffn_post", y)

        @block.gpsimd
        def _(pool):
            def split_lo(c, st, m, dst, src, hi):
                pool.wait_ge(res_hi, c.at("R", st, m + 1))
                nc.gpsimd.tensor_tensor(dst, src, hi.bitcast(F32), ALU.subtract).then_inc(res_split, 1)

            def norm(c, st, which):
                _, _, hi, lo, width = NORMS[which][st]
                for m in range(KD):
                    r = c.base[st]["R"] + m
                    split_lo(c, st, m, lo[:, m, :], res[:, r % 4, 0:width], hi[:, m, :])

            def merged_lo(c, which):
                _, hi, lo = MERGED[which]
                for m in range(KD):
                    r = c.base["cm"]["R"] + m
                    split_lo(c, "cm", m, lo[:, m, :], res[:, r % 4, :], hi[:, m, :])

            def gate_up(c):
                with pool.Fori(0, KF // 2) as i:
                    for p in range(2):
                        pool.wait_ge(res_hi, c.at("R", "gu", p + 1) + i * 2)
                        nc.gpsimd.tensor_tensor(a_lo[:, bass.ds(i * 2 + p, 1), :].rearrange("p a s -> p (a s)"), res[:, p, :],
                                                a_hi[:, bass.ds(i * 2 + p, 1), :].rearrange("p a s -> p (a s)").bitcast(F32),
                                                ALU.subtract).then_inc(res_split, 1)

            def add_squares(c, st, ready, kind):
                for j in range(1, KD - 1):
                    pool.wait_ge(ready, c.at(kind, st, j + 1))
                    if j >= 2:
                        pool.wait_ge(sq_added, c.at("AD", st, j - 1))
                    nc.gpsimd.tensor_tensor(sq_acc, sq[:, 0, :] if j == 1 else sq_acc, sq[:, j % 2, :], ALU.add).then_inc(sq_added, 1)

            def add_to_x(c, st):
                for m in range(KD):
                    pool.wait_ge(post_ready, c.at("X", st, m + 1))
                    nc.gpsimd.tensor_tensor(x[:, m, :], x[:, m, :], sg[:, m % 2, :], ALU.add).then_inc(x_ready, 1)

            pool.wait_ge(x_loaded, 16)
            pool.sem_inc(x_ready, 8)
            with pool.Fori(0, DEPTH) as L:
                c = Counts(BASE1, L)
                norm(c, "norm1", 1)
                for j in range(4):
                    r = c.base["qn"]["R"] + j
                    split_lo(c, "qn", j, cqn_lo[:, j, :], res[:, r % 4, :], cqn_hi[:, j, :])
                merged_lo(c, 1)
                add_squares(c, "wout", act_took, "A")
                add_to_x(c, "post1")
                gate_up(c)
                pool.wait_ge(p_hi_ready, L + 1)
                nc.gpsimd.tensor_tensor(p_lo[:, :, :], p_f[:, :, :], p_hi[:, :, :].bitcast(F32), ALU.subtract).then_inc(p_split, 1)
                add_squares(c, "dn", act_took, "A")
                add_to_x(c, "post2")
                add_squares(c, "ple", sq_ready, "SQ")
                add_to_x(c, "post3")

            c = Counts(BASE2, DEPTH)
            norm(c, "norm1", 2)
            nc.gpsimd.memset(pz[:, :, 0:PADW], 0.0).then_inc(pad_ready, 1)
            for j in range(4):
                split_lo(c, "z2", j, ua_lo[:, j, :], ua[:, j, :], ua_hi[:, j, :])
            for j in range(4):
                r = c.base["z2"]["R"] + 4 + j
                split_lo(c, "z2", 4 + j, pool_lo[:, j, :], res[:, r % 4, :], pool_hi[:, j, :])
            for j in range(4):
                split_lo(c, "lru", j, ya_lo[:, j, :], ua[:, j, :], ya_hi[:, j, :])
            norm(c, "normm", 2)
            merged_lo(c, 2)
            add_squares(c, "wout", act_took, "A")
            add_to_x(c, "post1")
            add_squares(c, "mo", act_took, "A")
            add_to_x(c, "postm")
            gate_up(c)
            add_squares(c, "dn", act_took, "A")
            add_to_x(c, "post2")


def lay_out(inputs):
    f32 = np.float32
    stream = np.zeros((UNITS_PADDED, P, UC), f32)
    at = [0]

    def put(blocks):
        for i, b in enumerate(blocks):
            if b is not None:
                j = i % BLK
                stream[at[0] + i // BLK, :, j * P:(j + 1) * P] = b
        at[0] += -(-len(blocks) // BLK)

    def cut(w, k, lo, n=P):
        return w[k * P:(k + 1) * P, lo:lo + n]

    def column(w, lo, k=KD):
        return [cut(w, j, lo) for j in range(k)]

    def merge(w_in, gate, w, k):
        out = []
        for m in range(KD):
            out += column(w_in, gate + m * P) + column(w, m * P, k)
        return out

    def ffn(gate, up, down):
        out = []
        for m in range(KF):
            out += column(gate, m * P) + column(up, m * P)
        put(out)
        out = []
        for pair in range(KD // 2):
            for part in range(3):
                for q in range(2):
                    for k in range(8 * part, 8 * part + 8):
                        out.append(cut(down, k, (2 * pair + q) * P) if k < KF else None)
        put(out)

    def by_column(w):
        out = []
        for m in range(KD):
            out += column(w, m * P, w.shape[0] // P)
        return out

    ch = np.arange(GW)
    ang = 2 * np.pi * ((ch[:, None] * ch[None, :]) % GW) / GW
    chan = np.concatenate([np.cos(ang)[:, 0:GH], np.sin(ang)[:, 0:GH], np.cos(ang)[:, GH:GH + 1], np.zeros((GW, GW - 1))], axis=1).astype(f32)
    tk = np.arange(S)
    ang = 2 * np.pi * ((tk[:, None] * tk[None, :]) % S) / S
    norm = 1 / np.sqrt(S * GW)
    tok_cos, tok_sin = (np.cos(ang) * norm).astype(f32), (-np.sin(ang) * norm).astype(f32)

    def wide(w, rows):
        return [cut(w, t, n * P) for t in rows for n in range(w.shape[1] // P)]

    for i in range(DEPTH):
        w_in = inputs["w_in"][i]
        put(wide(chan, range(2)))
        put(wide(tok_cos, range(ST)))
        put(wide(tok_sin, range(ST)))
        at_gate = Q_LORA + KV_LORA + ROPE + HEADS * HD + 2 * KV_HEADS * HD
        at_rope = Q_LORA + KV_LORA
        at_qc = at_rope + ROPE
        at_kc = at_qc + HEADS * HD
        at_vc = at_kc + KV_HEADS * HD
        group = np.arange(GROUPS)[:, None] * GW
        first, rest = np.arange(GH), np.concatenate([[GH], np.arange(GW - 1, GH, -1)])
        rows = np.concatenate([(group + first).ravel(), (group + rest).ravel()])
        put(merge(w_in, at_gate + D, inputs["w_branch_b"][i][rows], KD))
        rope = np.zeros((D, P), f32)
        rope[:, 0:64] = w_in[:, at_rope - 64:at_rope]
        rope[:, 64:96] = w_in[:, at_rope:at_rope + 32]
        rope[:, 96:112] = w_in[:, at_rope + 16:at_rope + 32]
        rope[:, 112:128] = w_in[:, at_rope:at_rope + 16]
        blocks = []
        for m in range(4):
            blocks += column(w_in, m * P)
        blocks += column(rope, 0) + column(w_in, at_kc)
        for m in range(2):
            blocks += column(w_in, at_qc + m * P)
        put(blocks)
        w_uq, w_ukv = inputs["w_uq"][i], inputs["w_ukv"][i]
        heads = np.zeros((Q_LORA, MLA_HEADS * P), f32)
        for hd in range(MLA_HEADS):
            src, dst = hd * MLA_QK, hd * P
            heads[:, dst:dst + 96] = w_uq[:, src:src + 96]
            heads[:, dst + 96:dst + 112] = w_uq[:, src + 80:src + 96]
            heads[:, dst + 112:dst + 128] = w_uq[:, src + 64:src + 80]
        kv = w_ukv.reshape(KV_LORA, MLA_HEADS, NOPE + MLA_V)
        k_cols = kv[:, :, 0:NOPE].reshape(KV_LORA, -1)
        v_cols = kv[:, :, NOPE:].reshape(KV_LORA, -1)
        blocks = []
        for hd in range(MLA_HEADS):
            blocks += column(heads, hd * P, 3)
        put(blocks + wide(k_cols, range(1)) + wide(v_cols, range(1)))
        put(column(w_in, at_qc + 2 * P) + column(w_in, at_qc + 3 * P) + column(w_in, at_vc))
        put(merge(w_in, at_gate, inputs["w_branch_a"][i], 4))
        put(merge(w_in, at_gate + 2 * D, inputs["w_branch_c"][i], 4))
        put(by_column(inputs["w_out"][i]))
        ffn(inputs["w_ffn_gate"][i], inputs["w_ffn_up"][i], inputs["w_ffn_down"][i])
        put(by_column(inputs["w_ple_proj"][i]))
        put(by_column(inputs["w_ple_gate"][i]))
        assert at[0] == (i + 1) * TOTAL1["U"]

    w_in = inputs["w_in_2"][0]
    sizes = dict(lru_x=512, lru_gate=512, pool=512, q=512, k=64, v=64, q_idx=512, k_idx=64, w_idx=8, gates=3 * D)
    off, n = {}, 0
    for name, width in sizes.items():
        off[name] = n
        n += width
    twice = np.zeros((D, 3 * P), f32)
    for j in range(2):
        twice[:, 64 * j:64 * j + 64] = w_in[:, off["k"]:off["k"] + 64]
        twice[:, P + 64 * j:P + 64 * j + 64] = w_in[:, off["k_idx"]:off["k_idx"] + 64]
    twice[:, 2 * P:2 * P + 64] = w_in[:, off["v"]:off["v"] + 64]
    twice[:, 2 * P + 64:2 * P + 72] = w_in[:, off["w_idx"]:off["w_idx"] + 8]
    blocks = []
    for name in ("lru_x", "q_idx", "k_idx", "v", "pool", "lru_gate", "q", "k"):
        if name in ("k", "k_idx", "v"):
            blocks += column(twice, ("k", "k_idx", "v").index(name) * P)
        else:
            for m in range(4):
                blocks += column(w_in, off[name] + m * P)
    put(blocks)
    blocks = [inputs["w_pool_2"][0, g] for g in range(4)]
    for name in ("lru_w_a_2", "lru_w_x_2"):
        for m in range(4):
            two = np.zeros((P, P), f32)
            two[0:64, 0:64] = inputs[name][0, 2 * m]
            two[64:, 64:] = inputs[name][0, 2 * m + 1]
            blocks.append(two)
    put(blocks)
    for br in (1, 0):
        put(merge(w_in, off["gates"] + br * D, inputs["w_branch_2"][0, br], 4))
    w_kv = inputs["w_mem_kv_2"][0]
    blocks = []
    for m in range(4):
        blocks += column(w_kv, m * P)
    put(blocks)
    put(wide(w_kv[:, 512:], range(KD)))
    put(merge(w_in, off["gates"] + 2 * D, inputs["w_branch_2"][0, 2], 4))
    put(by_column(inputs["w_out_2"][0]))
    blocks = []
    for m in range(4):
        blocks += column(inputs["w_mem_q_2"][0], m * P)
    put(blocks)
    put(by_column(inputs["w_mem_o_2"][0]))
    w_f = inputs["w_ffn_in_2"][0]
    ffn(w_f[:, 0:FFN], w_f[:, FFN:], inputs["w_ffn_out_2"][0])
    assert at[0] == UNITS

    vec1 = np.zeros((DEPTH, P, NV1), f32)
    for i in range(DEPTH):
        for name, key in (("mix_pre", "norm_mix_pre"), ("q_norm", "mla_q_norm"), ("kv_norm", "mla_kv_norm"), ("mix_post", "norm_mix_post"),
                          ("ffn_pre", "norm_ffn_pre"), ("ffn_post", "norm_ffn_post"), ("ple", "norm_ple")):
            v = inputs[key][i].reshape(-1, P).T
            vec1[i, :, VEC1[name]:VEC1[name] + v.shape[1]] = v
        vec1[i, :, VEC1["sink"]:VEC1["sink"] + 8] = inputs["gqa_sink"][i][None, :]

    cst = np.zeros((P, NCST), f32)
    cst[:, CST["ident"]:CST["ident"] + P] = np.eye(P, dtype=f32)
    cst[:, CST["ones"]:CST["ones"] + P] = 1.0
    qi, kj = np.arange(P)[:, None], np.arange(3 * P)[None, :]
    cst[:, CST["window"]:CST["window"] + 3 * P] = np.where(np.abs(kj - P - qi) <= P, 0.0, FAR)
    half = ROPE // 2
    freq = (np.float32(10000.0) ** (-np.arange(half, dtype=f32) / f32(half))).astype(f32)
    cst[64:P, CST["freq"]] = np.tile(freq, 4)
    cst[64:96, CST["phase"]] = np.pi / 2
    cst[64:112, CST["sign"]] = 1.0
    cst[96:112, CST["sign"]] = -1.0
    cst[112:P, CST["sign"]] = 1.0
    for g, w in enumerate(POOL_W):
        cst[:, CST["head"] + 16 * g:CST["head"] + 16 * g + 16] = np.array([w / min(t + 1, w) for t in range(16)], f32)[None, :]
    for name, key in (("mix_pre", "g_mix_pre_2"), ("mix_post", "g_mix_post_2"), ("mem_pre", "g_mem_pre_2"), ("mem_kv", "g_mem_kv_2"),
                      ("mem_post", "g_mem_post_2"), ("ffn_pre", "g_ffn_pre_2"), ("ffn_post", "g_ffn_post_2"), ("conv_w", "conv_w_2"),
                      ("conv_b", "conv_b_2"), ("b_a", "lru_b_a_2"), ("b_x", "lru_b_x_2"), ("a_param", "lru_a_param_2"),
                      ("pool", "pool_scale_2"), ("b_gate", "b_gate_2")):
        v = inputs[key][0].reshape(-1, P).T
        cst[:, CST[name]:CST[name] + v.shape[1]] = v

    pos = np.zeros((P, S + ST), np.int32)
    pos[:, 0:S] = inputs["positions"][0][None, :]
    pos[:, S:] = inputs["positions"][0].reshape(ST, P).T
    return {
        "stream": stream,
        "xT": np.ascontiguousarray(inputs["x"][0].T),
        "pT": np.ascontiguousarray(inputs["p"][:, 0].transpose(0, 2, 1)),
        "memT": np.ascontiguousarray(inputs["mem_2"][0].T),
        "vec1": vec1, "cst": cst, "pos": pos,
    }


def kernel(**inputs):
    import concourse.bacc as bacc
    from concourse.bass_utils import run_bass_kernel_spmd

    nc = bacc.Bacc("TRN2", target_bir_lowering=False, num_devices=1, dynamic_dma_scratch_size=2048)
    arrays = lay_out({k: np.asarray(v) for k, v in inputs.items()})
    feed, args = {}, []
    for name, a in arrays.items():
        feed[f"in_{name}"] = a
        args.append(nc.dram_tensor(f"in_{name}", a.shape, mybir.dt.from_np(a.dtype), kind="ExternalInput").ap())
    args.append(nc.dram_tensor("out_T", (D, S), F32, kind="ExternalOutput").ap())
    block_kernel(nc, *args)
    got = run_bass_kernel_spmd(nc, [feed], core_ids=[0]).results[0]["out_T"]
    return np.ascontiguousarray(got.T).reshape(1, S, D)
```
